# Optimizing a Trainium2 kernel written in Bass

```python
import math
import jax, jax.numpy as jnp
from jax import lax
import numpy as np

D_MODEL = 1024
BATCH = 1
SEQ = 512
DEPTH = 1
DEC_BATCH = 8
DEC_SEQ = 8
PAST_LEN = 4096
PAGE_SIZE = 128

M_HEADS = 4
M_DK = D_MODEL // 8
M_DV = D_MODEL // M_HEADS
G_HEADS = 4
G_DK = D_MODEL // 8
G_DV = D_MODEL // G_HEADS
G_RANK = 16
G_TAU = 16.0
D_FF = 2688
CONV_W = 3
PLE_DIM = 256
CHUNK = 64
EPS = 1e-6

MQK_W = M_HEADS * M_DK
MV_W = M_HEADS * M_DV
GK_W = G_HEADS * G_DK
GV_W = G_HEADS * G_DV
IN_SIZES = [MQK_W, MQK_W, MV_W, M_HEADS, M_HEADS, MV_W,
            GK_W, GK_W, GV_W, G_RANK, GV_W,
            D_MODEL, D_MODEL]
N_IN = sum(IN_SIZES)
SPLIT_IDX = [int(v) for v in np.cumsum(IN_SIZES)[:-1]]

kernel_name = "mlstm_gla_gated_hybrid_step"

def rmsnorm(x, g):
    x32 = x.astype(jnp.float32)
    y = x32 * lax.rsqrt(jnp.mean(x32 * x32, axis=-1, keepdims=True) + EPS)
    return (y * g.astype(jnp.float32)).astype(x.dtype)

def head_layernorm(h):
    mu = jnp.mean(h, axis=-1, keepdims=True)
    var = jnp.mean(jnp.square(h - mu), axis=-1, keepdims=True)
    return (h - mu) * lax.rsqrt(var + EPS)

def head_rmsnorm(h):
    return h * lax.rsqrt(jnp.mean(h * h, axis=-1, keepdims=True) + EPS)

def chunk_len(S):
    return CHUNK if S % CHUNK == 0 else S

def to_chunks(t, L):
    B, S = t.shape[:2]
    return jnp.moveaxis(t.reshape((B, S // L, L) + t.shape[2:]), 1, 0)

def from_chunks(t):
    NC, B, L = t.shape[:3]
    return jnp.moveaxis(t, 0, 1).reshape((B, NC * L) + t.shape[3:])

def mlstm_scan(q, k, v, li, lf, C0, n0, m0):
    S = q.shape[1]
    L = chunk_len(S)
    tril = jnp.tril(jnp.ones((L, L), dtype=bool))

    def step(carry, inp):
        C, n, m = carry
        qc, kc, vc, lic, lfc = inp
        b = jnp.cumsum(lfc, axis=1)
        D = b[:, :, None, :] - b[:, None, :, :] + lic[:, None, :, :]
        D = jnp.where(tril[None, :, :, None], D, -jnp.inf)
        inter = b + m[:, None, :]
        mt = jnp.maximum(inter, jnp.max(D, axis=2))
        w_inter = jnp.exp(inter - mt)
        P = jnp.exp(D - mt[:, :, None, :])
        A = P * jnp.einsum('bthd,bshd->btsh', qc, kc)
        num = jnp.einsum('btsh,bshv->bthv', A, vc) + w_inter[..., None] * jnp.einsum('bthd,bhdv->bthv', qc, C)
        den = jnp.sum(A, axis=2) + w_inter * jnp.einsum('bthd,bhd->bth', qc, n)
        den = jnp.maximum(jnp.abs(den), jnp.exp(-mt))
        h = num / den[..., None]
        mL = mt[:, -1]
        ws = jnp.exp(b[:, -1][:, None, :] - b + lic - mL[:, None, :])
        carry_w = jnp.exp(b[:, -1] + m - mL)
        C_new = carry_w[..., None, None] * C + jnp.einsum('bsh,bshd,bshv->bhdv', ws, kc, vc)
        n_new = carry_w[..., None] * n + jnp.einsum('bsh,bshd->bhd', ws, kc)
        return (C_new, n_new, mL), h

    xs = (to_chunks(q, L), to_chunks(k, L), to_chunks(v, L), to_chunks(li, L), to_chunks(lf, L))
    (C, n, m), hs = lax.scan(step, (C0, n0, m0), xs)
    return from_chunks(hs), C, n, m

def gla_scan(q, k, v, la, S0):
    S = q.shape[1]
    L = chunk_len(S)
    tril = jnp.tril(jnp.ones((L, L), dtype=bool))

    def step(Sst, inp):
        qc, kc, vc, lac = inp
        Bc = jnp.cumsum(lac, axis=1)
        diff = Bc[:, :, None] - Bc[:, None, :]
        decay = jnp.exp(jnp.where(tril[None, :, :, None, None], diff, -jnp.inf))
        A = jnp.einsum('bthd,bshd,btshd->btsh', qc, kc, decay)
        o = jnp.einsum('btsh,bshv->bthv', A, vc) + jnp.einsum('bthd,bhdv->bthv', qc * jnp.exp(Bc), Sst)
        BL = Bc[:, -1]
        S_new = jnp.exp(BL)[..., None] * Sst + jnp.einsum('bshd,bshv->bhdv', kc * jnp.exp(BL[:, None] - Bc), vc)
        return S_new, o

    xs = (to_chunks(q, L), to_chunks(k, L), to_chunks(v, L), to_chunks(la, L))
    Sf, os_ = lax.scan(step, S0, xs)
    return from_chunks(os_), Sf

def token_mixers(a, W, i, C0, n0, m0, S0):
    B, S, _ = a.shape
    f32 = jnp.float32
    z = a @ W['w_in'][i]
    mq, mk, mv, mi, mf, mo, gq, gk, gv, glr, gg, ga, gb = jnp.split(z, SPLIT_IDX, axis=-1)
    mq = mq.reshape(B, S, M_HEADS, M_DK).astype(f32)
    mk = mk.reshape(B, S, M_HEADS, M_DK).astype(f32) * (M_DK ** -0.5)
    mv = mv.reshape(B, S, M_HEADS, M_DV).astype(f32)
    li = (mi + W['b_mi'][i]).astype(f32)
    lf = jax.nn.log_sigmoid((mf + W['b_mf'][i]).astype(f32))
    hm, C, n, m = mlstm_scan(mq, mk, mv, li, lf, C0.astype(f32), n0.astype(f32), m0.astype(f32))
    hm = head_layernorm(hm).reshape(B, S, MV_W) * W['g_mnorm'][i].astype(f32)
    hm = (hm * jax.nn.sigmoid(mo.astype(f32))).astype(a.dtype)
    gq = gq.reshape(B, S, G_HEADS, G_DK).astype(f32) * (G_DK ** -0.5)
    gk = gk.reshape(B, S, G_HEADS, G_DK).astype(f32)
    gv = gv.reshape(B, S, G_HEADS, G_DV).astype(f32)
    la = jax.nn.log_sigmoid((glr @ W['w_lr2'][i] + W['b_lr2'][i]).astype(f32)) / G_TAU
    la = la.reshape(B, S, G_HEADS, G_DK)
    hg, Sf = gla_scan(gq, gk, gv, la, S0.astype(f32))
    hg = head_rmsnorm(hg).reshape(B, S, GV_W) * W['g_gnorm'][i].astype(f32)
    hg = (hg * jax.nn.silu(gg.astype(f32))).astype(a.dtype)
    merged = jax.nn.sigmoid(ga) * (hm @ W['w_pa'][i]) + jax.nn.sigmoid(gb) * (hg @ W['w_pb'][i])
    return merged @ W['w_o'][i], C, n, m, Sf

def conv_ffn(c, W, i, buf):
    S = c.shape[1]
    uz = c @ W['w_up'][i]
    u_gate, u_val = jnp.split(uz, [D_FF], axis=-1)
    xp = jnp.concatenate([buf.astype(u_gate.dtype), u_gate], axis=1)
    cw = W['conv_w'][i]
    conv = W['conv_b'][i] + sum(cw[j] * xp[:, j:j + S] for j in range(CONV_W))
    act = jax.nn.silu(conv) * u_val
    return act @ W['w_down'][i], xp[:, -(CONV_W - 1):]

def trunk(x, p, C0, n0, m0, S0, cv0, W):
    h = x
    Cs, ns, ms, Ss, cvs = [], [], [], [], []
    for i in range(DEPTH):
        a = rmsnorm(h, W['norm_mix_g'][i])
        mix, C, n, m, Sf = token_mixers(a, W, i, C0[i], n0[i], m0[i], S0[i])
        h = h + mix
        c = rmsnorm(h, W['norm_ffn_g'][i])
        f, cv = conv_ffn(c, W, i, cv0[i])
        h = h + f
        e = rmsnorm(h, W['norm_ple_g'][i])
        h = h + jax.nn.sigmoid(e @ W['w_ple_gate'][i]) * (p[i] @ W['w_ple_proj'][i])
        Cs.append(C); ns.append(n); ms.append(m); Ss.append(Sf); cvs.append(cv)
    y = rmsnorm(h, W['final_norm_g'])
    return y, jnp.stack(Cs), jnp.stack(ns), jnp.stack(ms), jnp.stack(Ss), jnp.stack(cvs)

def setup_inputs(seed: int = 0) -> dict:
    key = jax.random.key(seed)
    ks = iter(jax.random.split(key, 40))

    def nrm(shape, scale):
        return jax.random.normal(next(ks), shape, jnp.float32) * scale

    def gain(shape):
        return 1.0 + nrm(shape, 0.05)

    d = {}
    d['x_prompt'] = nrm((BATCH, SEQ, D_MODEL), 1.0)
    d['x_sample'] = nrm((DEC_BATCH, DEC_SEQ, D_MODEL), 1.0)
    d['state_mlstm_C'] = nrm((DEPTH, DEC_BATCH, M_HEADS, M_DK, M_DV), 0.05)
    d['state_mlstm_n'] = nrm((DEPTH, DEC_BATCH, M_HEADS, M_DK), 0.5)
    d['state_mlstm_m'] = nrm((DEPTH, DEC_BATCH, M_HEADS), 1.0)
    d['state_gla_S'] = nrm((DEPTH, DEC_BATCH, G_HEADS, G_DK, G_DV), 0.1)
    d['state_ffn_conv'] = nrm((DEPTH, DEC_BATCH, CONV_W - 1, D_FF), 1.0)
    d['p_prompt'] = nrm((DEPTH, BATCH, SEQ, PLE_DIM), 1.0)
    d['p_sample'] = nrm((DEPTH, DEC_BATCH, DEC_SEQ, PLE_DIM), 1.0)
    d['norm_mix_g'] = gain((DEPTH, D_MODEL))
    d['w_in'] = nrm((DEPTH, D_MODEL, N_IN), D_MODEL ** -0.5)
    d['b_mi'] = nrm((DEPTH, M_HEADS), 0.1)
    d['b_mf'] = jnp.linspace(3.0, 6.0, M_HEADS, dtype=jnp.float32)[None, :] + nrm((DEPTH, M_HEADS), 0.1)
    d['g_mnorm'] = gain((DEPTH, MV_W))
    d['w_lr2'] = nrm((DEPTH, G_RANK, GK_W), G_RANK ** -0.5)
    d['b_lr2'] = nrm((DEPTH, GK_W), 0.1)
    d['g_gnorm'] = gain((DEPTH, GV_W))
    d['w_pa'] = nrm((DEPTH, MV_W, D_MODEL), MV_W ** -0.5)
    d['w_pb'] = nrm((DEPTH, GV_W, D_MODEL), GV_W ** -0.5)
    d['w_o'] = nrm((DEPTH, D_MODEL, D_MODEL), 0.5 * D_MODEL ** -0.5)
    d['norm_ffn_g'] = gain((DEPTH, D_MODEL))
    d['w_up'] = nrm((DEPTH, D_MODEL, 2 * D_FF), D_MODEL ** -0.5)
    d['conv_w'] = nrm((DEPTH, CONV_W, D_FF), CONV_W ** -0.5)
    d['conv_b'] = nrm((DEPTH, D_FF), 0.02)
    d['w_down'] = nrm((DEPTH, D_FF, D_MODEL), 0.5 * D_FF ** -0.5)
    d['norm_ple_g'] = gain((DEPTH, D_MODEL))
    d['w_ple_gate'] = nrm((DEPTH, D_MODEL, D_MODEL), D_MODEL ** -0.5)
    d['w_ple_proj'] = nrm((DEPTH, PLE_DIM, D_MODEL), 0.5 * PLE_DIM ** -0.5)
    d['final_norm_g'] = gain((D_MODEL,))
    return d

def reference(x_prompt, x_sample, state_mlstm_C, state_mlstm_n, state_mlstm_m, state_gla_S,
              state_ffn_conv, p_prompt, p_sample, norm_mix_g, w_in, b_mi, b_mf, g_mnorm, w_lr2,
              b_lr2, g_gnorm, w_pa, w_pb, w_o, norm_ffn_g, w_up, conv_w, conv_b, w_down,
              norm_ple_g, w_ple_gate, w_ple_proj, final_norm_g):
    W = dict(norm_mix_g=norm_mix_g, w_in=w_in, b_mi=b_mi, b_mf=b_mf, g_mnorm=g_mnorm,
             w_lr2=w_lr2, b_lr2=b_lr2, g_gnorm=g_gnorm, w_pa=w_pa, w_pb=w_pb, w_o=w_o,
             norm_ffn_g=norm_ffn_g, w_up=w_up, conv_w=conv_w, conv_b=conv_b, w_down=w_down,
             norm_ple_g=norm_ple_g, w_ple_gate=w_ple_gate, w_ple_proj=w_ple_proj,
             final_norm_g=final_norm_g)
    B = x_prompt.shape[0]
    f32 = jnp.float32
    C0 = jnp.zeros((DEPTH, B, M_HEADS, M_DK, M_DV), f32)
    n0 = jnp.zeros((DEPTH, B, M_HEADS, M_DK), f32)
    m0 = jnp.zeros((DEPTH, B, M_HEADS), f32)
    S0 = jnp.zeros((DEPTH, B, G_HEADS, G_DK, G_DV), f32)
    cv0 = jnp.zeros((DEPTH, B, CONV_W - 1, D_FF), x_prompt.dtype)
    y_prompt, C_p, n_p, m_p, S_p, conv_p = trunk(x_prompt, p_prompt, C0, n0, m0, S0, cv0, W)
    y_sample, C_s, n_s, m_s, S_s, conv_s = trunk(x_sample, p_sample, state_mlstm_C, state_mlstm_n,
                                                 state_mlstm_m, state_gla_S, state_ffn_conv, W)
    return (y_prompt, y_sample, C_p, n_p, m_p, S_p, conv_p, C_s, n_s, m_s, S_s, conv_s)


_drawn_inputs = setup_inputs


def setup_inputs(seed=0):
    import zlib

    import numpy as np

    out = dict(_drawn_inputs(seed))
    spreads = {}
    factors = {'g_mnorm': 7.476, 'g_gnorm': 6.989, 'conv_b': 8.0, 'norm_ple_g': 133.857}
    for name, (base, spread) in spreads.items():
        noise = np.random.default_rng([zlib.crc32(name.encode()), seed]).standard_normal(out[name].shape)
        drawn = base * np.exp(spread * noise) if base else spread * noise
        out[name] = __import__('jax').numpy.asarray(drawn.astype(out[name].dtype))
    for name, factor in factors.items():
        out[name] = (out[name] * factor).astype(out[name].dtype)
    return out
```

```python
from contextlib import ExitStack

import numpy as np
import concourse.bass as bass
from concourse import mybir

F32 = mybir.dt.float32
F32R = mybir.dt.float32r
I8 = mybir.dt.int8
ALU = mybir.AluOpType
ACT = mybir.ActivationFunctionType

P = 128
D = 1024
KT = D // P
TP, NB, LS = 512, 8, 8
TS = NB * LS
T = TP + TS
HALF = T // 2
H = 4
DK, DV = 128, 256
L = 128
NC = TP // L
FF = 2688
FT = FF // P
PLE = 256
PK = PLE // P
RANK = 16
TAU = 16.0
EPS = 1e-6
UW = 2048
NORM_MIX, NORM_M, NORM_G, NORM_FFN, NORM_PLE, NORM_OUT = range(6)
PROMPT_LEVELS = [64, 32, 16, 8, 4, 2, 1]
SAMPLE_LEVELS = [4, 2, 1]
ZMO, ZGG, ZGA, ZGB = 0, 8, 16, 24


def chunk_span(c):
    return (c * L, L) if c < NC else (TP, TS)


def plan():
    units = [("misc", 0)]
    units += [("mq", i) for i in range(2)] + [("mk", i) for i in range(2)] + [("mv", i) for i in range(4)]
    units += [("gq", i) for i in range(2)] + [("gk", i) for i in range(2)] + [("gv", i) for i in range(4)]
    units += [(n, i) for n in ("mo", "gg", "ga", "gb") for i in range(4)]
    units += [(n, i) for n in ("pa", "pb", "wo") for i in range(4)]
    units += [("up", i) for i in range(FT)] + [("down", i) for i in range(2 * KT)]
    units += [("pproj", 0)] + [("pgate", i) for i in range(4)]
    at = {x: n for n, x in enumerate(units)}
    sched = [("norm_in",)]

    def unit(kind, i, *stages):
        sched.append(("unit", at[(kind, i)]))
        sched.extend(stages)

    unit("misc", 0, ("rms", 0), ("rs_cols",), ("rows",))
    for n in ("mq", "mk"):
        unit(n, 0)
        unit(n, 1)
    for i in range(4):
        unit("mv", i)
    unit("gq", 0, ("mchunk", 0))
    unit("gq", 1, ("mchunk", 1))
    unit("gk", 0, ("mchunk", 2))
    unit("gk", 1, ("mchunk", 3), ("mchunk", NC))
    for i in range(4):
        unit("gv", i, ("head", "m", i))
    sched.append(("la",))
    for i in range(4):
        unit("mo", i, ("gchunk", i), ("tnorm", "m", i))
    sched.append(("gchunk", NC))
    for i in range(4):
        unit("gg", i, ("head", "g", i), ("tnorm", "g", i), *([("tnorm", "m", NC)] if i == 0 else []))
    sched.append(("tnorm", "g", NC))
    for n in ("ga", "gb"):
        for i in range(4):
            unit(n, i, ("bt", "m", i + 4 * (n == "gb")))
    for i in range(4):
        unit("pa", i, ("bt", "g", 2 * i), ("bt", "g", 2 * i + 1))
    for i in range(4):
        unit("pb", i)
    for i in range(4):
        unit("wo", i)
    for i in range(FT):
        unit("up", i, *([("rms", 1)] if i == 0 else []))
    for i in range(2 * KT):
        unit("down", i)
    unit("pproj", 0, ("rms", 2))
    for i in range(4):
        unit("pgate", i)
    sched.append(("rms", 3))
    return units, sched


def tiles_of(kind, i):
    if kind == "misc":
        return [("misc", 0)]
    if kind in ("mv", "gv"):
        return [(kind, (i, c)) for c in range(NC + 1)]
    if kind == "up":
        return [("gate", i), ("val", i)]
    if kind == "down":
        return [("down", i // 2)] if i % 2 else []
    if kind == "pproj":
        return [("pproj", n) for n in range(KT)]
    return [(kind, 2 * i), (kind, 2 * i + 1)]


def aux_jobs(stage):
    if stage[0] == "rms":
        return 2
    if stage[0] == "rs_cols":
        return 1
    if stage[0] == "rows":
        return 3
    if stage[0] == "mchunk":
        return 4 + (2 * H if stage[1] < NC else 0)
    if stage[0] == "la":
        return 2 * H
    if stage[0] == "gchunk":
        return (len(PROMPT_LEVELS) + 2 + 2 * H) if stage[1] < NC else len(SAMPLE_LEVELS) + 2
    if stage[0] == "head":
        return 1 + NB
    return 0


def build(nc, ins, outs):
    units, sched = plan()
    tile_at, job_at, nt, nj = {}, {}, 0, 0
    for s in sched:
        if s[0] == "unit":
            tile_at[s] = nt
            nt += len(tiles_of(*units[s[1]]))
        elif s[0] == "bt":
            tile_at[s] = nt
            nt += 1
        job_at[s] = nj
        nj += aux_jobs(s)

    zs = nc.dram_tensor("gate_scratch", [32, P, T], F32).ap()
    hs = nc.dram_tensor("residual_scratch", [KT, P, T], F32).ap()

    with ExitStack() as ctx:
        base = 16512
        where = [base]

        def at(name, shape, dt, offset):
            return nc.alloc_sbuf_tensor_at(name, shape, dt, offset=offset)

        def put(name, shape, dt=F32):
            n = int(np.prod(shape[1:])) * (1 if dt == I8 else 4)
            t = at(name, shape, dt, where[0])
            where[0] += (n + 31) // 32 * 32
            return t

        ident = put("ident", [P, P])
        ones = put("ones", [P, P])
        cmask = put("cmask", [P, 8, P], I8)
        nmask = put("nmask", [P, 2, P])
        bmask = put("bmask", [TS, NB])
        gains = put("gains", [P, 6, KT])
        convw = put("convw", [P, 3, FT])
        convb = put("convb", [P, FT])
        blr = put("blr", [P, H])
        bgate = put("bgate", [H, 2])
        m0 = put("m0", [H, NB])
        wlr = put("wlr", [RANK, H * DK])
        nst = put("nst", [P, H, NB])
        nout = put("nout", [P, H, NB + 1])
        mout = put("mout", [H, NB + 1])
        convst = put("convst", [P, FT, NB, 2])
        wraw = put("wraw", [P, 2, UW])
        whi = put("whi", [P, 2, UW], F32R)
        wlo = put("wlo", [P, 2, UW], F32R)
        X = where[0]
        fm = [P, KT, T]
        ahi = at("ahi", fm, F32R, X)
        alo = at("alo", fm, F32R, X + 18432)
        VM = X + 36864
        vm = at("vm", [P, NC + 1, H, DV + 1], F32, VM)
        xT = at("xT", fm, F32, VM)
        VG = VM + 20576
        vg = at("vg", [P, NC + 1, H, DV], F32, VG)
        cst = at("cst", [P, 2, H, DV + 1], F32, VG)
        cmaskf = at("cmaskf", [P, 8, P], F32, VG)
        r1 = at("r1", [H, T], F32, VG + 8224)
        ri = at("ri", [H, T], F32, VG + 8224 + 2304)
        rr = at("rr", [P, T], F32, VG + 8224 + 4608)
        sel = at("sel", [H, H, P], F32, VG + 8224 + 6912)
        QM = VG + 20480
        mq = at("mq", [P, H, T], F32, QM)
        mk = at("mk", [P, H, T], F32, QM + 9216)
        cum = at("cum", [P, H, T], F32, QM)
        stg = at("stg", [P, 2, T], F32, QM + 9216)
        xl01 = at("xl01", [P, 2, H, L], F32, QM + 9216 + 4608)
        QG = QM + 18432
        gq = at("gq", [P, H, T], F32, QG)
        gk = at("gk", [P, H, T], F32, QG + 9216)
        rowt = [at(f"rowt{i}", [H, T], F32, QG + 2304 * i) for i in range(8)]
        ROW_LI, ROW_XF, ROW_LF, ROW_B, ROW_M, ROW_D0, ROW_D1, ROW_T = range(8)
        ST = QG + 18432
        st = [at(f"st{i}", [P, NB, DV + 1], F32, ST + 8224 * i) for i in range(2)]
        gst = at("gst", [P, 2, H, DV], F32, ST + 8224)
        acc0 = at("acc0", [P, T], F32, ST)
        sq = at("sq", [P, 2, T], F32, ST + 2304)
        G0 = ST + 16448
        pw = at("pw", [P, H, L], F32, G0)
        qt = at("qt", [P, H, L], F32, G0 + 2048)
        att = at("att", [P, H, L], F32, G0 + 4096)
        ktok = at("ktok", [P, H, L], F32, G0 + 6144)
        QB = G0 + 8192
        qb = at("qb", [P, T], F32, QB)
        kb = at("kb", [TS, NB, P], F32, QB + 2304)
        kf = at("kf", [P, H, L], F32, QB + 2304)
        so = at("so", [TS, 1, DV + 1], F32, QB + 6400)
        MK = QB + 6400 + 1056
        reset = at("reset", [P, T], F32, MK)
        glr = at("glr", [RANK, T], F32, MK + 2304)
        xl2 = at("xl2", [P, 1, H, L], F32, MK + 2304)
        rs = at("rs", [P, T], F32, MK + 4608)
        SM = MK + 6912
        colT = at("colT", [P, NC + 1, 3, H], F32, SM)
        carry = at("carry", [P, H, NC + NB], F32, SM + 256)
        rscol = at("rscol", [P, NC + 1], F32, SM + 448)
        nstat = at("nstat", [P, H, 6], F32, SM + 480)
        nmv = at("nmv", [P, H, 2], F32, SM + 576)
        nsm = at("nsm", [P, 6, H], F32, SM + 608)
        rowc = at("rowc", [H, 5, NC + NB], F32, SM + 704)
        assert SM + 704 + 240 <= 229368, SM + 944 - 229368
        hmhi = at("hmhi", fm, F32R, QG)
        hmlo = at("hmlo", fm, F32R, QG + 18432)
        gt = at("gt", [P, 2, T], F32, QB)
        bt_t = at("bt_t", [P, 1, T], F32, QB + 4608)
        merged = at("merged", fm, F32, VM)
        mghi = at("mghi", fm, F32R, VG)
        mglo = at("mglo", fm, F32R, QM)
        xr = at("xr", [P, 2, T], F32, VM)
        hst = at("hst", [P, 2, T], F32, VM + 4608)
        achi = at("achi", [P, FT, T], F32R, X + 36864)
        aclo = at("aclo", [P, FT, T], F32R, X + 36864 + FT * T * 4)
        FS = X + 36864 + 2 * FT * T * 4
        GW = 2 + TP + NB * (2 + LS)
        gbuf = at("gbuf", [P, GW], F32, FS)
        cv = at("cv", [P, GW], F32, FS + 2400)
        sg = at("sg", [P, GW], F32, FS + 4800)
        vrs = at("vrs", [P, T], F32, FS + 7200)
        af = at("af", [P, T], F32, FS + 9504)
        acc = at("acc", [P, T], F32, FS + 11808)
        sq2 = at("sq2", [P, T], F32, FS + 14112)
        rsv = at("rsv", [P, T], F32, FS + 16416)
        convout = at("convout", [P, FT, 2 + 2 * NB], F32, FS + 18720)
        h2 = at("h2", fm, F32, X)
        h3 = at("h3", fm, F32, X + 18432)
        ehi = at("ehi", fm, F32R, X + 36864)
        elo = at("elo", fm, F32R, X + 36864 + 18432)
        pj = at("pj", fm, F32, X + 36864 * 2)
        praw = at("praw", [P, PK, T], F32, X + 18432)
        phi = at("phi", [P, PK, T], F32R, X + 18432 + 4608)
        plo = at("plo", [P, PK, T], F32R, X + 18432 + 9216)
        sgp = at("sgp", [P, 2, T], F32, X + 36864 * 3)
        yt = at("yt", [P, 2, T], F32, X + 36864 * 3 + 4608)

        ps = ctx.enter_context(nc.psum_tensor("ps", [P, 2, 2, 512], F32))
        aux = ctx.enter_context(nc.psum_tensor("aux", [P, 4, 512], F32))

        def sem(name):
            return ctx.enter_context(nc.semaphore(name))

        def sems(name, n):
            return [sem(f"{name}{i}") for i in range(n)]

        raw_in = sems("raw_in", 2)
        split_hi = sem("split_hi")
        split_lo = sem("split_lo")
        half_done = sem("half_done")
        tile_ready = sem("tile_ready")
        tile_free = sems("tile_free", 2)
        aux_ready = sem("aux_ready")
        aux_free = sems("aux_free", 4)
        const_in = sem("const_in")
        gains_in = sem("gains_in")
        x_in = sems("x_in", 4)
        dve_step = sem("dve_step")
        act_step = sem("act_step")
        pool_step = sem("pool_step")
        init_done = sem("init_done")
        wraw_zero = sem("wraw_zero")
        in_sq = sem("in_sq")
        in_sq_used = sem("in_sq_used")
        a_hi = sem("a_hi")
        a_lo = sem("a_lo")
        sq_sum = sem("sq_sum")
        ms_ready = sem("ms_ready")
        rs_guess = sem("rs_guess")
        rs_ready = sem("rs_ready")
        rsc_ready = sem("rsc_ready")
        row_abs = sem("row_abs")
        row_ln = sem("row_ln")
        row_pre = sem("row_pre")
        row_exp = sem("row_exp")
        rows_zero = sem("rows_zero")
        fm_ready = sem("fm_ready")
        v_ready = sem("v_ready")
        p_pre = sem("p_pre")
        p_exp = sem("p_exp")
        qt_ready = sem("qt_ready")
        kt_ready = sem("kt_ready")
        at_ready = sem("at_ready")
        c_ready = sem("c_ready")
        s_ready = sem("s_ready")
        blk_ready = sem("blk_ready")
        st_in = sems("st_in", 2)
        st_n = sem("st_n")
        st_new = sem("st_new")
        st_out = sems("st_out", 2)
        cp_out = sem("cp_out")
        out_done = sem("out_done")
        h_out = sem("h_out")
        la_abs = sem("la_abs")
        la_ln = sem("la_ln")
        cum_ready = sem("cum_ready")
        g_go = sem("g_go")
        eb_ready = sem("eb_ready")
        kd_sub = sem("kd_sub")
        kd_exp = sem("kd_exp")
        kf_ready = sem("kf_ready")
        xl_sub = sem("xl_sub")
        xl_exp = sem("xl_exp")
        xl_ready = sem("xl_ready")
        stg_full = sem("stg_full")
        stg_out = sems("stg_out", 2)
        tn_pre = sem("tn_pre")
        tn_exp = sem("tn_exp")
        tn_done = sem("tn_done")
        gt_in = sems("gt_in", 2)
        gt_sig = sem("gt_sig")
        gt_used = sem("gt_used")
        bt_pre = sem("bt_pre")
        bt_hi = sem("bt_hi")
        bt_lo = sem("bt_lo")
        mg_pre = sem("mg_pre")
        mg_hi = sem("mg_hi")
        mg_lo = sem("mg_lo")
        xr_in = sems("xr_in", 2)
        h_pre = sem("h_pre")
        c_hi = sem("c_hi")
        c_lo = sem("c_lo")
        hs_out = sems("hs_out", 2)
        ff_g = sem("ff_g")
        ff_cv = sem("ff_cv")
        ff_sg = sem("ff_sg")
        ff_pre = sem("ff_pre")
        ff_hi = sem("ff_hi")
        ff_lo = sem("ff_lo")
        h2_in = sem("h2_in")
        h2_new = sem("h2_new")
        p_in = sem("p_in")
        p_hi = sem("p_hi")
        p_lo = sem("p_lo")
        pj_ready = sem("pj_ready")
        e_hi = sem("e_hi")
        e_lo = sem("e_lo")
        pg_pre = sem("pg_pre")
        pg_sig = sem("pg_sig")
        y_ready = sem("y_ready")
        y_out = sems("y_out", 2)

        block = ctx.enter_context(nc.Block())

        def two(ap):
            return ap.rearrange("p (a b) -> p a b", a=2)

        def tile(t):
            return ps[:, t % 2, :, 0:HALF]

        def bcast(ap, n, where_):
            shape = list(ap.shape)
            return ap.unsqueeze(where_).broadcast_to(shape[:where_] + [n] + shape[where_:])

        def f32(ap):
            return ap.bitcast(F32)

        def head_jobs():
            return [s for s in sched if s[0] == "head"]

        head_no = {s: n for n, s in enumerate(head_jobs())}

        def out_count(q):
            return 16 * (q // 2 + 1)

        h_out_of, copied, = {}, 0
        for s in sched:
            if s[0] in ("mchunk", "gchunk") and s[1] < NC:
                copied += H
                h_out_of[(s[0][0], s[1])] = copied
            elif s[0] == "head":
                copied += 1
                h_out_of[(s[1], NC)] = copied

        sched_v = list(sched)
        for n in (0, 1):
            k = sched_v.index(("rms", n))
            sched_v[k - 1], sched_v[k] = sched_v[k], sched_v[k - 1]

        @block.sync
        def _(sp):
            sp.dma_start(gains[:, :, :], ins["gains"]).then_inc(gains_in, 16)
            for u, (kind, i) in enumerate(units):
                s = u % 2
                if u >= 2:
                    sp.wait_ge(split_hi, u - 1)
                    sp.wait_ge(split_lo, u - 1)
                if kind == "misc":
                    sp.wait_ge(wraw_zero, 1)
                    v = wraw[:, 0, 0:KT * P].rearrange("p (k c) -> p k c", k=KT)
                    sp.dma_start(v[:, :, 0:H], ins["w_misc"][:, :, 0:H]).then_inc(raw_in[0], 16)
                    sp.dma_start(v[:, :, 32:32 + H], ins["w_misc"][:, :, H:2 * H]).then_inc(raw_in[0], 16)
                    sp.dma_start(v[:, :, 64:64 + RANK], ins["w_misc"][:, :, 2 * H:]).then_inc(raw_in[0], 16)
                    for n, dst in (("ident", ident[:, :]), ("cmask", cmaskf[:, :, :]), ("nmask", nmask[:, :, :]),
                                   ("sel", sel[:, :, :]), ("bmask", bmask[:, :]), ("convw", convw[:, :, :]),
                                   ("convb", convb[:, :]), ("blr", blr[:, :]), ("bgate", bgate[:, :]),
                                   ("m0", m0[:, :]), ("wlr", wlr[:, :]), ("nst", nst[:, :, :]),
                                   ("convst", convst[:, :, :, :])):
                        sp.dma_start(dst, ins[n]).then_inc(const_in, 16)
                else:
                    src = {"pa": "w_pa", "pb": "w_pb", "wo": "w_o", "up": "w_up", "pproj": "w_pproj",
                           "pgate": "w_pgate", "down": "w_down"}.get(kind, "w_in")
                    if src == "w_in":
                        row = {"mq": 0, "mk": 2, "mv": 4, "gq": 8, "gk": 10, "gv": 12,
                               "mo": 16, "gg": 20, "ga": 24, "gb": 28}[kind] + i
                        sp.dma_start(wraw[:, s, :], ins["w_in"][row, :, :]).then_inc(raw_in[s], 16)
                    elif kind == "down":
                        a, b = (0, 11 * P) if i % 2 == 0 else (11 * P, FF)
                        sp.dma_start(wraw[:, s, 0:b - a], ins["w_down"][i // 2, :, a:b]).then_inc(raw_in[s], 16)
                    else:
                        sp.dma_start(wraw[:, s, :], ins[src][i, :, :]).then_inc(raw_in[s], 16)

        NCONST = 13 * 16

        def raw_count(u):
            return 16 * (u // 2 + 1) + (32 if u % 2 == 0 else 0)

        def width(u):
            kind, i = units[u]
            if kind == "misc":
                return KT * P
            if kind == "down":
                return 11 * P if i % 2 == 0 else 10 * P
            return UW

        def used(eng, u):
            kind, i = units[u]
            if kind == "down" and i % 2 == 0:
                eng.wait_ge(half_done, i // 2 + 1)
            else:
                eng.wait_ge(tile_ready, tile_at[("unit", u)] + len(tiles_of(kind, i)))

        @block.gpsimd
        def _(pool):
            nc.gpsimd.memset(wraw[:, 0, 0:KT * P], 0.0).then_inc(wraw_zero, 1)
            for u in range(len(units)):
                s, n = u % 2, width(u)
                pool.wait_ge(raw_in[s], raw_count(u))
                pool.wait_ge(split_hi, u + 1)
                if u >= 2:
                    used(pool, u - 2)
                nc.gpsimd.tensor_tensor(wlo[:, s, 0:n], wraw[:, s, 0:n], f32(whi[:, s, 0:n]), ALU.subtract)\
                    .then_inc(split_lo, 1)

        @block.tensor
        def _(pe):
            def bank(j):
                if j >= 4:
                    pe.wait_ge(aux_free[j % 4], j // 4)
                return aux[:, j % 4, :]

            def slot(t):
                if t >= 2:
                    pe.wait_ge(tile_free[t % 2], t // 2)

            def product(t, blocks, hi, lo, s, start=True, stop=True, ready=None):
                for n, (col, k) in enumerate(blocks):
                    if ready:
                        for q in ready:
                            pe.wait_ge(q, k + 1)
                    first, last = start and n == 0, stop and n == len(blocks) - 1
                    wh, wl = whi[:, s, col:col + P], wlo[:, s, col:col + P]
                    for x, w, f, e in ((hi, wh, first, False), (lo, wh, False, False), (hi, wl, False, last)):
                        for a in range(2):
                            mm = nc.tensor.matmul(ps[:, t % 2, a, 0:HALF], w, x[:, k, a * HALF:(a + 1) * HALF],
                                                  start=f, stop=e)
                if stop:
                    mm.then_inc(tile_ready, 1)
                return mm

            counts = {"lv": 0}
            for s in sched:
                j, t = job_at[s], tile_at.get(s)
                if s[0] == "unit":
                    u = s[1]
                    kind, i = units[u]
                    w = u % 2
                    pe.wait_ge(split_hi, u + 1)
                    pe.wait_ge(split_lo, u + 1)
                    mm = None
                    if kind == "misc":
                        slot(t)
                        mm = product(t, [(k * P, k) for k in range(KT)], ahi, alo, w, ready=(a_hi, a_lo))
                    elif kind in ("mv", "gv"):
                        for n, c in enumerate(range(NC + 1)):
                            slot(t + n)
                            t0, ln = chunk_span(c)
                            for k in range(KT):
                                wh = whi[:, w, k * DV:(k + 1) * DV]
                                wl = wlo[:, w, k * DV:(k + 1) * DV]
                                xh, xlw = ahi[:, k, t0:t0 + ln], alo[:, k, t0:t0 + ln]
                                for x, y, f, e in ((xh, wh, k == 0, False), (xlw, wh, False, False),
                                                   (xh, wl, False, k == KT - 1)):
                                    mm = nc.tensor.matmul(ps[0:ln, (t + n) % 2, 0, 0:DV], x, y, start=f, stop=e)
                            mm.then_inc(tile_ready, 1)
                    elif kind == "down":
                        n = i // 2
                        if i == 0:
                            pe.wait_ge(ff_hi, FT)
                            pe.wait_ge(ff_lo, FT)
                        if i % 2 == 0:
                            slot(t)
                            mm = product(t, [(b * P, b) for b in range(11)], achi, aclo, w, stop=False)
                        else:
                            mm = product(t, [(b * P, 11 + b) for b in range(10)], achi, aclo, w, start=False)
                    elif kind == "pproj":
                        pe.wait_ge(p_hi, PK)
                        pe.wait_ge(p_lo, PK)
                        for n in range(KT):
                            slot(t + n)
                            mm = product(t + n, [(k * D + n * P, k) for k in range(PK)], phi, plo, w)
                    else:
                        hi, lo, ready = {
                            "pa": (hmhi, hmlo, (bt_hi, bt_lo)), "pb": (ahi, alo, None), "wo": (mghi, mglo, (mg_hi, mg_lo)),
                            "up": (ahi, alo, (c_hi, c_lo)), "pgate": (ehi, elo, (e_hi, e_lo)),
                        }.get(kind, (ahi, alo, None))
                        if i > 0:
                            ready = None
                        if kind == "pb" and i == 0:
                            pe.wait_ge(bt_hi, 2 * KT)
                            pe.wait_ge(bt_lo, 2 * KT)
                        for n in range(2):
                            slot(t + n)
                            mm = product(t + n, [(k * 2 * P + n * P, k) for k in range(KT)], hi, lo, w,
                                         ready=ready if n == 0 else None)
                    if kind == "down" and i % 2 == 0:
                        mm.then_inc(half_done, 1)
                elif s[0] == "bt":
                    which, n = s[1], s[2]
                    v = vm if which == "m" else vg
                    slot(t)
                    pe.wait_ge(tn_done, 2 * (NC + 1))
                    hd, c0 = n // 2, (n % 2) * P
                    for c in range(NC + 1):
                        t0, ln = chunk_span(c)
                        out = ps[:, t % 2, 0, t0:t0 + ln] if c < NC else ps[:, t % 2, 1, 0:ln]
                        mm = nc.tensor.transpose(out, v[0:ln, c, hd, c0:c0 + P], ident[0:ln, 0:ln])
                    mm.then_inc(tile_ready, 1)
                elif s[0] == "rms":
                    pe.wait_ge(sq_sum, s[1] + 1)
                    src = acc if s[1] else acc0
                    for a in range(2):
                        b = bank(j + a)
                        nc.tensor.matmul(b[:, 0:HALF], ones[:, :], src[:, a * HALF:(a + 1) * HALF],
                                         start=True, stop=True).then_inc(aux_ready, 1)
                elif s[0] == "rs_cols":
                    pe.wait_ge(rs_ready, 1)
                    pe.wait_ge(const_in, NCONST)
                    b = bank(j)
                    for c in range(NC + 1):
                        t0, ln = chunk_span(c)
                        mm = nc.tensor.matmul(b[0:ln, c:c + 1], rs[:, t0:t0 + ln], ident[:, 0:1],
                                              start=True, stop=True)
                    mm.then_inc(aux_ready, 1)
                elif s[0] == "rows":
                    pe.wait_ge(row_exp, 4)
                    b = bank(j)
                    for c in range(NC):
                        mm = nc.tensor.transpose(b[:, c * P:(c + 1) * P], rr[:, c * L:(c + 1) * L], ident[:, :])
                    mm.then_inc(aux_ready, 1)
                    b = bank(j + 1)
                    nc.tensor.transpose(b[0:TS, 0:P], rr[:, TP:T], ident[:, :]).then_inc(aux_ready, 1)
                    b = bank(j + 2)
                    n = NC + NB
                    for h in range(H):
                        mm = nc.tensor.matmul(b[:, h * n:(h + 1) * n], sel[:, h, :], rowc[:, 4, :],
                                              start=True, stop=True)
                    mm.then_inc(aux_ready, 1)
                elif s[0] == "mchunk":
                    c = s[1]
                    t0, ln = chunk_span(c)
                    b = bank(j)
                    for h in range(H):
                        mm = nc.tensor.matmul(b[:, h * ln:(h + 1) * ln], sel[:, h, :], r1[:, t0:t0 + ln],
                                              start=True, stop=True)
                    mm.then_inc(aux_ready, 1)
                    b = bank(j + 1)
                    for h in range(H):
                        mm = nc.tensor.matmul(b[:, h * ln:(h + 1) * ln], sel[:, h, :], ri[:, t0:t0 + ln],
                                              start=True, stop=True)
                    mm.then_inc(aux_ready, 1)
                    if c == 0:
                        pe.wait_ge(fm_ready, 2 * H)
                    b = bank(j + 2)
                    for h in range(H):
                        mm = nc.tensor.transpose(b[0:ln, h * P:(h + 1) * P], mk[:, h, t0:t0 + ln], ident[:, :])
                    mm.then_inc(aux_ready, 1)
                    b = bank(j + 3)
                    for h in range(H):
                        mm = nc.tensor.matmul(b[0:ln, h * ln:(h + 1) * ln], mk[:, h, t0:t0 + ln],
                                              mq[:, h, t0:t0 + ln], start=True, stop=True)
                    mm.then_inc(aux_ready, 1)
                    if c < NC:
                        if c == 0:
                            pe.wait_ge(v_ready, H * (NC + 1))
                        pe.wait_ge(kt_ready, c + 1)
                        for h in range(H):
                            b = bank(j + 4 + h)
                            nc.tensor.matmul(b[:, 0:DV + 1], ktok[:, h, :], vm[:, c, h, :], start=True, stop=True)\
                                .then_inc(aux_ready, 1)
                        pe.wait_ge(at_ready, c + 1)
                        pe.wait_ge(qt_ready, c + 1)
                        for h in range(H):
                            b = bank(j + 4 + H + h)
                            mm = nc.tensor.matmul(b[:, 0:DV + 1], att[:, h, :], vm[:, c, h, :],
                                                  start=True, stop=c == 0)
                            if c:
                                pe.wait_ge(c_ready, H * (c - 1) + h + 1)
                                mm = nc.tensor.matmul(b[:, 0:DV + 1], qt[:, h, :], cst[:, c % 2, h, :],
                                                      start=False, stop=True)
                            mm.then_inc(aux_ready, 1)
                elif s[0] == "head":
                    which, h = s[1], s[2]
                    q = head_no[s]
                    v, wd = (vm, DV + 1) if which == "m" else (vg, DV)
                    pe.wait_ge(at_ready, (NC + 1) * (1 + (which == "g")))
                    pe.wait_ge(blk_ready, q + 1)
                    pe.wait_ge(st_in[q % 2], 16 * (q // 2 + 1))
                    if which == "m":
                        pe.wait_ge(st_n, h + 1)
                    else:
                        pe.wait_ge(v_ready, 2 * H * (NC + 1))
                    b = bank(j)
                    nc.tensor.matmul(b[0:TS, 0:wd], att[0:TS, h, 0:TS], v[0:TS, NC, h, 0:wd], start=True, stop=False)
                    for n in range(NB):
                        mm = nc.tensor.matmul(b[0:TS, 0:wd], qb[:, n * TS:(n + 1) * TS], st[q % 2][:, n, 0:wd],
                                              start=False, stop=n == NB - 1)
                    mm.then_inc(aux_ready, 1)
                    for n in range(NB):
                        b = bank(j + 1 + n)
                        nc.tensor.matmul(b[:, 0:wd], kb[:, n, :], v[0:TS, NC, h, 0:wd], start=True, stop=True)\
                            .then_inc(aux_ready, 1)
                elif s[0] == "la":
                    for h in range(H):
                        for a in range(2):
                            b = bank(j + 2 * h + a)
                            nc.tensor.matmul(b[:, 0:HALF], wlr[:, h * DK:(h + 1) * DK],
                                             glr[:, a * HALF:(a + 1) * HALF], start=True, stop=True)\
                                .then_inc(aux_ready, 1)
                elif s[0] == "gchunk":
                    c = s[1]
                    t0, ln = chunk_span(c)
                    levels = PROMPT_LEVELS if c < NC else SAMPLE_LEVELS
                    if c == 0:
                        pe.wait_ge(fm_ready, 4 * H)
                    b = bank(j)
                    for h in range(H):
                        mm = nc.tensor.matmul(b[0:ln, h * ln:(h + 1) * ln], gk[:, h, t0:t0 + ln],
                                              gq[:, h, t0:t0 + ln], start=True, stop=True)
                    mm.then_inc(aux_ready, 1)
                    pe.wait_ge(kf_ready, c + 1)
                    b = bank(j + 1)
                    for h in range(H):
                        mm = nc.tensor.transpose(b[0:ln, h * P:(h + 1) * P], kf[:, h, 0:ln], ident[:, :])
                    mm.then_inc(aux_ready, 1)
                    for n, w in enumerate(levels):
                        counts["lv"] += 1
                        pe.wait_ge(xl_ready, counts["lv"])
                        xl = xl01[:, n % 3, :, :] if n % 3 < 2 else xl2[:, 0, :, :]
                        b = bank(j + 2 + n)
                        for h in range(H):
                            mm = nc.tensor.matmul(b[0:ln, h * ln:(h + 1) * ln], xl[:, h, 0:ln], xl[:, h, 0:ln],
                                                  start=True, stop=True)
                        mm.then_inc(aux_ready, 1)
                    j += 2 + len(levels)
                    if c < NC:
                        if c == 0:
                            pe.wait_ge(v_ready, 2 * H * (NC + 1))
                        pe.wait_ge(kt_ready, NC + 1 + c + 1)
                        for h in range(H):
                            b = bank(j + h)
                            nc.tensor.matmul(b[:, 0:DV], ktok[:, h, :], vg[:, c, h, :], start=True, stop=True)\
                                .then_inc(aux_ready, 1)
                        pe.wait_ge(at_ready, NC + 1 + c + 1)
                        pe.wait_ge(qt_ready, NC + 1 + c + 1)
                        for h in range(H):
                            b = bank(j + H + h)
                            mm = nc.tensor.matmul(b[:, 0:DV], att[:, h, :], vg[:, c, h, :], start=True, stop=c == 0)
                            if c:
                                pe.wait_ge(s_ready, H * (c - 1) + h + 1)
                                mm = nc.tensor.matmul(b[:, 0:DV], qt[:, h, :], gst[:, c % 2, h, :],
                                                      start=False, stop=True)
                            mm.then_inc(aux_ready, 1)

        @block.vector
        def _(dve):
            V = nc.vector
            n_step = [0]

            def link(ins):
                n_step[0] += 1
                ins.then_inc(dve_step, 1)
                dve.wait_ge(dve_step, n_step[0])

            def job(j):
                dve.wait_ge(aux_ready, j + 1)
                return aux[:, j % 4, :]

            def free(ins, j):
                ins.then_inc(aux_free[j % 4], 1)

            V.memset(ones[:, :], 1.0)
            V.memset(reset[:, :], 1.0)
            V.memset(qb[:, :], 0.0)
            link(V.memset(rowc[:, :, :], 0.0))
            V.memset(reset[:, 0:TP:L], 0.0)
            V.memset(reset[:, TP:T:LS], 0.0).then_inc(init_done, 1)
            dve.wait_ge(init_done, 1)

            lv = 0
            ng = {"gt": 0, "stg": 0, "tn": 0}

            def rms(n, j):
                out = rsv if n else rs
                tmp = sq2[:, :] if n else sq[:, 0, :]
                for a in range(2):
                    b = job(j + a)
                    free(V.tensor_scalar(tmp[:, a * HALF:(a + 1) * HALF], b[:, 0:HALF], 1.0 / D, EPS,
                                         ALU.mult, ALU.add), j + a)
                for a in range(2):
                    dve.wait_ge(aux_free[(j + a) % 4], (j + a) // 4 + 1)
                dve.sem_inc(ms_ready, 1)
                dve.wait_ge(rs_guess, n + 1)
                t = sq[:, 1, :] if not n else vrs[:, :]
                link(V.tensor_tensor(t, out[:, :], out[:, :], ALU.mult))
                link(V.tensor_tensor(t, t, tmp, ALU.mult))
                link(V.tensor_scalar(t, t, -0.5, 1.5, ALU.mult, ALU.add))
                V.tensor_tensor(out[:, :], out[:, :], t, ALU.mult).then_inc(rs_ready, 1)
                dve.wait_ge(rs_ready, n + 1)

            def split_lo_of(dst, src, hi, done):
                V.tensor_tensor(dst, src, f32(hi), ALU.subtract).then_inc(done, 1)

            def add_square(n, x):
                if n == 0:
                    link(V.tensor_tensor(acc[:, :], x, x, ALU.mult))
                else:
                    link(V.tensor_tensor(sq2[:, :], x, x, ALU.mult))
                    i = V.tensor_tensor(acc[:, :], acc[:, :], sq2[:, :], ALU.add)
                    if n == KT - 1:
                        i.then_inc(sq_sum, 1)
                    else:
                        link(i)

            def evac(kind, i, t):
                dve.wait_ge(tile_ready, t + 1)
                full, fr = tile(t), tile_free[t % 2]
                if kind == "misc":
                    p = ps[:, t % 2, :, 0:HALF]
                    V.tensor_tensor(two(rowt[ROW_LI][:, :]), p[0:H], two(rs[0:H, :]), ALU.mult)
                    V.tensor_copy(two(rowt[ROW_XF][:, :]), p[32:32 + H])
                    V.tensor_copy(two(glr[:, :]), p[64:64 + RANK]).then_inc(fr, 1)
                    dve.wait_ge(fr, t // 2 + 1)
                    V.tensor_tensor(rowt[ROW_XF][:, :], rowt[ROW_XF][:, :], rs[0:H, :], ALU.mult)
                    link(V.tensor_tensor(glr[:, :], glr[:, :], rs[0:RANK, :], ALU.mult))
                elif kind in ("mq", "mk", "gq", "gk"):
                    dst = {"mq": mq, "mk": mk, "gq": gq, "gk": gk}[kind][:, i, :]
                    c = DK ** -0.5 if kind in ("mk", "gq") else 1.0
                    ins_ = V.scalar_tensor_tensor(two(dst), full, c, two(rs[:, :]), ALU.mult, ALU.mult)
                    ins_.then_inc(fr, 1)
                    dve.wait_ge(fr, t // 2 + 1)
                    dve.sem_inc(fm_ready, 1)
                elif kind in ("mo", "gg", "ga", "gb"):
                    k = ng["stg"]
                    ng["stg"] += 1
                    if k >= 2:
                        dve.wait_ge(stg_out[k % 2], 16 * (k // 2))
                    V.tensor_tensor(two(stg[:, k % 2, :]), full, two(rs[:, :]), ALU.mult).then_inc(fr, 1)
                elif kind == "pa":
                    g = gt_take()
                    V.tensor_tensor(two(merged[:, i, :]), full, two(gt[:, g % 2, :]), ALU.mult).then_inc(fr, 1)
                    dve.wait_ge(fr, t // 2 + 1)
                    dve.sem_inc(gt_used, 1)
                elif kind == "pb":
                    g = gt_take()
                    V.tensor_tensor(two(gt[:, g % 2, :]), full, two(gt[:, g % 2, :]), ALU.mult).then_inc(fr, 1)
                    dve.wait_ge(fr, t // 2 + 1)
                    link(V.tensor_tensor(merged[:, i, :], merged[:, i, :], gt[:, g % 2, :], ALU.add))
                    dve.sem_inc(gt_used, 1)
                    dve.sem_inc(mg_pre, 1)
                    dve.wait_ge(mg_hi, i + 1)
                    split_lo_of(mglo[:, i, :], merged[:, i, :], mghi[:, i, :], mg_lo)
                elif kind == "wo":
                    dve.wait_ge(xr_in[i % 2], 16 * (i // 2 + 1))
                    if i >= 2:
                        dve.wait_ge(hs_out[i % 2], 16 * (i // 2))
                    x = hst[:, i % 2, :]
                    V.tensor_tensor(two(x), full, two(xr[:, i % 2, :]), ALU.add).then_inc(fr, 1)
                    dve.wait_ge(fr, t // 2 + 1)
                    dve.sem_inc(h_pre, 1)
                    add_square(i, x)
                    dve.wait_ge(c_hi, i + 1)
                    V.scalar_tensor_tensor(alo[:, i, :], x, gains[:, NORM_FFN, i:i + 1], f32(ahi[:, i, :]),
                                           ALU.mult, ALU.subtract).then_inc(c_lo, 1)
                elif kind == "gate":
                    if i >= 1:
                        dve.wait_ge(ff_g, 2 * i)
                    p0, p1 = ps[:, t % 2, 0, :], ps[:, t % 2, 1, :]
                    n1 = TP - HALF
                    tail = gbuf[:, 2 + TP:].rearrange("p (b s) -> p b s", s=2 + LS)
                    if i == 0:
                        V.memset(gbuf[:, 0:2], 0.0)
                    V.tensor_copy(tail[:, :, 0:2], convst[:, i, :, :])
                    V.tensor_tensor(gbuf[:, 2:2 + HALF], p0[:, 0:HALF], rsv[:, 0:HALF], ALU.mult)
                    V.tensor_tensor(gbuf[:, 2 + HALF:2 + TP], p1[:, 0:n1], rsv[:, HALF:TP], ALU.mult)
                    V.tensor_tensor(tail[:, :, 2:], p1[:, n1:HALF].rearrange("p (b s) -> p b s", s=LS),
                                    rsv[:, TP:].rearrange("p (b s) -> p b s", s=LS), ALU.mult).then_inc(fr, 1)
                    dve.wait_ge(fr, t // 2 + 1)
                    dve.sem_inc(ff_g, 1)
                    n = GW - 2
                    c = cv[:, 2:]
                    link(V.tensor_scalar(c, gbuf[:, 2:], convw[:, 2, i:i + 1], convb[:, i:i + 1], ALU.mult, ALU.add))
                    link(V.scalar_tensor_tensor(c, gbuf[:, 1:1 + n], convw[:, 1, i:i + 1], c, ALU.mult, ALU.add))
                    V.scalar_tensor_tensor(c, gbuf[:, 0:n], convw[:, 0, i:i + 1], c, ALU.mult, ALU.add)\
                        .then_inc(ff_cv, 1)
                elif kind == "val":
                    V.tensor_tensor(two(vrs[:, :]), full, two(rsv[:, :]), ALU.mult).then_inc(fr, 1)
                    dve.wait_ge(ff_sg, i + 1)
                    link(V.tensor_tensor(cv[:, 2:], cv[:, 2:], sg[:, 2:], ALU.mult))
                    dve.wait_ge(fr, t // 2 + 1)
                    tail = cv[:, 2 + TP:].rearrange("p (b s) -> p b s", s=2 + LS)
                    V.tensor_tensor(af[:, 0:TP], cv[:, 2:2 + TP], vrs[:, 0:TP], ALU.mult)
                    V.tensor_tensor(af[:, TP:].rearrange("p (b s) -> p b s", s=LS), tail[:, :, 2:],
                                    vrs[:, TP:].rearrange("p (b s) -> p b s", s=LS), ALU.mult).then_inc(ff_pre, 1)
                    dve.wait_ge(ff_hi, i + 1)
                    split_lo_of(aclo[:, i, :], af[:, :], achi[:, i, :], ff_lo)
                    dve.wait_ge(ff_lo, i + 1)
                elif kind == "down":
                    if i == 0:
                        dve.wait_ge(p_hi, PK)
                        V.tensor_tensor(plo[:, :, :], praw[:, :, :], f32(phi[:, :, :]), ALU.subtract)\
                            .then_inc(p_lo, PK)
                        dve.wait_ge(h2_in, 16)
                    x = h2[:, i, :]
                    V.tensor_tensor(two(x), full, two(x), ALU.add).then_inc(fr, 1)
                    dve.wait_ge(fr, t // 2 + 1)
                    dve.sem_inc(h2_new, 1)
                    add_square(i, x)
                elif kind == "pproj":
                    V.tensor_copy(two(pj[:, i, :]), full).then_inc(fr, 1)
                    dve.wait_ge(fr, t // 2 + 1)
                    dve.wait_ge(e_hi, i + 1)
                    V.scalar_tensor_tensor(elo[:, i, :], h2[:, i, :], gains[:, NORM_PLE, i:i + 1],
                                           f32(ehi[:, i, :]), ALU.mult, ALU.subtract).then_inc(e_lo, 1)
                elif kind == "pgate":
                    g = sgp[:, i % 2, :]
                    V.tensor_tensor(two(g), full, two(rsv[:, :]), ALU.mult).then_inc(fr, 1)
                    dve.wait_ge(fr, t // 2 + 1)
                    dve.sem_inc(pg_pre, 1)
                    dve.wait_ge(pg_sig, i + 1)
                    link(V.tensor_tensor(g, g, pj[:, i, :], ALU.mult))
                    link(V.tensor_tensor(h3[:, i, :], g, h2[:, i, :], ALU.add))
                    add_square(i, h3[:, i, :])

            def gt_take():
                k = ng["gt"]
                ng["gt"] += 1
                dve.wait_ge(gt_sig, k + 1)
                return k

            def tnorm(which, c):
                n = ng["tn"]
                ng["tn"] += 1
                t0, ln = chunk_span(c)
                v = (vm if which == "m" else vg)[0:ln, c]
                S = [nsm[0:ln, k, :] for k in range(6)]
                mean, var = nmv[0:ln, :, 0], nmv[0:ln, :, 1]
                dve.wait_ge(h_out, h_out_of[(which, c)])
                for h in range(H):
                    i = V.bn_stats(nstat[0:ln, h, :], v[:, h, 0:DV])
                link(i)
                for h in range(H):
                    i = V.bn_aggr(nmv[0:ln, h, :], nstat[0:ln, h, :])
                link(i)
                if which == "m":
                    link(V.scalar_tensor_tensor(S[0], v[:, :, DV], -1.0, v[:, :, DV], ALU.mult, ALU.max))
                    link(V.tensor_tensor(S[0], S[0], colT[0:ln, c, 2, :], ALU.max))
                    link(V.reciprocal(S[1], S[0]))
                    link(V.tensor_tensor(S[2], var, S[1], ALU.mult))
                    link(V.tensor_tensor(S[2], S[2], S[1], ALU.mult))
                else:
                    link(V.tensor_tensor(S[2], mean, mean, ALU.mult))
                    link(V.tensor_tensor(S[2], S[2], var, ALU.add))
                V.tensor_scalar(S[2], S[2], 1.0, EPS, ALU.mult, ALU.add).then_inc(tn_pre, 1)
                dve.wait_ge(tn_exp, n + 1)
                link(V.tensor_tensor(S[4], S[3], S[3], ALU.mult))
                link(V.tensor_tensor(S[4], S[4], S[2], ALU.mult))
                link(V.tensor_scalar(S[4], S[4], -0.5, 1.5, ALU.mult, ALU.add))
                link(V.tensor_tensor(S[3], S[3], S[4], ALU.mult))
                if which == "m":
                    link(V.tensor_tensor(S[3], S[3], S[1], ALU.mult))
                for h in range(H):
                    if which == "m":
                        i = V.tensor_scalar(v[:, h, 0:DV], v[:, h, 0:DV], nmv[0:ln, h, 0:1], nsm[0:ln, 3, h:h + 1],
                                            ALU.subtract, ALU.mult)
                    else:
                        i = V.tensor_scalar(v[:, h, 0:DV], v[:, h, 0:DV], nsm[0:ln, 3, h:h + 1], None, ALU.mult)
                i.then_inc(tn_done, 1)
                dve.wait_ge(tn_done, n + 1)

            for s in sched_v:
                j, t = job_at[s], tile_at.get(s)
                if s[0] == "norm_in":
                    dve.wait_ge(gains_in, 16)
                    for k in range(KT):
                        dve.wait_ge(a_hi, k + 1)
                        V.scalar_tensor_tensor(alo[:, k, :], xT[:, k, :], gains[:, NORM_MIX, k:k + 1],
                                               f32(ahi[:, k, :]), ALU.mult, ALU.subtract).then_inc(a_lo, 1)
                        dve.wait_ge(in_sq, k + 1)
                        if k == 0:
                            i = V.tensor_copy(acc0[:, :], sq[:, 0, :])
                        else:
                            i = V.tensor_tensor(acc0[:, :], acc0[:, :], sq[:, k % 2, :], ALU.add)
                        i.then_inc(in_sq_used, 1)
                        dve.wait_ge(in_sq_used, k + 1)
                    dve.sem_inc(sq_sum, 1)
                elif s[0] == "unit":
                    for n, (kind, i) in enumerate(tiles_of(*units[s[1]])):
                        if kind in ("mv", "gv"):
                            continue
                        evac(kind, i, t + n)
                elif s[0] == "rms":
                    rms(s[1], j)
                    if s[1] == 3:
                        for n in range(KT):
                            if n >= 2:
                                dve.wait_ge(y_out[n % 2], 16 * (n // 2))
                            V.scalar_tensor_tensor(yt[:, n % 2, :], h3[:, n, :], gains[:, NORM_OUT, n:n + 1],
                                                   rsv[:, :], ALU.mult, ALU.mult).then_inc(y_ready, 1)
                elif s[0] == "rs_cols":
                    b = job(j)
                    V.tensor_copy(rscol[:, 0:NC], b[:, 0:NC])
                    i = V.tensor_copy(rscol[0:TS, NC:NC + 1], b[0:TS, NC:NC + 1])
                    free(i, j)
                    dve.wait_ge(aux_free[j % 4], j // 4 + 1)
                    dve.sem_inc(rsc_ready, 1)
                elif s[0] == "rows":
                    dve.wait_ge(const_in, NCONST)
                    R = [x[:, :] for x in rowt]
                    V.tensor_copy(cmask[:, :, :], cmaskf[:, :, :])
                    link(V.memset(rr[:, :], 0.0))
                    V.tensor_scalar(R[ROW_LI], R[ROW_LI], bgate[:, 0:1], None, ALU.add)
                    link(V.tensor_scalar(R[ROW_XF], R[ROW_XF], bgate[:, 1:2], None, ALU.add))
                    V.scalar_tensor_tensor(R[ROW_T], R[ROW_XF], -1.0, R[ROW_XF], ALU.mult, ALU.max)\
                        .then_inc(row_abs, 1)
                    dve.wait_ge(row_ln, 1)
                    link(V.scalar_tensor_tensor(R[ROW_LF], R[ROW_XF], 0.0, R[ROW_T], ALU.min, ALU.subtract))
                    V.tensor_tensor_scan(R[ROW_B], reset[0:H, :], R[ROW_LF], 0.0, ALU.mult, ALU.add)
                    V.tensor_copy(R[ROW_D0], R[ROW_LF])
                    V.tensor_copy(R[ROW_D1], R[ROW_LI])
                    link(V.tensor_tensor(rowc[:, 0, 0:NB], R[ROW_LF][:, TP:T:LS], m0[:, :], ALU.add))
                    V.memset(R[ROW_D0][:, TP:T:LS], -3.0e38)
                    link(V.tensor_tensor(R[ROW_D1][:, TP:T:LS], rowc[:, 0, 0:NB], R[ROW_LI][:, TP:T:LS], ALU.max))
                    link(V.tensor_tensor_scan(R[ROW_M], R[ROW_D0], R[ROW_D1], 0.0, ALU.add, ALU.max))
                    V.memset(rowc[:, 1, 0:1], 0.0)
                    V.tensor_copy(rowc[:, 1, 1:NC], R[ROW_M][:, L - 1:TP - 1:L])
                    V.tensor_copy(rowc[:, 1, NC:], m0[:, :])
                    V.tensor_copy(rowc[:, 2, 0:NC], R[ROW_B][:, L - 1:TP:L])
                    V.tensor_copy(rowc[:, 2, NC:], R[ROW_B][:, TP + LS - 1:T:LS])
                    V.tensor_copy(rowc[:, 3, 0:NC], R[ROW_M][:, L - 1:TP:L])
                    V.tensor_copy(rowc[:, 3, NC:], R[ROW_M][:, TP + LS - 1:T:LS])
                    V.tensor_tensor(r1[:, :], R[ROW_B], R[ROW_M], ALU.subtract)
                    link(V.tensor_tensor(rr[0:H, :], R[ROW_LI], R[ROW_B], ALU.subtract))
                    V.tensor_copy(mout[:, 0:NB], rowc[:, 3, NC:])
                    V.tensor_copy(mout[:, NB:], rowc[:, 3, NC - 1:NC])
                    link(V.tensor_tensor(rowc[:, 2, :], rowc[:, 2, :], rowc[:, 3, :], ALU.subtract))
                    link(V.tensor_tensor(rowc[:, 4, :], rowc[:, 2, :], rowc[:, 1, :], ALU.add))

                    def spread(dst, row, k):
                        for lo, hi, n, w, c0 in ((0, TP, NC, L, 0), (TP, T, NB, LS, NC)):
                            V.tensor_tensor(dst[:, lo:hi].rearrange("p (c s) -> p c s", s=w),
                                            row[:, lo:hi].rearrange("p (c s) -> p c s", s=w),
                                            bcast(rowc[:, k, c0:c0 + n], w, 2), ALU.add)
                    spread(ri[:, :], r1[:, :], 1)
                    spread(R[ROW_T], rr[0:H, :], 2)
                    link(V.tensor_scalar(rowc[:, 4, :], rowc[:, 4, :], 0.0, None, ALU.min))
                    V.tensor_scalar(ri[:, :], ri[:, :], 0.0, None, ALU.min)
                    V.tensor_scalar(R[ROW_T], R[ROW_T], 0.0, None, ALU.min).then_inc(row_pre, 1)
                    b = job(j)
                    for c in range(NC):
                        i = V.tensor_copy(colT[:, c], b[:, c * P:(c + 1) * P]
                                          .rearrange("p (r k) -> p r k", k=32)[:, 0:3, 0:H])
                    free(i, j)
                    b = job(j + 1)
                    free(V.tensor_copy(colT[0:TS, NC], b[0:TS, 0:P].rearrange("p (r k) -> p r k", k=32)[:, 0:3, 0:H]),
                         j + 1)
                    b = job(j + 2)
                    free(V.tensor_copy(carry[:, :, :].rearrange("p h c -> p (h c)"), b[:, 0:H * (NC + NB)]), j + 2)
                    dve.wait_ge(aux_free[(j + 2) % 4], (j + 2) // 4 + 1)
                elif s[0] == "mchunk":
                    c = s[1]
                    t0, ln = chunk_span(c)

                    def hv(x, n=ln):
                        return x.rearrange("p (h s) -> p h s", h=H)
                    b = job(j)
                    for h in range(H):
                        i = V.scalar_tensor_tensor(pw[0:ln, h, 0:ln], b[0:ln, h * ln:(h + 1) * ln],
                                                   colT[0:ln, c, 0, h:h + 1], nmask[0:ln, int(c == NC), 0:ln],
                                                   ALU.add, ALU.min)
                    free(i, j)
                    dve.wait_ge(aux_free[j % 4], j // 4 + 1)
                    dve.sem_inc(p_pre, 1)
                    b = job(j + 1)
                    i = V.tensor_tensor(qt[:, :, 0:ln], mq[:, :, t0:t0 + ln], hv(b[:, 0:H * ln]), ALU.mult)
                    free(i, j + 1)
                    dve.wait_ge(aux_free[(j + 1) % 4], (j + 1) // 4 + 1)
                    dve.sem_inc(qt_ready, 1)
                    b = job(j + 2)
                    i = V.tensor_tensor(ktok[0:ln, :, :], hv(b[0:ln, 0:H * P]), bcast(colT[0:ln, c, 1, :], P, 2),
                                        ALU.mult)
                    free(i, j + 2)
                    dve.wait_ge(aux_free[(j + 2) % 4], (j + 2) // 4 + 1)
                    dve.sem_inc(kt_ready, 1)
                    b = job(j + 3)
                    dve.wait_ge(p_exp, c + 1)
                    i = V.tensor_tensor(att[0:ln, :, 0:ln], pw[0:ln, :, 0:ln], hv(b[0:ln, 0:H * ln]), ALU.mult)
                    free(i, j + 3)
                    dve.wait_ge(aux_free[(j + 3) % 4], (j + 3) // 4 + 1)
                    dve.sem_inc(at_ready, 1)
                    if c < NC:
                        for h in range(H):
                            b = job(j + 4 + h)
                            new = cst[:, (c + 1) % 2, h, :]
                            if c == 0:
                                i = V.tensor_copy(new, b[:, 0:DV + 1])
                            else:
                                i = V.scalar_tensor_tensor(new, cst[:, c % 2, h, :], carry[:, h, c:c + 1],
                                                           b[:, 0:DV + 1], ALU.mult, ALU.add)
                            free(i, j + 4 + h)
                            dve.wait_ge(aux_free[(j + 4 + h) % 4], (j + 4 + h) // 4 + 1)
                            dve.sem_inc(c_ready, 1)
                        if c == NC - 1:
                            V.tensor_copy(nout[:, :, NB], cst[:, 0, :, DV]).then_inc(c_ready, 1)
                elif s[0] == "la":
                    dve.wait_ge(aux_ready, j)
                    for h in range(H):
                        for a in range(2):
                            b = job(j + 2 * h + a)
                            i = V.tensor_scalar(cum[:, h, a * HALF:(a + 1) * HALF], b[:, 0:HALF], blr[:, h:h + 1],
                                                None, ALU.add)
                            free(i, j + 2 * h + a)
                        dve.wait_ge(aux_free[(j + 2 * h + 1) % 4], (j + 2 * h + 1) // 4 + 1)
                        V.scalar_tensor_tensor(stg[:, h % 2, :], cum[:, h, :], -1.0, cum[:, h, :], ALU.mult, ALU.max)\
                            .then_inc(la_abs, 1)
                        dve.wait_ge(la_ln, h + 1)
                        link(V.scalar_tensor_tensor(cum[:, h, :], cum[:, h, :], 0.0, stg[:, h % 2, :],
                                                    ALU.min, ALU.subtract))
                        V.tensor_tensor_scan(cum[:, h, :], reset[:, :], cum[:, h, :], 0.0, ALU.mult, ALU.add)\
                            .then_inc(cum_ready, 1)
                    dve.wait_ge(cum_ready, H)
                elif s[0] == "gchunk":
                    c = s[1]
                    t0, ln = chunk_span(c)
                    levels = PROMPT_LEVELS if c < NC else SAMPLE_LEVELS
                    nseq, sl = (1, L) if c < NC else (NB, LS)

                    def seqs(x):
                        return x.rearrange("p h (b s) -> p h b s", s=sl)
                    cc = cum[:, :, t0:t0 + ln]
                    dve.wait_ge(aux_ready, j)
                    if c == 0:
                        dve.wait_ge(st_out[1], out_count(3))
                    dve.sem_inc(g_go, 1)
                    link(V.memset(att[:, :, :], 0.0))
                    b = job(j)
                    i = V.copy_predicated(att[0:ln, :, 0:ln], bcast(cmask[0:ln, 7, 0:ln], H, 1),
                                          b[0:ln, 0:H * ln].rearrange("p (h s) -> p h s", h=H))
                    free(i, j)
                    for h in range(H):
                        x = cc[:, h, :].rearrange("p (b s) -> p b s", s=sl)
                        i = V.tensor_tensor(kf[:, h, 0:ln].rearrange("p (b s) -> p b s", s=sl),
                                            bcast(x[:, :, sl - 1], sl, 2), x, ALU.subtract)
                    i.then_inc(kd_sub, 1)

                    def sub(n):
                        w = levels[n]
                        xl = xl01[:, n % 3, :, 0:ln] if n % 3 < 2 else xl2[:, 0, :, 0:ln]
                        for h in range(H):
                            x = cc[:, h, :].rearrange("p (b s) -> p b s", s=2 * w)
                            i = V.tensor_tensor(xl[:, h, :].rearrange("p (b s) -> p b s", s=2 * w), x,
                                                bcast(x[:, :, w - 1], 2 * w, 2), ALU.subtract)
                        i.then_inc(xl_sub, 1)

                    def weigh(n):
                        w = levels[n]
                        xl = xl01[:, n % 3, :, 0:ln] if n % 3 < 2 else xl2[:, 0, :, 0:ln]
                        dve.wait_ge(xl_exp, lv + n + 1)
                        for src, lo in ((gk, 0), (gq, w)):
                            x = xl.rearrange("p h (b s) -> p h b s", s=2 * w)[:, :, :, lo:lo + w]
                            y = src[:, :, t0:t0 + ln].rearrange("p h (b s) -> p h b s", s=2 * w)[:, :, :, lo:lo + w]
                            i = V.tensor_tensor(x, x, y, ALU.mult)
                        i.then_inc(xl_ready, 1)

                    def place(n):
                        last = j + 1 + n if n else j
                        dve.wait_ge(aux_free[last % 4], last // 4 + 1)
                        b = job(j + 2 + n)
                        k = PROMPT_LEVELS.index(levels[n])
                        i = V.copy_predicated(att[0:ln, :, 0:ln], bcast(cmask[0:ln, k, 0:ln], H, 1),
                                              b[0:ln, 0:H * ln].rearrange("p (h s) -> p h s", h=H))
                        free(i, j + 2 + n)

                    sub(0)
                    dve.wait_ge(kd_exp, c + 1)
                    V.tensor_tensor(kf[:, :, 0:ln], kf[:, :, 0:ln], gk[:, :, t0:t0 + ln], ALU.mult)\
                        .then_inc(kf_ready, 1)
                    dve.wait_ge(eb_ready, c + 1)
                    V.tensor_tensor(qt[:, :, 0:ln], pw[:, :, 0:ln], gq[:, :, t0:t0 + ln], ALU.mult)\
                        .then_inc(qt_ready, 1)
                    b = job(j + 1)
                    i = V.tensor_copy(ktok[0:ln, :, :], b[0:ln, 0:H * P].rearrange("p (h s) -> p h s", h=H))
                    free(i, j + 1)
                    dve.wait_ge(aux_free[(j + 1) % 4], (j + 1) // 4 + 1)
                    dve.sem_inc(kt_ready, 1)
                    for n in range(len(levels)):
                        if n + 1 < len(levels):
                            sub(n + 1)
                        weigh(n)
                        if n:
                            place(n - 1)
                    place(len(levels) - 1)
                    jl = j + 1 + len(levels)
                    dve.wait_ge(aux_free[jl % 4], jl // 4 + 1)
                    dve.sem_inc(at_ready, 1)
                    lv += len(levels)
                    j = jl + 1
                    if c < NC:
                        for h in range(H):
                            b = job(j + h)
                            new = gst[:, (c + 1) % 2, h, :]
                            if c == 0:
                                i = V.tensor_copy(new, b[:, 0:DV])
                            else:
                                i = V.scalar_tensor_tensor(new, gst[:, c % 2, h, :], pw[:, h, L - 1:L], b[:, 0:DV],
                                                           ALU.mult, ALU.add)
                            free(i, j + h)
                            dve.wait_ge(aux_free[(j + h) % 4], (j + h) // 4 + 1)
                            dve.sem_inc(s_ready, 1)
                elif s[0] == "head":
                    which, h = s[1], s[2]
                    q = head_no[s]
                    x = st[q % 2]
                    wd = DV + 1 if which == "m" else DV
                    dve.wait_ge(aux_ready, j)
                    V.tensor_copy(qb[:, :].rearrange("p (b s) -> p b s", s=TS + LS)[:, :, 0:LS],
                                  qt[:, h, 0:TS].rearrange("p (b s) -> p b s", s=LS))
                    V.tensor_tensor(kb[:, :, :], bcast(ktok[0:TS, h, :], NB, 1), bcast(bmask[:, :], P, 2), ALU.mult)\
                        .then_inc(blk_ready, 1)
                    dve.wait_ge(st_in[q % 2], 16 * (q // 2 + 1))
                    if which == "m":
                        V.tensor_copy(x[:, :, DV], nst[:, h, :]).then_inc(st_n, 1)
                        dve.wait_ge(st_n, h + 1)
                    for n in range(NB):
                        b = job(j + 1 + n)
                        k = carry[:, h, NC + n:NC + n + 1] if which == "m" else \
                            pw[:, h, (n + 1) * LS - 1:(n + 1) * LS]
                        i = V.scalar_tensor_tensor(x[:, n, 0:wd], x[:, n, 0:wd], k, b[:, 0:wd], ALU.mult, ALU.add)
                        free(i, j + 1 + n)
                    dve.wait_ge(aux_free[(j + NB) % 4], (j + NB) // 4 + 1)
                    if which == "m":
                        link(V.tensor_copy(nout[:, h, 0:NB], x[:, :, DV]))
                    dve.sem_inc(st_new, 1)
                elif s[0] == "tnorm":
                    tnorm(s[1], s[2])
                elif s[0] == "bt":
                    which, n = s[1], s[2]
                    dve.wait_ge(tile_ready, t + 1)
                    if which == "m" and n == 0:
                        for k in range(2):
                            dve.wait_ge(st_out[k], out_count(6 + k))
                    g = gt_take()
                    k = gains[:, NORM_M if which == "m" else NORM_G, n:n + 1]
                    V.scalar_tensor_tensor(bt_t[:, 0, 0:TP], ps[:, t % 2, 0, 0:TP], k, gt[:, g % 2, 0:TP],
                                           ALU.mult, ALU.mult)
                    V.scalar_tensor_tensor(bt_t[:, 0, TP:], ps[:, t % 2, 1, 0:TS], k, gt[:, g % 2, TP:],
                                           ALU.mult, ALU.mult).then_inc(tile_free[t % 2], 1)
                    dve.wait_ge(tile_free[t % 2], t // 2 + 1)
                    dve.sem_inc(gt_used, 1)
                    dve.sem_inc(bt_pre, 1)
                    m = n + (KT if which == "g" else 0)
                    dve.wait_ge(bt_hi, m + 1)
                    split_lo_of((hmlo if which == "m" else alo)[:, n, :], bt_t[:, 0, :],
                                (hmhi if which == "m" else ahi)[:, n, :], bt_lo)
                    dve.wait_ge(bt_lo, m + 1)

        @block.scalar
        def _(act):
            A = nc.scalar
            n_step = [0]

            def link(ins):
                n_step[0] += 1
                ins.then_inc(act_step, 1)
                act.wait_ge(act_step, n_step[0])

            def hi_part(u):
                s, n = u % 2, width(u)
                act.wait_ge(raw_in[s], raw_count(u))
                if u >= 2:
                    used(act, u - 2)
                A.activation(whi[:, s, 0:n], wraw[:, s, 0:n], ACT.Copy).then_inc(split_hi, 1)

            def root(src, dst, done):
                link(A.activation(dst, src, ACT.Ln))
                A.activation(dst, dst, ACT.Exp, scale=-0.5).then_inc(done, 1)

            gate_use = []
            for s in sched:
                if s[0] == "bt":
                    gate_use.append(((ZMO if s[1] == "m" else ZGG) + s[2], s[1] == "g"))
                elif s[0] == "unit" and units[s[1]][0] in ("pa", "pb"):
                    z = ZGA if units[s[1]][0] == "pa" else ZGB
                    gate_use += [(z + i, False) for _, i in tiles_of(*units[s[1]])]
            ng = {"gt": 0, "gl": 0, "stg": 0, "tn": 0, "lv": 0}

            def gate_load():
                k = ng["gl"]
                if k >= len(gate_use):
                    return
                ng["gl"] += 1
                if k >= 2:
                    act.wait_ge(gt_used, k - 1)
                z = gate_use[k][0]
                act.wait_ge(stg_out[z % 2], 16 * (z // 2 + 1))
                act.dma_start(gt[:, k % 2, :], zs[z, :, :]).then_inc(gt_in[k % 2], 16)

            def gate_sigmoid():
                k = ng["gt"]
                ng["gt"] += 1
                act.wait_ge(gt_in[k % 2], 16 * (k // 2 + 1))
                fn = ACT.Silu if gate_use[k][1] else ACT.Sigmoid
                A.activation(gt[:, k % 2, :], gt[:, k % 2, :], fn).then_inc(gt_sig, 1)

            def state_load(q):
                if q >= 2:
                    act.wait_ge(st_out[q % 2], out_count(q - 2))
                if q == 5:
                    act.wait_ge(cp_out, 32)
                src = ins["C_in"] if q < H else ins["S_in"]
                act.dma_start(st[q % 2][:, :, 0:DV], src[q % H, :, :, :]).then_inc(st_in[q % 2], 16)

            def copy_out(j, dst, src_p, wd):
                act.wait_ge(aux_ready, j + 1)
                i = A.activation(dst, aux[0:src_p, j % 4, 0:wd], ACT.Copy)
                i.then_inc(aux_free[j % 4], 1)
                act.wait_ge(aux_free[j % 4], j // 4 + 1)
                act.sem_inc(h_out, 1)

            for n in range(4):
                act.dma_start(xT[:, 2 * n:2 * n + 2, :], ins["xT"][:, 2 * n:2 * n + 2, :]).then_inc(x_in[n], 16)
            act.wait_ge(gains_in, 16)
            for s in sched_v:
                j, t = job_at[s], tile_at.get(s)
                if s[0] == "norm_in":
                    for k in range(KT):
                        act.wait_ge(x_in[k // 2], 16)
                        A.activation(ahi[:, k, :], xT[:, k, :], ACT.Copy, scale=gains[:, NORM_MIX, k:k + 1])\
                            .then_inc(a_hi, 1)
                        if k >= 2:
                            act.wait_ge(in_sq_used, k - 1)
                        A.activation(sq[:, k % 2, :], xT[:, k, :], ACT.Square).then_inc(in_sq, 1)
                        if k == 0:
                            hi_part(0)
                    hi_part(1)
                elif s[0] == "unit":
                    u = s[1]
                    if u >= 1 and u + 1 < len(units):
                        hi_part(u + 1)
                    kind, i0 = units[u]
                    for n, (kind, i) in enumerate(tiles_of(kind, i0)):
                        tt = t + n
                        if kind in ("mv", "gv"):
                            h, c = i
                            t0, ln = chunk_span(c)
                            if kind == "mv" and h == 0 and c == 0:
                                act.wait_ge(a_lo, KT)
                                act.wait_ge(rsc_ready, 1)
                                A.activation(vm[:, 0:NC, :, DV], ones[:, 0:NC * H]
                                             .rearrange("p (c h) -> p c h", h=H), ACT.Copy)
                                A.activation(vm[0:TS, NC, :, DV], ones[0:TS, 0:H], ACT.Copy)
                            if kind == "gv" and h == 0 and c == 0:
                                act.wait_ge(cp_out, 16)
                                act.wait_ge(aux_ready, job_at[("mchunk", NC)] + 4)
                            act.wait_ge(tile_ready, tt + 1)
                            dst = vm[0:ln, c, h, 0:DV] if kind == "mv" else vg[0:ln, c, h, :]
                            A.activation(dst, ps[0:ln, tt % 2, 0, 0:DV], ACT.Copy, scale=rscol[0:ln, c:c + 1])\
                                .then_inc(tile_free[tt % 2], 1)
                            act.wait_ge(tile_free[tt % 2], tt // 2 + 1)
                            act.sem_inc(v_ready, 1)
                        elif kind in ("mo", "gg", "ga", "gb"):
                            k = ng["stg"]
                            ng["stg"] += 1
                            act.wait_ge(tile_free[tt % 2], tt // 2 + 1)
                            act.dma_start(zs[k, :, :], stg[:, k % 2, :]).then_inc(stg_out[k % 2], 16)
                        elif kind in ("pa", "pb"):
                            gate_sigmoid()
                            if kind == "pb":
                                act.wait_ge(mg_pre, i + 1)
                                A.activation(mghi[:, i, :], merged[:, i, :], ACT.Copy).then_inc(mg_hi, 1)
                            if kind == "pb" and i == KT - 1:
                                act.wait_ge(mg_lo, KT)
                                for k in range(2):
                                    act.dma_start(xr[:, k, :], ins["xT"][:, k, :]).then_inc(xr_in[k], 16)
                            gate_load()
                        elif kind == "wo":
                            act.wait_ge(h_pre, i + 1)
                            act.dma_start(hs[i, :, :], hst[:, i % 2, :]).then_inc(hs_out[i % 2], 16)
                            if i + 2 < KT:
                                act.dma_start(xr[:, i % 2, :], ins["xT"][:, i + 2, :]).then_inc(xr_in[i % 2], 16)
                            A.activation(ahi[:, i, :], hst[:, i % 2, :], ACT.Copy,
                                         scale=gains[:, NORM_FFN, i:i + 1]).then_inc(c_hi, 1)
                        elif kind == "gate":
                            act.wait_ge(ff_g, 2 * i + 1)
                            A.activation(convout[:, i, 0:2], gbuf[:, TP:TP + 2], ACT.Copy)
                            A.activation(convout[:, i, 2:].rearrange("p (b s) -> p b s", s=2),
                                         gbuf[:, 2 + TP:].rearrange("p (b s) -> p b s", s=2 + LS)[:, :, LS:],
                                         ACT.Copy).then_inc(ff_g, 1)
                            act.wait_ge(ff_cv, i + 1)
                            A.activation(sg[:, 2:], cv[:, 2:], ACT.Sigmoid).then_inc(ff_sg, 1)
                        elif kind == "val":
                            act.wait_ge(ff_pre, i + 1)
                            if i == 0:
                                act.wait_ge(hs_out[0], 16 * KT // 2)
                                act.wait_ge(hs_out[1], 16 * KT // 2)
                            A.activation(achi[:, i, :], af[:, :], ACT.Copy).then_inc(ff_hi, 1)
                            if i == FT - 1:
                                act.wait_ge(tile_ready, tt + 1)
                                act.dma_start(h2[:, :, :], hs.rearrange("k p t -> p k t")).then_inc(h2_in, 16)
                                act.dma_start(praw[:, :, :], ins["pT"]).then_inc(p_in, 16)
                                act.wait_ge(ff_g, 2 * FT)
                                act.dma_start(outs["conv"], convout[:, :, :]).then_inc(out_done, 16)
                        elif kind == "down" and i == 0:
                            act.wait_ge(p_in, 16)
                            A.activation(phi[:, :, :], praw[:, :, :], ACT.Copy).then_inc(p_hi, PK)
                        elif kind == "pproj":
                            if i == 0:
                                act.wait_ge(h2_new, KT)
                            A.activation(ehi[:, i, :], h2[:, i, :], ACT.Copy,
                                         scale=gains[:, NORM_PLE, i:i + 1]).then_inc(e_hi, 1)
                        elif kind == "pgate":
                            act.wait_ge(pg_pre, i + 1)
                            A.activation(sgp[:, i % 2, :], sgp[:, i % 2, :], ACT.Sigmoid).then_inc(pg_sig, 1)
                elif s[0] == "rms":
                    n = s[1]
                    act.wait_ge(ms_ready, n + 1)
                    if n == 0:
                        root(sq[:, 0, :], rs[:, :], rs_guess)
                    else:
                        root(sq2[:, :], rsv[:, :], rs_guess)
                    if n == 3:
                        for k in range(KT):
                            act.wait_ge(y_ready, k + 1)
                            act.dma_start(outs["yT"][:, k, :], yt[:, k % 2, :]).then_inc(y_out[k % 2], 16)
                elif s[0] == "rows":
                    act.wait_ge(row_abs, 1)
                    x = rowt[ROW_T][:, :]
                    link(A.activation(x, x, ACT.Exp, scale=-1.0))
                    A.activation(x, x, ACT.Ln, bias=1.0).then_inc(row_ln, 1)
                    act.wait_ge(row_pre, 1)
                    A.activation(ri[:, :], ri[:, :], ACT.Exp)
                    A.activation(rr[32:32 + H, :], x, ACT.Exp)
                    A.activation(rr[64:64 + H, :], rowt[ROW_M][:, :], ACT.Exp, scale=-1.0)
                    A.activation(rowc[:, 4, :], rowc[:, 4, :], ACT.Exp).then_inc(row_exp, 4)
                    act.dma_start(outs["m"], mout[:, :]).then_inc(out_done, 16)
                    act.wait_ge(rs_ready, 1)
                    state_load(0)
                    state_load(1)
                elif s[0] == "mchunk":
                    c = s[1]
                    t0, ln = chunk_span(c)
                    act.wait_ge(p_pre, c + 1)
                    A.activation(pw[0:ln, :, 0:ln], pw[0:ln, :, 0:ln], ACT.Exp).then_inc(p_exp, 1)
                    if c < NC:
                        for h in range(H):
                            copy_out(j + 4 + H + h, vm[:, c, h, :], P, DV + 1)
                        if c == NC - 1:
                            act.wait_ge(c_ready, NC * H + 1)
                            act.dma_start(outs["C_p"], cst[:, 0, :, 0:DV]).then_inc(cp_out, 16)
                elif s[0] == "head":
                    which, h = s[1], s[2]
                    q = head_no[s]
                    wd = DV + 1 if which == "m" else DV
                    act.wait_ge(aux_ready, j + 1)
                    i = A.activation(so[:, 0, 0:wd], aux[0:TS, j % 4, 0:wd], ACT.Copy)
                    i.then_inc(aux_free[j % 4], 1)
                    act.wait_ge(aux_free[j % 4], j // 4 + 1)
                    act.wait_ge(aux_ready, j + 1 + NB)
                    link(A.activation((vm if which == "m" else vg)[0:TS, NC, h, 0:wd], so[:, 0, 0:wd], ACT.Copy))
                    act.sem_inc(h_out, 1)
                    act.wait_ge(st_new, q + 1)
                    dst = outs["C_s"] if which == "m" else outs["S_s"]
                    act.dma_start(dst[h, :, :, :], st[q % 2][:, :, 0:DV]).then_inc(st_out[q % 2], 16)
                    if q == 3:
                        act.dma_start(outs["n"], nout[:, :, :]).then_inc(out_done, 16)
                    if q >= 1 and q + 1 < 2 * H:
                        state_load(q + 1)
                elif s[0] == "la":
                    for h in range(H):
                        act.wait_ge(la_abs, h + 1)
                        x = stg[:, h % 2, :]
                        link(A.activation(x, x, ACT.Exp, scale=-1.0))
                        A.activation(x, x, ACT.Ln, bias=1.0).then_inc(la_ln, 1)
                elif s[0] == "gchunk":
                    c = s[1]
                    t0, ln = chunk_span(c)
                    levels = PROMPT_LEVELS if c < NC else SAMPLE_LEVELS
                    act.wait_ge(g_go, c + 1)
                    act.wait_ge(kd_sub, c + 1)
                    A.activation(kf[:, :, 0:ln], kf[:, :, 0:ln], ACT.Exp, scale=1 / TAU).then_inc(kd_exp, 1)
                    A.activation(pw[:, :, 0:ln], cum[:, :, t0:t0 + ln], ACT.Exp, scale=1 / TAU).then_inc(eb_ready, 1)
                    for n, w in enumerate(levels):
                        ng["lv"] += 1
                        act.wait_ge(xl_sub, ng["lv"])
                        xl = xl01[:, n % 3, :, 0:ln] if n % 3 < 2 else xl2[:, 0, :, 0:ln]
                        x = xl.rearrange("p h (b s) -> p h b s", s=2 * w)
                        A.activation(x[:, :, :, 0:w], x[:, :, :, 0:w], ACT.Exp, scale=-1 / TAU)
                        A.activation(x[:, :, :, w:], x[:, :, :, w:], ACT.Exp, scale=1 / TAU).then_inc(xl_exp, 1)
                    if c < NC:
                        j += 2 + len(levels)
                        for h in range(H):
                            copy_out(j + H + h, vg[:, c, h, :], P, DV)
                        if c == NC - 1:
                            act.wait_ge(s_ready, NC * H)
                            act.dma_start(outs["S_p"], gst[:, 0, :, :]).then_inc(cp_out, 16)
                elif s[0] == "tnorm":
                    ng["tn"] += 1
                    act.wait_ge(tn_pre, ng["tn"])
                    ln = chunk_span(s[2])[1]
                    root(nsm[0:ln, 2, :], nsm[0:ln, 3, :], tn_exp)
                elif s[0] == "bt":
                    m = s[2] + (KT if s[1] == "g" else 0)
                    if m == 0:
                        act.wait_ge(tn_done, 2 * (NC + 1))
                        gate_load()
                        gate_load()
                    gate_sigmoid()
                    act.wait_ge(bt_pre, m + 1)
                    A.activation((hmhi if s[1] == "m" else ahi)[:, s[2], :], bt_t[:, 0, :], ACT.Copy)\
                        .then_inc(bt_hi, 1)
                    gate_load()
            act.wait_ge(out_done, 48)
            for k in range(2):
                act.wait_ge(y_out[k], 16 * KT // 2)
                act.wait_ge(st_out[k], out_count(6 + k))
            act.wait_ge(cp_out, 32)


def pack(w, width):
    k, n = w.shape
    v = w.reshape(k // P, P, n // width, width).transpose(2, 1, 0, 3)
    return np.ascontiguousarray(v).reshape(n // width, P, k // P * width)


def vec(g):
    return np.ascontiguousarray(g.reshape(-1, P).T)


def constants():
    i = np.arange(P)
    s, t = i[:, None], i[None, :]
    cmask = np.zeros((P, 8, P), np.float32)
    for n, w in enumerate(PROMPT_LEVELS):
        cmask[:, n, :] = (s // (2 * w) == t // (2 * w)) & (s // w % 2 == 0) & (t // w % 2 == 1)
    cmask[:, 7, :] = s == t
    nmask = np.full((P, 2, P), -1e30, np.float32)
    nmask[:, 0, :][s <= t] = 0.0
    nmask[:, 1, :][(s <= t) & (s // LS == t // LS)] = 0.0
    sel = np.zeros((H, H, P), np.float32)
    for h in range(H):
        sel[h, h, :] = 1.0
    bmask = (np.arange(TS)[:, None] // LS == np.arange(NB)[None, :]).astype(np.float32)
    return {"ident": np.eye(P, dtype=np.float32), "cmask": cmask, "nmask": nmask, "sel": sel, "bmask": bmask}


def kernel(x_prompt, x_sample, state_mlstm_C, state_mlstm_n, state_mlstm_m, state_gla_S,
           state_ffn_conv, p_prompt, p_sample, norm_mix_g, w_in, b_mi, b_mf, g_mnorm, w_lr2,
           b_lr2, g_gnorm, w_pa, w_pb, w_o, norm_ffn_g, w_up, conv_w, conv_b, w_down,
           norm_ple_g, w_ple_gate, w_ple_proj, final_norm_g):
    import concourse.bacc as bacc
    from concourse.bass_utils import run_bass_kernel_spmd as run

    a = np.asarray

    def tokens(p, s):
        x = np.concatenate([a(p).reshape(TP, -1), a(s).reshape(TS, -1)], axis=0)
        return np.ascontiguousarray(x.T.reshape(-1, P, T).transpose(1, 0, 2))

    w = a(w_in)[0]
    sizes = [512, 512, 1024, 4, 4, 1024, 512, 512, 1024, RANK, 1024, 1024, 1024]
    o = np.concatenate([[0], np.cumsum(sizes)])
    col = {n: w[:, o[k]:o[k + 1]] for k, n in enumerate(
        ("mq", "mk", "mv", "mi", "mf", "mo", "gq", "gk", "gv", "glr", "gg", "ga", "gb"))}
    main = np.concatenate([col[n] for n in ("mq", "mk", "mv", "gq", "gk", "gv", "mo", "gg", "ga", "gb")], axis=1)
    misc = np.concatenate([col["mi"], col["mf"], col["glr"]], axis=1)
    up = a(w_up)[0].reshape(D, 2, FT, P).transpose(0, 2, 1, 3).reshape(D, 2 * FF)
    arrays = dict(
        xT=tokens(x_prompt, x_sample), pT=tokens(p_prompt, p_sample),
        C_in=np.ascontiguousarray(a(state_mlstm_C)[0].transpose(1, 2, 0, 3)),
        S_in=np.ascontiguousarray(a(state_gla_S)[0].transpose(1, 2, 0, 3)),
        nst=np.ascontiguousarray(a(state_mlstm_n)[0].transpose(2, 1, 0)),
        m0=np.ascontiguousarray(a(state_mlstm_m)[0].T),
        convst=np.ascontiguousarray(a(state_ffn_conv)[0].reshape(NB, 2, FT, P).transpose(3, 2, 0, 1)),
        gains=np.ascontiguousarray(np.stack([vec(a(g).reshape(-1)) for g in (
            norm_mix_g, g_mnorm, g_gnorm, norm_ffn_g, norm_ple_g, final_norm_g)], axis=1)),
        convw=np.ascontiguousarray(a(conv_w)[0].reshape(3, FT, P).transpose(2, 0, 1)),
        convb=vec(a(conv_b)[0]), blr=vec(a(b_lr2)[0]),
        bgate=np.ascontiguousarray(np.stack([a(b_mi)[0], a(b_mf)[0]], axis=1)),
        wlr=np.ascontiguousarray(a(w_lr2)[0]),
        w_misc=np.ascontiguousarray(misc.reshape(KT, P, -1).transpose(1, 0, 2)),
        w_in=pack(main, 2 * P), w_pa=pack(a(w_pa)[0], 2 * P), w_pb=pack(a(w_pb)[0], 2 * P),
        w_o=pack(a(w_o)[0], 2 * P), w_up=pack(up, 2 * P), w_down=pack(a(w_down)[0], P),
        w_pproj=pack(a(w_ple_proj)[0], D), w_pgate=pack(a(w_ple_gate)[0], 2 * P),
    )
    arrays.update(constants())

    nc = bacc.Bacc("TRN2", target_bir_lowering=False, num_devices=1)
    ins = {n: nc.dram_tensor(f"in_{n}", x.shape, mybir.dt.from_np(x.dtype), kind="ExternalInput").ap()
           for n, x in arrays.items()}
    shapes = dict(yT=(P, KT, T), C_p=(P, H, DV), S_p=(P, H, DV), n=(P, H, NB + 1), m=(H, NB + 1),
                  conv=(P, FT, 2 + 2 * NB), C_s=(H, P, NB, DV), S_s=(H, P, NB, DV))
    outs = {n: nc.dram_tensor(f"out_{n}", s, F32, kind="ExternalOutput").ap() for n, s in shapes.items()}
    build(nc, ins, outs)
    r = run(nc, [{f"in_{n}": x for n, x in arrays.items()}], core_ids=[0]).results[0]
    g = {n: a(r[f"out_{n}"]) for n in shapes}

    y = g["yT"].transpose(2, 1, 0).reshape(T, D)
    n, m, conv = g["n"], g["m"], g["conv"]
    cv = conv.transpose(2, 1, 0).reshape(2 + 2 * NB, FF)
    c = np.ascontiguousarray
    return (c(y[:TP]).reshape(1, TP, D), c(y[TP:]).reshape(NB, LS, D),
            c(g["C_p"].transpose(1, 0, 2))[None, None], c(n[:, :, NB].T)[None, None], c(m[:, NB])[None, None],
            c(g["S_p"].transpose(1, 0, 2))[None, None], c(cv[:2])[None, None],
            c(g["C_s"].transpose(2, 0, 1, 3))[None], c(n[:, :, :NB].transpose(2, 1, 0))[None],
            c(m[:, :NB].T)[None], c(g["S_s"].transpose(2, 0, 1, 3))[None],
            c(cv[2:].reshape(NB, 2, FF))[None])
```

```python
from contextlib import ExitStack

import numpy as np
import concourse.bass as bass
from concourse import mybir

F32 = mybir.dt.float32
F32R = mybir.dt.float32r
I8 = mybir.dt.int8
ALU = mybir.AluOpType
ACT = mybir.ActivationFunctionType

P = 128
D = 1024
KT = D // P
TP, NB, LS = 512, 8, 8
TS = NB * LS
T = TP + TS
HALF = T // 2
H = 4
DK, DV = 128, 256
L = 128
NC = TP // L
FF = 2688
FT = FF // P
PLE = 256
PK = PLE // P
RANK = 16
TAU = 16.0
EPS = 1e-6
NY_POOL = 3
NGT = 4
V_BY_VECTOR = (1, 3)
UW = 2048
NORM_MIX, NORM_M, NORM_G, NORM_FFN, NORM_PLE, NORM_OUT = range(6)
PROMPT_LEVELS = [64, 32, 16, 8, 4, 2, 1]
SAMPLE_LEVELS = [4, 2, 1]
ZMO, ZGG, ZGA, ZGB = 0, 8, 16, 24


def chunk_span(c):
    return (c * L, L) if c < NC else (TP, TS)


def plan():
    units = [("misc", 0)]
    units += [("mq", i) for i in range(2)] + [("mk", i) for i in range(2)] + [("mv", i) for i in range(4)]
    units += [("gq", i) for i in range(2)] + [("gk", i) for i in range(2)] + [("gv", i) for i in range(4)]
    units += [(n, i) for n in ("mo", "gg", "ga", "gb") for i in range(4)]
    units += [(n, i) for n in ("pa", "pb", "wo") for i in range(4)]
    units += [("up", i) for i in range(FT)] + [("down", i) for i in range(2 * KT)]
    units += [("pproj", 0)] + [("pgate", i) for i in range(4)]
    at = {x: n for n, x in enumerate(units)}
    sched = [("norm_in",)]

    def unit(kind, i, after=None, before=()):
        u = at[(kind, i)]
        sched.append(("unit", u))
        sched.extend(before)
        for n in range(len(tiles_of(kind, i))):
            sched.append(("tile", u, n))
            sched.extend((after or {}).get(n, ()))

    def units_of(kind, n, after):
        for i in range(n):
            unit(kind, i, {0: after.get(2 * i, ()), 1: after.get(2 * i + 1, ())})

    unit("misc", 0, before=(("rsum", 0), ("rspread", 0)))
    units_of("mq", 2, {0: [("rows", 0)], 1: [("rows", 1)]})
    units_of("mk", 2, {0: [("rows", 2)], 2: [("rows", 3)]})
    for i in range(4):
        unit("mv", i, {2: [("m1", 0)]} if i == 3 else None)
    units_of("gq", 2, {n: [("m2", n), ("m1", n + 1)] for n in range(NC)})
    units_of("gk", 2, {0: [("hpre", "m", 0), ("tnorm", "m", 0)], 1: [("head", "m", 0)],
                       2: [("hpre", "m", 1), ("tnorm", "m", 1)], 3: [("head", "m", 1)]})
    unit("gv", 0, {1: [("hpre", "m", 2)], 3: [("head", "m", 2)], 4: [("la", 0)]})
    unit("gv", 1, {1: [("hpre", "m", 3)], 3: [("head", "m", 3)], 4: [("la", 1)]})
    unit("gv", 2, {1: [("la", 2)], 3: [("tnorm", "m", 2)]})
    unit("gv", 3, {0: [("la", 3)], 4: [("gpre", 0), ("lpre", 0, 0)]})
    for c in range(NC):
        units_of_gate = {
            0: [("gkt", c), ("lev", c, 0), ("lpre", c, 1)],
            1: [("lev", c, 1), ("lpre", c, 2), ("tnorm", *(("g", c - 1) if c else ("m", 3)))],
            2: [("lev", c, 2), ("lpre", c, 3)],
            3: [("lev", c, 3), ("gout", c), ("gpre", c + 1), ("lpre", c + 1, 0)],
        }
        kind, i = ("mo", 2 * c) if c < 2 else ("gg", 2 * c - 4)
        unit(kind, i, {n: units_of_gate[n] for n in range(2)})
        unit(kind, i + 1, {n: units_of_gate[2 + n] for n in range(2)})
    units_of("ga", 4, {0: [("gkt", NC), ("lev", NC, 0), ("lpre", NC, 1), ("hpre", "g", 0)],
                       1: [("lev", NC, 1), ("tnorm", "g", NC - 1)],
                       2: [("head", "g", 0)], 3: [("hpre", "g", 1)], 4: [("head", "g", 1)],
                       5: [("hpre", "g", 2), ("tnorm", "m", NC)], 6: [("head", "g", 2)], 7: [("hpre", "g", 3)]})
    units_of("gb", 4, {0: [("head", "g", 3), ("tnorm", "g", NC)], 2: [("bt", "m", 0), ("bt", "m", 1)],
                       3: [("bt", "m", 2), ("bt", "m", 3)], 4: [("bt", "m", 4), ("bt", "m", 5)],
                       5: [("bt", "m", 6)], 6: [("bt", "m", 7)]})
    units_of("pa", 4, {0: [("bt", "g", 0), ("bt", "g", 1)], **{n: [("bt", "g", n + 1)] for n in range(1, 7)}})
    units_of("pb", 4, {})
    units_of("wo", 4, {})
    for i in range(FT):
        unit("up", i, before=(("rsum", 1), ("rspread", 1)) if i == 0 else ())
    for i in range(2 * KT):
        unit("down", i)
    unit("pproj", 0)
    for i in range(4):
        unit("pgate", i, before=(("rsum", 2), ("rspread", 2)) if i == 0 else ())
    sched += [("rsum", 3), ("rspread", 3)]
    return units, sched


MID = {("misc", 0, 0): {KT: ("rsum", 0)}, ("mq", 0, 0): {5: ("rspread", 0)},
       ("up", 0, 0): {KT - 1: ("rsum", 1)}, ("up", 0, 1): {4: ("rspread", 1)},
       ("pgate", 0, 0): {2: ("rsum", 2), KT - 1: ("rspread", 2)}}


def levels_of(c, g):
    return (PROMPT_LEVELS if c < NC else SAMPLE_LEVELS)[2 * g:2 * g + 2]


def tiles_of(kind, i):
    if kind == "misc":
        return [("misc", 0)]
    if kind in ("mv", "gv"):
        return [(kind, (i, c)) for c in range(NC + 1)]
    if kind == "up":
        return [("gate", i), ("val", i)]
    if kind == "down":
        return [("down", i // 2)] if i % 2 else []
    if kind == "pproj":
        return [("pproj", n) for n in range(KT)]
    return [(kind, 2 * i), (kind, 2 * i + 1)]


def aux_jobs(stage):
    if stage[0] in ("rsum", "gkt"):
        return 1 + (stage[0] == "gkt")
    if stage[0] in ("rspread", "bt", "la"):
        return 2
    if stage[0] == "rows":
        return 3 if stage[1] == 3 else 0
    if stage[0] == "m1":
        return 4
    if stage[0] in ("m2", "gout"):
        return 2 * H
    if stage[0] == "lev":
        return len(levels_of(*stage[1:]))
    if stage[0] == "head":
        return 1 + NB
    return 0


def build(nc, ins, outs):
    units, sched = plan()
    tile_at, job_at, nt, nj = {}, {}, 0, 0
    for s in sched:
        if s[0] == "unit":
            tile_at[s] = nt
            nt += len(tiles_of(*units[s[1]]))
        elif s[0] == "tile":
            tile_at[s] = tile_at[("unit", s[1])] + s[2]
        job_at[s] = nj
        nj += aux_jobs(s)

    zs = nc.dram_tensor("gate_scratch", [32, P, T], F32).ap()
    hs = nc.dram_tensor("residual_scratch", [KT, P, T], F32).ap()

    with ExitStack() as ctx:
        base = 16512
        where = [base]

        def at(name, shape, dt, offset):
            return nc.alloc_sbuf_tensor_at(name, shape, dt, offset=offset)

        def put(name, shape, dt=F32):
            n = int(np.prod(shape[1:])) * (1 if dt == I8 else 4)
            t = at(name, shape, dt, where[0])
            where[0] += (n + 31) // 32 * 32
            return t

        ident = put("ident", [P, P])
        ones = put("ones", [P, P])
        cmask = put("cmask", [P, 8, P], I8)
        nmask = put("nmask", [P, 2, P])
        bmask = put("bmask", [TS, NB])
        gains = put("gains", [P, 6, KT])
        convw = put("convw", [P, 3, FT])
        convb = put("convb", [P, FT])
        blr = put("blr", [P, H])
        bgate = put("bgate", [H, 2])
        m0 = put("m0", [H, NB])
        wlr = put("wlr", [RANK, H * DK])
        nst = put("nst", [P, H, NB])
        nout = put("nout", [P, H, NB + 1])
        mout = put("mout", [H, NB + 1])
        convst = put("convst", [P, FT, NB, 2])
        stat = put("stat", [P, 3, NC + 1])
        wraw = put("wraw", [P, 2, UW])
        whi = put("whi", [P, 2, UW], F32R)
        wlo = put("wlo", [P, 2, UW], F32R)
        X = where[0]
        fm = [P, KT, T]
        ahi = at("ahi", fm, F32R, X)
        alo = at("alo", fm, F32R, X + 18432)
        VM = X + 36864
        vm = at("vm", [P, NC + 1, H, DV + 1], F32, VM)
        xT = at("xT", fm, F32, VM)
        VG = VM + 20576
        vg = at("vg", [P, NC + 1, H, DV], F32, VG)
        cst = at("cst", [P, 2, H, DV + 1], F32, VG)
        cmaskf = at("cmaskf", [P, 8, P], F32, VG)
        r1 = at("r1", [H, T], F32, VG + 8224)
        ri = at("ri", [H, T], F32, VG + 8224 + 2304)
        rr = at("rr", [P, T], F32, VG + 8224 + 4608)
        sel = at("sel", [H, H, P], F32, VG + 8224 + 6912)
        QM = VG + 20480
        mq = at("mq", [P, H, T], F32, QM)
        mk = at("mk", [P, H, T], F32, QM + 9216)
        cum = at("cum", [P, H, T], F32, QM)
        stg = at("stg", [P, 2, T], F32, QM + 9216)
        xl01 = at("xl01", [P, 2, H, L], F32, QM + 9216 + 4608)
        QG = QM + 18432
        gq = at("gq", [P, H, T], F32, QG)
        gk = at("gk", [P, H, T], F32, QG + 9216)
        rowt = [at(f"rowt{i}", [H, T], F32, QG + 2304 * i) for i in range(8)]
        ROW_LI, ROW_XF, ROW_LF, ROW_B, ROW_M, ROW_D0, ROW_D1, ROW_T = range(8)
        ST = QG + 18432
        st = [at(f"st{i}", [P, NB, DV + 1], F32, ST + 8224 * i) for i in range(2)]
        gst = at("gst", [P, 2, H, DV], F32, ST + 8224)
        acc0 = at("acc0", [P, T], F32, ST)
        sq = at("sq", [P, 2, T], F32, ST + 2304)
        G0 = ST + 16448
        pw = at("pw", [P, H, L], F32, G0)
        qt = at("qt", [P, H, L], F32, G0 + 2048)
        att = at("att", [P, H, L], F32, G0 + 4096)
        ktok = at("ktok", [P, H, L], F32, G0 + 6144)
        QB = G0 + 8192
        qb = at("qb", [P, T], F32, QB)
        kb = at("kb", [TS, NB, P], F32, QB + 2304)
        kf = at("kf", [P, H, L], F32, QB + 2304)
        xl3 = at("xl3", [P, 1, H, L], F32, QB + 2304 + 2048)
        so = at("so", [TS, 1, DV + 1], F32, QB + 6400)
        MK = QB + 6400 + 1056
        reset = at("reset", [P, T], F32, MK)
        glr = at("glr", [RANK, T], F32, MK + 2304)
        xl2 = at("xl2", [P, 1, H, L], F32, MK + 2304)
        rs = at("rs", [P, T], F32, MK + 4608)
        SM = MK + 6912
        colT = at("colT", [P, NC + 1, 3, H], F32, SM)
        carry = at("carry", [P, H, NC + NB], F32, SM + 256)
        rscol = at("rscol", [P, NC + 1], F32, SM + 448)
        nstat = at("nstat", [P, H, 6], F32, SM + 480)
        nmv = at("nmv", [P, H, 2], F32, SM + 576)
        nsm = at("nsm", [P, 6, H], F32, SM + 608)
        rowc = at("rowc", [H, 5, NC + NB], F32, SM + 704)
        assert SM + 704 + 240 <= 229368, SM + 944 - 229368
        hmhi = at("hmhi", fm, F32R, QG)
        hmlo = at("hmlo", fm, F32R, QG + 18432)
        gt = at("gt", [P, NGT, T], F32, G0 + 2048)
        sgt = at("sgt", [P, T], F32, MK)
        bt_t = at("bt_t", [P, 1, T], F32, QB + 4608)
        merged = at("merged", fm, F32, VM)
        mghi = at("mghi", fm, F32R, VG)
        mglo = at("mglo", fm, F32R, QM)
        xr = at("xr", [P, 2, T], F32, VM)
        hst = at("hst", [P, 2, T], F32, VM + 4608)
        achi = at("achi", [P, FT, T], F32R, X + 36864)
        aclo = at("aclo", [P, FT, T], F32R, X + 36864 + FT * T * 4)
        FS = X + 36864 + 2 * FT * T * 4
        GW = 2 + TP + NB * (2 + LS)
        gbuf = at("gbuf", [P, GW], F32, FS)
        cv = at("cv", [P, GW], F32, FS + 2400)
        sg = at("sg", [P, GW], F32, FS + 4800)
        vrs = at("vrs", [P, T], F32, FS + 7200)
        af = at("af", [P, T], F32, FS + 9504)
        acc = at("acc", [P, T], F32, FS + 11808)
        sq2 = at("sq2", [P, T], F32, FS + 14112)
        rsv = at("rsv", [P, T], F32, FS + 16416)
        convout = at("convout", [P, FT, 2 + 2 * NB], F32, FS + 18720)
        h2 = at("h2", fm, F32, X)
        h3 = at("h3", fm, F32, X + 18432)
        ehi = at("ehi", fm, F32R, X + 36864)
        elo = at("elo", fm, F32R, X + 36864 + 18432)
        pj = at("pj", fm, F32, X + 36864 * 2)
        praw = at("praw", [P, PK, T], F32, X + 18432)
        phi = at("phi", [P, PK, T], F32R, X + 18432 + 4608)
        plo = at("plo", [P, PK, T], F32R, X + 18432 + 9216)
        sgp = at("sgp", [P, 2, T], F32, X + 36864 * 3)
        yt = at("yt", fm, F32, X + 36864 * 3 + 4608)

        ps = ctx.enter_context(nc.psum_tensor("ps", [P, 2, 2, 512], F32))
        aux = ctx.enter_context(nc.psum_tensor("aux", [P, 4, 512], F32))

        def sem(name):
            return ctx.enter_context(nc.semaphore(name))

        def sems(name, n):
            return [sem(f"{name}{i}") for i in range(n)]

        raw_in = sems("raw_in", 2)
        split_hi = sem("split_hi")
        split_lo = sem("split_lo")
        first_half = sem("first_half")
        half_done = sem("half_done")
        tile_ready = sem("tile_ready")
        tile_free = sems("tile_free", 2)
        aux_ready = sem("aux_ready")
        aux_free = sems("aux_free", 4)
        const_in = sem("const_in")
        ident_in = sem("ident_in")
        gains_in = sem("gains_in")
        x_in = sems("x_in", 4)
        dve_step = sem("dve_step")
        act_step = sem("act_step")
        pool_step = sem("pool_step")
        init_done = sem("init_done")
        in_sq = sem("in_sq")
        in_sq_used = sem("in_sq_used")
        a_hi = sem("a_hi")
        a_lo = sem("a_lo")
        sq_half = sem("sq_half")
        sq_sum = sem("sq_sum")
        ms_ready = sem("ms_ready")
        ms_root = sem("ms_root")
        rs_diag = sem("rs_diag")
        rs_ready = sem("rs_ready")
        row_abs = sem("row_abs")
        row_ln = sem("row_ln")
        row_pre = sem("row_pre")
        row_exp = sem("row_exp")
        rows_zero = sem("rows_zero")
        fm_ready = sem("fm_ready")
        v_ready = sem("v_ready")
        p_pre = sem("p_pre")
        p_exp = sem("p_exp")
        qt_ready = sem("qt_ready")
        kt_ready = sem("kt_ready")
        at_ready = sem("at_ready")
        c_ready = sem("c_ready")
        s_ready = sem("s_ready")
        blk_ready = sem("blk_ready")
        st_in = sems("st_in", 2)
        st_n = sem("st_n")
        st_new = sem("st_new")
        st_out = sems("st_out", 2)
        cp_out = sem("cp_out")
        out_done = sem("out_done")
        h_out = sem("h_out")
        la_abs = sem("la_abs")
        la_ln = sem("la_ln")
        cum_ready = sem("cum_ready")
        g_go = sem("g_go")
        eb_ready = sem("eb_ready")
        kd_sub = sem("kd_sub")
        kd_exp = sem("kd_exp")
        kf_ready = sem("kf_ready")
        xl_sub = sem("xl_sub")
        xl_exp = sem("xl_exp")
        xl_ready = sem("xl_ready")
        stg_full = sem("stg_full")
        stg_out = sems("stg_out", 2)
        tn_pre = sem("tn_pre")
        tn_root = sem("tn_root")
        tn_done = sem("tn_done")
        gt_in = sems("gt_in", NGT)
        gt_sig = sem("gt_sig")
        gt_used = sem("gt_used")
        silu_used = sem("silu_used")
        bt_pre = sem("bt_pre")
        bt_hi = sem("bt_hi")
        bt_lo = sem("bt_lo")
        mg_pre = sem("mg_pre")
        mg_hi = sem("mg_hi")
        mg_lo = sem("mg_lo")
        xr_in = sems("xr_in", 2)
        h_pre = sem("h_pre")
        c_hi = sem("c_hi")
        c_lo = sem("c_lo")
        hs_out = sems("hs_out", 2)
        ff_g = sem("ff_g")
        ff_cv = sem("ff_cv")
        ff_sg = sem("ff_sg")
        ff_pre = sem("ff_pre")
        ff_hi = sem("ff_hi")
        ff_lo = sem("ff_lo")
        h2_in = sem("h2_in")
        h2_new = sem("h2_new")
        p_in = sem("p_in")
        p_hi = sem("p_hi")
        p_lo = sem("p_lo")
        pj_ready = sem("pj_ready")
        e_hi = sem("e_hi")
        e_lo = sem("e_lo")
        pg_pre = sem("pg_pre")
        pg_sig = sem("pg_sig")
        h3_new = sem("h3_new")
        y_pre = sem("y_pre")
        yp_ready = sem("yp_ready")
        y_ready = sem("y_ready")
        y_out = sem("y_out")

        block = ctx.enter_context(nc.Block())

        def two(ap):
            return ap.rearrange("p (a b) -> p a b", a=2)

        def tile(t):
            return ps[:, t % 2, :, 0:HALF]

        def bcast(ap, n, where_):
            shape = list(ap.shape)
            return ap.unsqueeze(where_).broadcast_to(shape[:where_] + [n] + shape[where_:])

        def f32(ap):
            return ap.bitcast(F32)

        def head_jobs():
            return [s for s in sched if s[0] == "head"]

        head_no = {s: n for n, s in enumerate(head_jobs())}

        def out_count(q):
            return 16 * (q // 2 + 1)

        h_out_of, copied, = {}, 0
        for s in sched:
            if s[0] in ("m2", "gout"):
                copied += H
                h_out_of[(s[0][0], s[1])] = copied
            elif s[0] == "head":
                copied += 1
                h_out_of[(s[1], NC)] = copied

        def xl_buffer(c, g, n):
            return (xl01[:, 0], xl01[:, 1], xl2[:, 0], xl3[:, 0])[2 * (g % 2) + n]

        @block.sync
        def _(sp):
            sp.dma_start(gains[:, :, :], ins["gains"]).then_inc(gains_in, 16)
            for u, (kind, i) in enumerate(units):
                s = u % 2
                if u >= 2:
                    sp.wait_ge(split_hi, u - 1)
                    sp.wait_ge(split_lo, u - 1)
                if kind == "misc":
                    sp.dma_start(wraw[:, 0, 0:KT * P], ins["w_misc"]).then_inc(raw_in[0], 16)
                else:
                    src = {"pa": "w_pa", "pb": "w_pb", "wo": "w_o", "up": "w_up", "pproj": "w_pproj",
                           "pgate": "w_pgate", "down": "w_down"}.get(kind, "w_in")
                    if src == "w_in":
                        row = {"mq": 0, "mk": 2, "mv": 4, "gq": 8, "gk": 10, "gv": 12,
                               "mo": 16, "gg": 20, "ga": 24, "gb": 28}[kind] + i
                        sp.dma_start(wraw[:, s, :], ins["w_in"][row, :, :]).then_inc(raw_in[s], 16)
                        if u == 1:
                            sp.dma_start(ident[:, :], ins["ident"]).then_inc(ident_in, 16)
                            for n, dst in (("cmask", cmaskf[:, :, :]), ("nmask", nmask[:, :, :]),
                                           ("sel", sel[:, :, :]), ("bmask", bmask[:, :]), ("convw", convw[:, :, :]),
                                           ("convb", convb[:, :]), ("blr", blr[:, :]), ("bgate", bgate[:, :]),
                                           ("m0", m0[:, :]), ("wlr", wlr[:, :]), ("nst", nst[:, :, :]),
                                           ("convst", convst[:, :, :, :])):
                                sp.dma_start(dst, ins[n]).then_inc(const_in, 16)
                    elif kind == "down":
                        a, b = (0, 11 * P) if i % 2 == 0 else (11 * P, FF)
                        sp.dma_start(wraw[:, s, 0:b - a], ins["w_down"][i // 2, :, a:b]).then_inc(raw_in[s], 16)
                    else:
                        sp.dma_start(wraw[:, s, :], ins[src][i, :, :]).then_inc(raw_in[s], 16)

            for n in range(NY_POOL):
                sp.wait_ge(yp_ready, n + 1)
                sp.dma_start(outs["yT"][:, n, :], yt[:, n, :]).then_inc(y_out, 16)

        NCONST = 12 * 16

        def raw_count(u):
            return 16 * (u // 2 + 1)

        def width(u):
            kind, i = units[u]
            if kind == "misc":
                return KT * P
            if kind == "down":
                return 11 * P if i % 2 == 0 else 10 * P
            return UW

        def used(eng, u):
            kind, i = units[u]
            if kind == "down" and i % 2 == 0:
                eng.wait_ge(half_done, i // 2 + 1)
            else:
                eng.wait_ge(tile_ready, tile_at[("unit", u)] + len(tiles_of(kind, i)))

        @block.gpsimd
        def _(pool):
            for u in range(len(units)):
                s, n = u % 2, width(u)
                pool.wait_ge(raw_in[s], raw_count(u))
                pool.wait_ge(split_hi, u + 1)
                if u >= 2:
                    used(pool, u - 2)
                nc.gpsimd.tensor_tensor(wlo[:, s, 0:n], wraw[:, s, 0:n], f32(whi[:, s, 0:n]), ALU.subtract)\
                    .then_inc(split_lo, 1)
            pool.wait_ge(rs_ready, 4)
            for n in range(NY_POOL):
                pool.wait_ge(y_pre, n + 1)
                nc.gpsimd.tensor_tensor(yt[:, n, :], yt[:, n, :], rsv[:, :], ALU.mult).then_inc(yp_ready, 1)

        @block.tensor
        def _(pe):
            def bank(j):
                if j >= 4:
                    pe.wait_ge(aux_free[j % 4], j // 4)
                return aux[:, j % 4, :]

            def slot(t):
                if t >= 2:
                    pe.wait_ge(tile_free[t % 2], t // 2)

            def rsum(n):
                pe.wait_ge(sq_sum, n + 1)
                src, b = acc if n else acc0, bank(job_at[("rsum", n)])
                for c in range(NC + 1):
                    t0, ln = chunk_span(c)
                    mm = nc.tensor.matmul(b[0:ln, c:c + 1], src[:, t0:t0 + ln], ones[:, 0:1], start=True, stop=True)
                mm.then_inc(aux_ready, 1)

            def rspread(n):
                pe.wait_ge(rs_diag, n + 1)
                j, d = job_at[("rspread", n)], vrs if n else sq[:, 1]
                nc.tensor.matmul(bank(j), ones[:, :], d[:, 0:TP], start=True, stop=True).then_inc(aux_ready, 1)
                nc.tensor.matmul(bank(j + 1)[:, 0:TS], ones[0:TS, :], d[0:TS, TP:], start=True, stop=True)\
                    .then_inc(aux_ready, 1)

            def mid_stage(s):
                (rsum if s[0] == "rsum" else rspread)(s[1])

            def product(t, blocks, hi, lo, s, start=True, stop=True, ready=None, mid={}, low_part=None):
                for n, (col, k) in enumerate(blocks):
                    if n in mid:
                        mid_stage(mid[n])
                    if ready:
                        for q in ready:
                            pe.wait_ge(q, k + 1)
                    first, last = start and n == 0, stop and n == len(blocks) - 1
                    wh, wl = whi[:, s, col:col + P], wlo[:, s, col:col + P]
                    for x, w, f, e in ((hi, wh, first, False), (lo, wh, False, False), (hi, wl, False, last)):
                        if w is wl and low_part:
                            continue
                        for a in range(2):
                            mm = nc.tensor.matmul(ps[:, t % 2, a, 0:HALF], w, x[:, k, a * HALF:(a + 1) * HALF],
                                                  start=f, stop=e)
                if low_part:
                    pe.wait_ge(split_lo, low_part)
                    for n, (col, k) in enumerate(blocks):
                        for a in range(2):
                            mm = nc.tensor.matmul(ps[:, t % 2, a, 0:HALF], wlo[:, s, col:col + P],
                                                  hi[:, k, a * HALF:(a + 1) * HALF],
                                                  start=False, stop=n == len(blocks) - 1)
                if stop:
                    mm.then_inc(tile_ready, 1)
                if len(blocks) in mid:
                    mid_stage(mid[len(blocks)])
                return mm

            def last_product(t, s):
                for a in range(2):
                    for k in range(KT):
                        col = k * 2 * P + P
                        wh, wl = whi[:, s, col:col + P], wlo[:, s, col:col + P]
                        for x, w, f, e in ((ehi, wh, k == 0, False), (elo, wh, False, False), (ehi, wl, False, k == KT - 1)):
                            mm = nc.tensor.matmul(ps[:, t % 2, a, 0:HALF], w, x[:, k, a * HALF:(a + 1) * HALF],
                                                  start=f, stop=e)
                    mm.then_inc(tile_ready if a else first_half, 1)

            counts = {"lv": 0}
            for s in sched:
                j, t = job_at[s], tile_at.get(s)
                if s[0] == "unit":
                    u = s[1]
                    kind, i = units[u]
                    pe.wait_ge(split_hi, u + 1)
                    if kind in ("misc", "down"):
                        pe.wait_ge(split_lo, u + 1)
                    if kind == "down" and i % 2 == 0:
                        slot(t)
                        product(t, [(b * P, b) for b in range(11)], achi, aclo, u % 2, stop=False,
                                ready=(ff_hi, ff_lo) if i == 0 else None).then_inc(half_done, 1)
                elif s[0] == "tile":
                    u, n = s[1:]
                    kind, i = units[u]
                    w = u % 2
                    mid = MID.get((kind, i, n), {})
                    if kind != "down":
                        slot(t)
                    if kind == "misc":
                        product(t, [(k * P, k) for k in range(KT)], ahi, alo, w, ready=(a_hi, a_lo), mid=mid)
                    elif kind in ("mv", "gv"):
                        t0, ln = chunk_span(n)
                        out = ps[0:ln, t % 2, 0, 0:DV]
                        for k in range(KT):
                            wh = whi[:, w, k * DV:(k + 1) * DV]
                            nc.tensor.matmul(out, ahi[:, k, t0:t0 + ln], wh, start=k == 0, stop=False)
                            nc.tensor.matmul(out, alo[:, k, t0:t0 + ln], wh, start=False, stop=False)
                        if n == 0:
                            pe.wait_ge(split_lo, u + 1)
                        for k in range(KT):
                            mm = nc.tensor.matmul(out, ahi[:, k, t0:t0 + ln], wlo[:, w, k * DV:(k + 1) * DV],
                                                  start=False, stop=k == KT - 1)
                        mm.then_inc(tile_ready, 1)
                    elif kind == "down":
                        product(t, [(b * P, 11 + b) for b in range(10)], achi, aclo, w, start=False,
                                ready=(ff_hi, ff_lo) if i == 1 else None)
                    elif kind == "pproj":
                        pe.wait_ge(p_hi, PK)
                        pe.wait_ge(p_lo, PK)
                        product(t, [(k * D + n * P, k) for k in range(PK)], phi, plo, w,
                                low_part=u + 1 if n == 0 else None)
                    elif (kind, i, n) == ("pgate", 3, 1):
                        last_product(t, w)
                    else:
                        hi, lo, ready = {
                            "pa": (hmhi, hmlo, (bt_hi, bt_lo)), "pb": (ahi, alo, None), "wo": (mghi, mglo, (mg_hi, mg_lo)),
                            "up": (ahi, alo, (c_hi, c_lo)), "pgate": (ehi, elo, (e_hi, e_lo)),
                        }.get(kind, (ahi, alo, None))
                        if i > 0 or n > 0:
                            ready = None
                        if ready:
                            pe.wait_ge(split_lo, u + 1)
                        if kind == "pb" and i == 0 and n == 0:
                            pe.wait_ge(bt_hi, 2 * KT)
                            pe.wait_ge(bt_lo, 2 * KT)
                        product(t, [(k * 2 * P + n * P, k) for k in range(KT)], hi, lo, w, ready=ready, mid=mid,
                                low_part=u + 1 if n == 0 and not ready else None)
                elif s[0] == "bt":
                    which, n = s[1], s[2]
                    v = vm if which == "m" else vg
                    pe.wait_ge(tn_done, 2 * (NC + 1))
                    hd, c0 = n // 2, (n % 2) * P
                    b = bank(j)
                    for c in range(NC):
                        mm = nc.tensor.transpose(b[:, c * L:(c + 1) * L], v[:, c, hd, c0:c0 + P], ident[:, :])
                    mm.then_inc(aux_ready, 1)
                    nc.tensor.transpose(bank(j + 1)[:, 0:TS], v[0:TS, NC, hd, c0:c0 + P], ident[0:TS, 0:TS])\
                        .then_inc(aux_ready, 1)
                elif s == ("rsum", 3):
                    rsum(3)
                elif s == ("rspread", 3):
                    rspread(3)
                elif s[0] == "rows" and s[1] == 3:
                    pe.wait_ge(row_exp, 4)
                    pe.wait_ge(const_in, NCONST)
                    b = bank(j)
                    for c in range(NC):
                        mm = nc.tensor.transpose(b[:, c * P:(c + 1) * P], rr[:, c * L:(c + 1) * L], ident[:, :])
                    mm.then_inc(aux_ready, 1)
                    b = bank(j + 1)
                    nc.tensor.transpose(b[0:TS, 0:P], rr[:, TP:T], ident[:, :]).then_inc(aux_ready, 1)
                    b = bank(j + 2)
                    n = NC + NB
                    for h in range(H):
                        mm = nc.tensor.matmul(b[:, h * n:(h + 1) * n], sel[:, h, :], rowc[:, 4, :],
                                              start=True, stop=True)
                    mm.then_inc(aux_ready, 1)
                elif s[0] == "m1":
                    c = s[1]
                    t0, ln = chunk_span(c)
                    b = bank(j)
                    for h in range(H):
                        mm = nc.tensor.matmul(b[:, h * ln:(h + 1) * ln], sel[:, h, :], r1[:, t0:t0 + ln],
                                              start=True, stop=True)
                    mm.then_inc(aux_ready, 1)
                    b = bank(j + 1)
                    for h in range(H):
                        mm = nc.tensor.matmul(b[:, h * ln:(h + 1) * ln], sel[:, h, :], ri[:, t0:t0 + ln],
                                              start=True, stop=True)
                    mm.then_inc(aux_ready, 1)
                    if c == 0:
                        pe.wait_ge(fm_ready, 2 * H)
                    b = bank(j + 2)
                    for h in range(H):
                        mm = nc.tensor.transpose(b[0:ln, h * P:(h + 1) * P], mk[:, h, t0:t0 + ln], ident[:, :])
                    mm.then_inc(aux_ready, 1)
                    b = bank(j + 3)
                    for h in range(H):
                        mm = nc.tensor.matmul(b[0:ln, h * ln:(h + 1) * ln], mk[:, h, t0:t0 + ln],
                                              mq[:, h, t0:t0 + ln], start=True, stop=True)
                    mm.then_inc(aux_ready, 1)
                elif s[0] == "m2":
                    c = s[1]
                    if c == 0:
                        pe.wait_ge(v_ready, H * (NC + 1))
                    pe.wait_ge(kt_ready, c + 1)
                    for h in range(H):
                        b = bank(j + h)
                        nc.tensor.matmul(b[:, 0:DV + 1], ktok[:, h, :], vm[:, c, h, :], start=True, stop=True)\
                            .then_inc(aux_ready, 1)
                    pe.wait_ge(at_ready, c + 1)
                    pe.wait_ge(qt_ready, c + 1)
                    for h in range(H):
                        b = bank(j + H + h)
                        mm = nc.tensor.matmul(b[:, 0:DV + 1], att[:, h, :], vm[:, c, h, :],
                                              start=True, stop=c == 0)
                        if c:
                            pe.wait_ge(c_ready, H * (c - 1) + h + 1)
                            mm = nc.tensor.matmul(b[:, 0:DV + 1], qt[:, h, :], cst[:, c % 2, h, :],
                                                  start=False, stop=True)
                        mm.then_inc(aux_ready, 1)
                elif s[0] == "head":
                    which, h = s[1], s[2]
                    q = head_no[s]
                    v, wd = (vm, DV + 1) if which == "m" else (vg, DV)
                    pe.wait_ge(at_ready, (NC + 1) * (1 + (which == "g")))
                    pe.wait_ge(blk_ready, q + 1)
                    pe.wait_ge(st_in[q % 2], 16 * (q // 2 + 1))
                    if which == "m":
                        pe.wait_ge(st_n, h + 1)
                    else:
                        pe.wait_ge(v_ready, 2 * H * (NC + 1))
                    b = bank(j)
                    nc.tensor.matmul(b[0:TS, 0:wd], att[0:TS, h, 0:TS], v[0:TS, NC, h, 0:wd], start=True, stop=False)
                    for n in range(NB):
                        mm = nc.tensor.matmul(b[0:TS, 0:wd], qb[:, n * TS:(n + 1) * TS], st[q % 2][:, n, 0:wd],
                                              start=False, stop=n == NB - 1)
                    mm.then_inc(aux_ready, 1)
                    for n in range(NB):
                        b = bank(j + 1 + n)
                        nc.tensor.matmul(b[:, 0:wd], kb[:, n, :], v[0:TS, NC, h, 0:wd], start=True, stop=True)\
                            .then_inc(aux_ready, 1)
                elif s[0] == "la":
                    h = s[1]
                    for a in range(2):
                        nc.tensor.matmul(bank(j + a)[:, 0:HALF], wlr[:, h * DK:(h + 1) * DK],
                                         glr[:, a * HALF:(a + 1) * HALF], start=True, stop=True)\
                            .then_inc(aux_ready, 1)
                elif s[0] == "gkt":
                    c = s[1]
                    t0, ln = chunk_span(c)
                    if c == 0:
                        pe.wait_ge(fm_ready, 4 * H)
                    b = bank(j)
                    for h in range(H):
                        mm = nc.tensor.matmul(b[0:ln, h * ln:(h + 1) * ln], gk[:, h, t0:t0 + ln],
                                              gq[:, h, t0:t0 + ln], start=True, stop=True)
                    mm.then_inc(aux_ready, 1)
                    pe.wait_ge(kf_ready, c + 1)
                    b = bank(j + 1)
                    for h in range(H):
                        mm = nc.tensor.transpose(b[0:ln, h * P:(h + 1) * P], kf[:, h, 0:ln], ident[:, :])
                    mm.then_inc(aux_ready, 1)
                elif s[0] == "lev":
                    c, g = s[1:]
                    ln = chunk_span(c)[1]
                    for n, w in enumerate(levels_of(c, g)):
                        counts["lv"] += 1
                        pe.wait_ge(xl_ready, counts["lv"])
                        xl = xl_buffer(c, g, n)
                        b = bank(j + n)
                        for h in range(H):
                            late = xl[:, h, 0:ln].rearrange("p (b s) -> p b s", s=2 * w)[:, :, w:]
                            mm = nc.tensor.matmul(b[0:ln, h * ln // 2:(h + 1) * ln // 2]
                                                  .rearrange("p (b s) -> p b s", s=w),
                                                  xl[:, h, 0:ln], late, start=True, stop=True)
                        mm.then_inc(aux_ready, 1)
                elif s[0] == "gout":
                    c = s[1]
                    if c == 0:
                        pe.wait_ge(v_ready, 2 * H * (NC + 1))
                    pe.wait_ge(kt_ready, NC + 1 + c + 1)
                    for h in range(H):
                        b = bank(j + h)
                        nc.tensor.matmul(b[:, 0:DV], ktok[:, h, :], vg[:, c, h, :], start=True, stop=True)\
                            .then_inc(aux_ready, 1)
                    pe.wait_ge(at_ready, NC + 1 + c + 1)
                    pe.wait_ge(qt_ready, NC + 1 + c + 1)
                    for h in range(H):
                        b = bank(j + H + h)
                        mm = nc.tensor.matmul(b[:, 0:DV], att[:, h, :], vg[:, c, h, :], start=True, stop=c == 0)
                        if c:
                            pe.wait_ge(s_ready, H * (c - 1) + h + 1)
                            mm = nc.tensor.matmul(b[:, 0:DV], qt[:, h, :], gst[:, c % 2, h, :],
                                                  start=False, stop=True)
                        mm.then_inc(aux_ready, 1)

        @block.vector
        def _(dve):
            V = nc.vector
            n_step = [0]

            def link(ins):
                n_step[0] += 1
                ins.then_inc(dve_step, 1)
                dve.wait_ge(dve_step, n_step[0])

            def job(j):
                dve.wait_ge(aux_ready, j + 1)
                return aux[:, j % 4, :]

            def free(ins, j):
                ins.then_inc(aux_free[j % 4], 1)

            V.memset(ones[:, :], 1.0)
            V.memset(reset[:, :], 1.0)
            V.memset(qb[:, :], 0.0)
            V.memset(stat[:, :, :], 1.0)
            V.memset(rscol[:, :], 1.0)
            link(V.memset(rowc[:, :, :], 0.0))
            V.memset(reset[:, 0:TP:L], 0.0)
            V.memset(reset[:, TP:T:LS], 0.0).then_inc(init_done, 1)
            dve.wait_ge(init_done, 1)

            lv = 0
            ng = {"gt": 0, "stg": 0, "tn": 0}

            def rsum(n, j):
                ms, y, t = stat[:, 0, :], rscol[:, :] if n == 0 else stat[:, 1, :], stat[:, 2, :]
                b = job(j)
                V.tensor_scalar(ms[:, 0:NC], b[:, 0:NC], 1.0 / D, EPS, ALU.mult, ALU.add)
                free(V.tensor_scalar(ms[0:TS, NC:], b[0:TS, NC:NC + 1], 1.0 / D, EPS, ALU.mult, ALU.add), j)
                dve.wait_ge(aux_free[j % 4], j // 4 + 1)
                dve.sem_inc(ms_ready, 1)
                dve.wait_ge(ms_root, n + 1)
                link(V.reciprocal(y, y))
                link(V.scalar_tensor_tensor(t, y, -0.5, y, ALU.mult, ALU.mult))
                link(V.tensor_tensor(t, t, ms, ALU.mult))
                link(V.scalar_tensor_tensor(y, t, 1.5, y, ALU.add, ALU.mult))
                if n == 0:
                    dve.wait_ge(ident_in, 16)
                d = vrs if n else sq[:, 1]
                V.tensor_tensor(d[:, 0:TP].rearrange("p (c s) -> p c s", s=P), bcast(ident[:, :], NC, 1),
                                bcast(y[:, 0:NC], P, 2), ALU.mult)
                V.tensor_scalar(d[0:TS, TP:], ident[0:TS, 0:TS], y[0:TS, NC:NC + 1], None, ALU.mult)\
                    .then_inc(rs_diag, 1)

            def rspread(n, j):
                out = rsv if n else rs
                free(V.tensor_copy(out[:, 0:TP], job(j)), j)
                i = V.tensor_copy(out[:, TP:], job(j + 1)[:, 0:TS])
                free(i, j + 1)
                for a in range(2):
                    dve.wait_ge(aux_free[(j + a) % 4], (j + a) // 4 + 1)
                dve.sem_inc(rs_ready, 1)

            def split_lo_of(dst, src, hi, done):
                V.tensor_tensor(dst, src, f32(hi), ALU.subtract).then_inc(done, 1)

            def add_square(n, x):
                if n == 0:
                    link(V.tensor_tensor(acc[:, :], x, x, ALU.mult))
                else:
                    link(V.tensor_tensor(sq2[:, :], x, x, ALU.mult))
                    i = V.tensor_tensor(acc[:, :], acc[:, :], sq2[:, :], ALU.add)
                    if n == KT - 1:
                        i.then_inc(sq_sum, 1)
                    else:
                        link(i)

            def evac(kind, i, t):
                if (kind, i) != ("pgate", KT - 1):
                    dve.wait_ge(tile_ready, t + 1)
                full, fr = tile(t), tile_free[t % 2]
                if kind == "misc":
                    p = ps[:, t % 2, :, 0:HALF]
                    V.tensor_tensor(two(rowt[ROW_LI][:, :]), p[0:H], two(rs[0:H, :]), ALU.mult)
                    V.tensor_copy(two(rowt[ROW_XF][:, :]), p[32:32 + H])
                    V.tensor_copy(two(glr[:, :]), p[64:64 + RANK]).then_inc(fr, 1)
                    dve.wait_ge(fr, t // 2 + 1)
                    V.tensor_tensor(rowt[ROW_XF][:, :], rowt[ROW_XF][:, :], rs[0:H, :], ALU.mult)
                    link(V.tensor_tensor(glr[:, :], glr[:, :], rs[0:RANK, :], ALU.mult))
                elif kind in ("mq", "mk", "gq", "gk"):
                    dst = {"mq": mq, "mk": mk, "gq": gq, "gk": gk}[kind][:, i, :]
                    c = DK ** -0.5 if kind in ("mk", "gq") else 1.0
                    ins_ = V.scalar_tensor_tensor(two(dst), full, c, two(rs[:, :]), ALU.mult, ALU.mult)
                    ins_.then_inc(fr, 1)
                    dve.wait_ge(fr, t // 2 + 1)
                    dve.sem_inc(fm_ready, 1)
                elif kind in ("mo", "gg", "ga", "gb"):
                    k = ng["stg"]
                    ng["stg"] += 1
                    if k >= 2:
                        dve.wait_ge(stg_out[k % 2], 16 * (k // 2))
                    V.tensor_tensor(two(stg[:, k % 2, :]), full, two(rs[:, :]), ALU.mult).then_inc(fr, 1)
                elif kind == "pa":
                    g = gt_take()
                    V.tensor_tensor(two(merged[:, i, :]), full, two(gt[:, g % NGT, :]), ALU.mult).then_inc(fr, 1)
                    dve.wait_ge(fr, t // 2 + 1)
                    dve.sem_inc(gt_used, 1)
                elif kind == "pb":
                    if i == 0:
                        for k in range(2):
                            dve.wait_ge(stg_out[k], 16 * 16)
                    g = gt_take()
                    V.tensor_tensor(two(gt[:, g % NGT, :]), full, two(gt[:, g % NGT, :]), ALU.mult).then_inc(fr, 1)
                    dve.wait_ge(fr, t // 2 + 1)
                    link(V.tensor_tensor(merged[:, i, :], merged[:, i, :], gt[:, g % NGT, :], ALU.add))
                    dve.sem_inc(gt_used, 1)
                    dve.sem_inc(mg_pre, 1)
                    dve.wait_ge(mg_hi, i + 1)
                    split_lo_of(mglo[:, i, :], merged[:, i, :], mghi[:, i, :], mg_lo)
                elif kind == "wo":
                    dve.wait_ge(xr_in[i % 2], 16 * (i // 2 + 1))
                    if i >= 2:
                        dve.wait_ge(hs_out[i % 2], 16 * (i // 2))
                    x = hst[:, i % 2, :]
                    V.tensor_tensor(two(x), full, two(xr[:, i % 2, :]), ALU.add).then_inc(fr, 1)
                    dve.wait_ge(fr, t // 2 + 1)
                    dve.sem_inc(h_pre, 1)
                    add_square(i, x)
                    dve.wait_ge(c_hi, i + 1)
                    V.scalar_tensor_tensor(alo[:, i, :], x, gains[:, NORM_FFN, i:i + 1], f32(ahi[:, i, :]),
                                           ALU.mult, ALU.subtract).then_inc(c_lo, 1)
                elif kind == "gate":
                    if i >= 1:
                        dve.wait_ge(ff_g, 2 * i)
                    p0, p1 = ps[:, t % 2, 0, :], ps[:, t % 2, 1, :]
                    n1 = TP - HALF
                    tail = gbuf[:, 2 + TP:].rearrange("p (b s) -> p b s", s=2 + LS)
                    if i == 0:
                        V.memset(gbuf[:, 0:2], 0.0)
                    V.tensor_copy(tail[:, :, 0:2], convst[:, i, :, :])
                    V.tensor_tensor(gbuf[:, 2:2 + HALF], p0[:, 0:HALF], rsv[:, 0:HALF], ALU.mult)
                    V.tensor_tensor(gbuf[:, 2 + HALF:2 + TP], p1[:, 0:n1], rsv[:, HALF:TP], ALU.mult)
                    V.tensor_tensor(tail[:, :, 2:], p1[:, n1:HALF].rearrange("p (b s) -> p b s", s=LS),
                                    rsv[:, TP:].rearrange("p (b s) -> p b s", s=LS), ALU.mult).then_inc(fr, 1)
                    dve.wait_ge(fr, t // 2 + 1)
                    dve.sem_inc(ff_g, 1)
                    n = GW - 2
                    c = cv[:, 2:]
                    link(V.tensor_scalar(c, gbuf[:, 2:], convw[:, 2, i:i + 1], convb[:, i:i + 1], ALU.mult, ALU.add))
                    link(V.scalar_tensor_tensor(c, gbuf[:, 1:1 + n], convw[:, 1, i:i + 1], c, ALU.mult, ALU.add))
                    V.scalar_tensor_tensor(c, gbuf[:, 0:n], convw[:, 0, i:i + 1], c, ALU.mult, ALU.add)\
                        .then_inc(ff_cv, 1)
                elif kind == "val":
                    V.tensor_tensor(two(vrs[:, :]), full, two(rsv[:, :]), ALU.mult).then_inc(fr, 1)
                    dve.wait_ge(ff_sg, i + 1)
                    link(V.tensor_tensor(cv[:, 2:], cv[:, 2:], sg[:, 2:], ALU.mult))
                    dve.wait_ge(fr, t // 2 + 1)
                    tail = cv[:, 2 + TP:].rearrange("p (b s) -> p b s", s=2 + LS)
                    V.tensor_tensor(af[:, 0:TP], cv[:, 2:2 + TP], vrs[:, 0:TP], ALU.mult)
                    V.tensor_tensor(af[:, TP:].rearrange("p (b s) -> p b s", s=LS), tail[:, :, 2:],
                                    vrs[:, TP:].rearrange("p (b s) -> p b s", s=LS), ALU.mult).then_inc(ff_pre, 1)
                    dve.wait_ge(ff_hi, i + 1)
                    split_lo_of(aclo[:, i, :], af[:, :], achi[:, i, :], ff_lo)
                    dve.wait_ge(ff_lo, i + 1)
                elif kind == "down":
                    if i == 0:
                        dve.wait_ge(p_hi, PK)
                        V.tensor_tensor(plo[:, :, :], praw[:, :, :], f32(phi[:, :, :]), ALU.subtract)\
                            .then_inc(p_lo, PK)
                        dve.wait_ge(h2_in, 16)
                    x = h2[:, i, :]
                    V.tensor_tensor(two(x), full, two(x), ALU.add).then_inc(fr, 1)
                    dve.wait_ge(fr, t // 2 + 1)
                    dve.sem_inc(h2_new, 1)
                    add_square(i, x)
                elif kind == "pproj":
                    V.tensor_copy(two(pj[:, i, :]), full).then_inc(fr, 1)
                    dve.wait_ge(fr, t // 2 + 1)
                    dve.wait_ge(e_hi, i + 1)
                    V.scalar_tensor_tensor(elo[:, i, :], h2[:, i, :], gains[:, NORM_PLE, i:i + 1],
                                           f32(ehi[:, i, :]), ALU.mult, ALU.subtract).then_inc(e_lo, 1)
                elif kind == "pgate" and i == KT - 1:
                    for a in range(2):
                        dve.wait_ge(tile_ready if a else first_half, t + 1 if a else 1)
                        lo, hi = a * HALF, (a + 1) * HALF
                        g = sgp[:, i % 2, lo:hi]
                        V.tensor_tensor(g, ps[:, t % 2, a, 0:HALF], rsv[:, lo:hi], ALU.mult).then_inc(pg_pre, 1)
                        dve.wait_ge(pg_sig, i + a + 1)
                        link(V.tensor_tensor(g, g, pj[:, i, lo:hi], ALU.mult))
                        link(V.tensor_tensor(h3[:, i, lo:hi], g, h2[:, i, lo:hi], ALU.add))
                        link(V.tensor_tensor(sq2[:, lo:hi], h3[:, i, lo:hi], h3[:, i, lo:hi], ALU.mult))
                        V.tensor_tensor(acc[:, lo:hi], acc[:, lo:hi], sq2[:, lo:hi], ALU.add)\
                            .then_inc(sq_sum if a else sq_half, 1)
                elif kind == "pgate":
                    g = sgp[:, i % 2, :]
                    V.tensor_tensor(two(g), full, two(rsv[:, :]), ALU.mult).then_inc(fr, 1)
                    dve.wait_ge(fr, t // 2 + 1)
                    dve.sem_inc(pg_pre, 1)
                    dve.wait_ge(pg_sig, i + 1)
                    link(V.tensor_tensor(g, g, pj[:, i, :], ALU.mult))
                    V.tensor_tensor(h3[:, i, :], g, h2[:, i, :], ALU.add).then_inc(h3_new, 1)
                    dve.wait_ge(h3_new, i + 1)
                    add_square(i, h3[:, i, :])

            def gt_take():
                k = ng["gt"]
                ng["gt"] += 1
                dve.wait_ge(gt_sig, k + 1)
                return k

            def tnorm(which, c):
                n = ng["tn"]
                ng["tn"] += 1
                t0, ln = chunk_span(c)
                v = (vm if which == "m" else vg)[0:ln, c]
                S = [nsm[0:ln, k, :] for k in range(6)]
                mean, var = nmv[0:ln, :, 0], nmv[0:ln, :, 1]
                dve.wait_ge(h_out, h_out_of[(which, c)])
                for h in range(H):
                    i = V.bn_stats(nstat[0:ln, h, :], v[:, h, 0:DV])
                link(i)
                for h in range(H):
                    i = V.bn_aggr(nmv[0:ln, h, :], nstat[0:ln, h, :])
                link(i)
                if which == "m":
                    link(V.scalar_tensor_tensor(S[0], v[:, :, DV], -1.0, v[:, :, DV], ALU.mult, ALU.max))
                    link(V.tensor_tensor(S[0], S[0], colT[0:ln, c, 2, :], ALU.max))
                    link(V.reciprocal(S[1], S[0]))
                    link(V.tensor_tensor(S[2], var, S[1], ALU.mult))
                    link(V.tensor_tensor(S[2], S[2], S[1], ALU.mult))
                else:
                    link(V.tensor_tensor(S[2], mean, mean, ALU.mult))
                    link(V.tensor_tensor(S[2], S[2], var, ALU.add))
                V.tensor_scalar(S[2], S[2], 1.0, EPS, ALU.mult, ALU.add).then_inc(tn_pre, 1)
                dve.wait_ge(tn_root, n + 1)
                link(V.reciprocal(S[3], S[3]))
                link(V.scalar_tensor_tensor(S[4], S[3], -0.5, S[3], ALU.mult, ALU.mult))
                link(V.tensor_tensor(S[4], S[4], S[2], ALU.mult))
                link(V.scalar_tensor_tensor(S[3], S[4], 1.5, S[3], ALU.add, ALU.mult))
                if which == "m":
                    link(V.tensor_tensor(S[3], S[3], S[1], ALU.mult))
                for h in range(H):
                    if which == "m":
                        i = V.tensor_scalar(v[:, h, 0:DV], v[:, h, 0:DV], nmv[0:ln, h, 0:1], nsm[0:ln, 3, h:h + 1],
                                            ALU.subtract, ALU.mult)
                    else:
                        i = V.tensor_scalar(v[:, h, 0:DV], v[:, h, 0:DV], nsm[0:ln, 3, h:h + 1], None, ALU.mult)
                i.then_inc(tn_done, 1)
                dve.wait_ge(tn_done, n + 1)

            for s in sched:
                j, t = job_at[s], tile_at.get(s)
                if s[0] == "norm_in":
                    dve.wait_ge(gains_in, 16)
                    for k in range(KT):
                        dve.wait_ge(a_hi, k + 1)
                        V.scalar_tensor_tensor(alo[:, k, :], xT[:, k, :], gains[:, NORM_MIX, k:k + 1],
                                               f32(ahi[:, k, :]), ALU.mult, ALU.subtract).then_inc(a_lo, 1)
                        dve.wait_ge(in_sq, k + 1)
                        if k == 0:
                            i = V.tensor_copy(acc0[:, :], sq[:, 0, :])
                        else:
                            i = V.tensor_tensor(acc0[:, :], acc0[:, :], sq[:, k % 2, :], ALU.add)
                        i.then_inc(in_sq_used, 1)
                        dve.wait_ge(in_sq_used, k + 1)
                    dve.sem_inc(sq_sum, 1)
                elif s[0] == "unit":
                    continue
                elif s[0] == "tile":
                    kind, i = tiles_of(*units[s[1]])[s[2]]
                    if kind not in ("mv", "gv"):
                        evac(kind, i, t)
                    elif i[1] in V_BY_VECTOR:
                        h, c = i
                        if kind == "gv" and h == 0:
                            dve.wait_ge(cp_out, 16)
                            dve.wait_ge(aux_ready, job_at[("m1", NC)] + 4)
                        dve.wait_ge(tile_ready, t + 1)
                        dst = vm[:, c, h, 0:DV] if kind == "mv" else vg[:, c, h, :]
                        V.tensor_scalar(dst, ps[:, t % 2, 0, 0:DV], rscol[:, c:c + 1], None, ALU.mult)\
                            .then_inc(tile_free[t % 2], 1)
                        dve.wait_ge(tile_free[t % 2], t // 2 + 1)
                        dve.sem_inc(v_ready, 1)
                elif s[0] == "rsum":
                    rsum(s[1], j)
                elif s[0] == "rspread":
                    rspread(s[1], j)
                    if s[1] == 3:
                        for n in range(NY_POOL, KT):
                            V.scalar_tensor_tensor(yt[:, n, :], h3[:, n, :], gains[:, NORM_OUT, n:n + 1],
                                                   rsv[:, :], ALU.mult, ALU.mult).then_inc(y_ready, 1)
                elif s[0] == "rows" and s[1] == 0:
                    dve.wait_ge(const_in, NCONST)
                    R = [x[:, :] for x in rowt]
                    V.tensor_copy(cmask[:, :, :], cmaskf[:, :, :])
                    link(V.memset(rr[:, :], 0.0))
                    V.tensor_scalar(R[ROW_LI], R[ROW_LI], bgate[:, 0:1], None, ALU.add)
                    link(V.tensor_scalar(R[ROW_XF], R[ROW_XF], bgate[:, 1:2], None, ALU.add))
                    V.scalar_tensor_tensor(R[ROW_T], R[ROW_XF], -1.0, R[ROW_XF], ALU.mult, ALU.max)\
                        .then_inc(row_abs, 1)
                elif s[0] == "rows" and s[1] == 1:
                    dve.wait_ge(row_ln, 1)
                    link(V.scalar_tensor_tensor(R[ROW_LF], R[ROW_XF], 0.0, R[ROW_T], ALU.min, ALU.subtract))
                    V.tensor_tensor_scan(R[ROW_B], reset[0:H, :], R[ROW_LF], 0.0, ALU.mult, ALU.add)
                    V.tensor_copy(R[ROW_D0], R[ROW_LF])
                    V.tensor_copy(R[ROW_D1], R[ROW_LI])
                    link(V.tensor_tensor(rowc[:, 0, 0:NB], R[ROW_LF][:, TP:T:LS], m0[:, :], ALU.add))
                    V.memset(R[ROW_D0][:, TP:T:LS], -3.0e38)
                    link(V.tensor_tensor(R[ROW_D1][:, TP:T:LS], rowc[:, 0, 0:NB], R[ROW_LI][:, TP:T:LS], ALU.max))
                    link(V.tensor_tensor_scan(R[ROW_M], R[ROW_D0], R[ROW_D1], 0.0, ALU.add, ALU.max))
                elif s[0] == "rows" and s[1] == 2:
                    V.memset(rowc[:, 1, 0:1], 0.0)
                    V.tensor_copy(rowc[:, 1, 1:NC], R[ROW_M][:, L - 1:TP - 1:L])
                    V.tensor_copy(rowc[:, 1, NC:], m0[:, :])
                    V.tensor_copy(rowc[:, 2, 0:NC], R[ROW_B][:, L - 1:TP:L])
                    V.tensor_copy(rowc[:, 2, NC:], R[ROW_B][:, TP + LS - 1:T:LS])
                    V.tensor_copy(rowc[:, 3, 0:NC], R[ROW_M][:, L - 1:TP:L])
                    V.tensor_copy(rowc[:, 3, NC:], R[ROW_M][:, TP + LS - 1:T:LS])
                    V.tensor_tensor(r1[:, :], R[ROW_B], R[ROW_M], ALU.subtract)
                    link(V.tensor_tensor(rr[0:H, :], R[ROW_LI], R[ROW_B], ALU.subtract))
                    V.tensor_copy(mout[:, 0:NB], rowc[:, 3, NC:])
                    V.tensor_copy(mout[:, NB:], rowc[:, 3, NC - 1:NC])
                    link(V.tensor_tensor(rowc[:, 2, :], rowc[:, 2, :], rowc[:, 3, :], ALU.subtract))
                    link(V.tensor_tensor(rowc[:, 4, :], rowc[:, 2, :], rowc[:, 1, :], ALU.add))

                    def spread(dst, row, k):
                        for lo, hi, n, w, c0 in ((0, TP, NC, L, 0), (TP, T, NB, LS, NC)):
                            V.tensor_tensor(dst[:, lo:hi].rearrange("p (c s) -> p c s", s=w),
                                            row[:, lo:hi].rearrange("p (c s) -> p c s", s=w),
                                            bcast(rowc[:, k, c0:c0 + n], w, 2), ALU.add)
                    spread(ri[:, :], r1[:, :], 1)
                    spread(R[ROW_T], rr[0:H, :], 2)
                    link(V.tensor_scalar(rowc[:, 4, :], rowc[:, 4, :], 0.0, None, ALU.min))
                    V.tensor_scalar(ri[:, :], ri[:, :], 0.0, None, ALU.min)
                    V.tensor_scalar(R[ROW_T], R[ROW_T], 0.0, None, ALU.min).then_inc(row_pre, 1)
                elif s[0] == "rows":
                    b = job(j)
                    for c in range(NC):
                        i = V.tensor_copy(colT[:, c], b[:, c * P:(c + 1) * P]
                                          .rearrange("p (r k) -> p r k", k=32)[:, 0:3, 0:H])
                    free(i, j)
                    b = job(j + 1)
                    free(V.tensor_copy(colT[0:TS, NC], b[0:TS, 0:P].rearrange("p (r k) -> p r k", k=32)[:, 0:3, 0:H]),
                         j + 1)
                    b = job(j + 2)
                    free(V.tensor_copy(carry[:, :, :].rearrange("p h c -> p (h c)"), b[:, 0:H * (NC + NB)]), j + 2)
                    dve.wait_ge(aux_free[(j + 2) % 4], (j + 2) // 4 + 1)
                elif s[0] == "m1":
                    c = s[1]
                    t0, ln = chunk_span(c)

                    def hv(x, n=ln):
                        return x.rearrange("p (h s) -> p h s", h=H)
                    b = job(j)
                    for h in range(H):
                        i = V.scalar_tensor_tensor(pw[0:ln, h, 0:ln], b[0:ln, h * ln:(h + 1) * ln],
                                                   colT[0:ln, c, 0, h:h + 1], nmask[0:ln, int(c == NC), 0:ln],
                                                   ALU.add, ALU.min)
                    free(i, j)
                    dve.wait_ge(aux_free[j % 4], j // 4 + 1)
                    dve.sem_inc(p_pre, 1)
                    b = job(j + 1)
                    i = V.tensor_tensor(qt[:, :, 0:ln], mq[:, :, t0:t0 + ln], hv(b[:, 0:H * ln]), ALU.mult)
                    free(i, j + 1)
                    dve.wait_ge(aux_free[(j + 1) % 4], (j + 1) // 4 + 1)
                    dve.sem_inc(qt_ready, 1)
                    b = job(j + 2)
                    i = V.tensor_tensor(ktok[0:ln, :, :], hv(b[0:ln, 0:H * P]), bcast(colT[0:ln, c, 1, :], P, 2),
                                        ALU.mult)
                    free(i, j + 2)
                    dve.wait_ge(aux_free[(j + 2) % 4], (j + 2) // 4 + 1)
                    dve.sem_inc(kt_ready, 1)
                    b = job(j + 3)
                    dve.wait_ge(p_exp, c + 1)
                    i = V.tensor_tensor(att[0:ln, :, 0:ln], pw[0:ln, :, 0:ln], hv(b[0:ln, 0:H * ln]), ALU.mult)
                    free(i, j + 3)
                    dve.wait_ge(aux_free[(j + 3) % 4], (j + 3) // 4 + 1)
                    dve.sem_inc(at_ready, 1)
                elif s[0] == "m2":
                    c = s[1]
                    for h in range(H):
                        b = job(j + h)
                        new = cst[:, (c + 1) % 2, h, :]
                        if c == 0:
                            i = V.tensor_copy(new, b[:, 0:DV + 1])
                        else:
                            i = V.scalar_tensor_tensor(new, cst[:, c % 2, h, :], carry[:, h, c:c + 1],
                                                       b[:, 0:DV + 1], ALU.mult, ALU.add)
                        free(i, j + h)
                        dve.wait_ge(aux_free[(j + h) % 4], (j + h) // 4 + 1)
                        dve.sem_inc(c_ready, 1)
                    if c == NC - 1:
                        V.tensor_copy(nout[:, :, NB], cst[:, 0, :, DV]).then_inc(c_ready, 1)
                elif s[0] == "la":
                    h = s[1]
                    for a in range(2):
                        b = job(j + a)
                        i = V.tensor_scalar(cum[:, h, a * HALF:(a + 1) * HALF], b[:, 0:HALF], blr[:, h:h + 1],
                                            None, ALU.add)
                        free(i, j + a)
                    dve.wait_ge(aux_free[(j + 1) % 4], (j + 1) // 4 + 1)
                    V.scalar_tensor_tensor(stg[:, h % 2, :], cum[:, h, :], -1.0, cum[:, h, :], ALU.mult, ALU.max)\
                        .then_inc(la_abs, 1)
                    dve.wait_ge(la_ln, h + 1)
                    link(V.scalar_tensor_tensor(cum[:, h, :], cum[:, h, :], 0.0, stg[:, h % 2, :],
                                                ALU.min, ALU.subtract))
                    V.tensor_tensor_scan(cum[:, h, :], reset[:, :], cum[:, h, :], 0.0, ALU.mult, ALU.add)\
                        .then_inc(cum_ready, 1)
                elif s[0] == "gpre":
                    c = s[1]
                    t0, ln = chunk_span(c)
                    sl = L if c < NC else LS
                    cc = cum[:, :, t0:t0 + ln]
                    dve.wait_ge(aux_ready, j)
                    if c == 0:
                        dve.wait_ge(cum_ready, H)
                    dve.sem_inc(g_go, 1)
                    link(V.memset(att[:, :, :], 0.0))
                    for h in range(H):
                        x = cc[:, h, :].rearrange("p (b s) -> p b s", s=sl)
                        i = V.tensor_tensor(kf[:, h, 0:ln].rearrange("p (b s) -> p b s", s=sl),
                                            bcast(x[:, :, sl - 1], sl, 2), x, ALU.subtract)
                    i.then_inc(kd_sub, 1)
                    dve.wait_ge(kd_exp, c + 1)
                    V.tensor_tensor(kf[:, :, 0:ln], kf[:, :, 0:ln], gk[:, :, t0:t0 + ln], ALU.mult)\
                        .then_inc(kf_ready, 1)
                    dve.wait_ge(eb_ready, c + 1)
                    V.tensor_tensor(qt[:, :, 0:ln], pw[:, :, 0:ln], gq[:, :, t0:t0 + ln], ALU.mult)\
                        .then_inc(qt_ready, 1)
                elif s[0] == "lpre":
                    c, g = s[1:]
                    t0, ln = chunk_span(c)
                    cc = cum[:, :, t0:t0 + ln]
                    for n, w in enumerate(levels_of(c, g)):
                        xl = xl_buffer(c, g, n)
                        for h in range(H):
                            x = cc[:, h, :].rearrange("p (b s) -> p b s", s=2 * w)
                            i = V.tensor_tensor(xl[:, h, 0:ln].rearrange("p (b s) -> p b s", s=2 * w), x,
                                                bcast(x[:, :, w - 1], 2 * w, 2), ALU.subtract)
                        i.then_inc(xl_sub, 1)
                    for n, w in enumerate(levels_of(c, g)):
                        lv += 1
                        dve.wait_ge(xl_exp, lv)
                        xl = xl_buffer(c, g, n)[:, :, 0:ln]
                        for src, lo in ((gk, 0), (gq, w)):
                            x = xl.rearrange("p h (b s) -> p h b s", s=2 * w)[:, :, :, lo:lo + w]
                            y = src[:, :, t0:t0 + ln].rearrange("p h (b s) -> p h b s", s=2 * w)[:, :, :, lo:lo + w]
                            i = V.tensor_tensor(x, x, y, ALU.mult)
                        i.then_inc(xl_ready, 1)
                elif s[0] == "gkt":
                    c = s[1]
                    ln = chunk_span(c)[1]
                    b = job(j)
                    i = V.copy_predicated(att[0:ln, :, 0:ln], bcast(cmask[0:ln, 7, 0:ln], H, 1),
                                          b[0:ln, 0:H * ln].rearrange("p (h s) -> p h s", h=H))
                    free(i, j)
                    b = job(j + 1)
                    i = V.tensor_copy(ktok[0:ln, :, :], b[0:ln, 0:H * P].rearrange("p (h s) -> p h s", h=H))
                    free(i, j + 1)
                    for a in range(2):
                        dve.wait_ge(aux_free[(j + a) % 4], (j + a) // 4 + 1)
                    dve.sem_inc(kt_ready, 1)
                elif s[0] == "lev":
                    c, g = s[1:]
                    ln = chunk_span(c)[1]
                    for n, w in enumerate(levels_of(c, g)):
                        b = job(j + n)
                        k = PROMPT_LEVELS.index(w)

                        def late(x):
                            return x.rearrange("p h (b s) -> p h b s", s=2 * w)[:, :, :, w:]
                        i = V.copy_predicated(late(att[0:ln, :, 0:ln]), late(bcast(cmask[0:ln, k, 0:ln], H, 1)),
                                              b[0:ln, 0:H * ln // 2].rearrange("p (h b s) -> p h b s", h=H, s=w))
                        free(i, j + n)
                        dve.wait_ge(aux_free[(j + n) % 4], (j + n) // 4 + 1)
                    if g == (3 if c < NC else 1):
                        dve.sem_inc(at_ready, 1)
                elif s[0] == "gout":
                    c = s[1]
                    if c == 0:
                        dve.wait_ge(st_out[1], out_count(3))
                    for h in range(H):
                        b = job(j + h)
                        new = gst[:, (c + 1) % 2, h, :]
                        if c == 0:
                            i = V.tensor_copy(new, b[:, 0:DV])
                        else:
                            i = V.scalar_tensor_tensor(new, gst[:, c % 2, h, :], pw[:, h, L - 1:L], b[:, 0:DV],
                                                       ALU.mult, ALU.add)
                        free(i, j + h)
                        dve.wait_ge(aux_free[(j + h) % 4], (j + h) // 4 + 1)
                        dve.sem_inc(s_ready, 1)
                elif s[0] == "hpre":
                    h = s[2]
                    q = head_no[("head",) + s[1:]]
                    dve.wait_ge(aux_ready, j)
                    V.tensor_copy(qb[:, :].rearrange("p (b s) -> p b s", s=TS + LS)[:, :, 0:LS],
                                  qt[:, h, 0:TS].rearrange("p (b s) -> p b s", s=LS))
                    V.tensor_tensor(kb[:, :, :], bcast(ktok[0:TS, h, :], NB, 1), bcast(bmask[:, :], P, 2), ALU.mult)\
                        .then_inc(blk_ready, 1)
                    dve.wait_ge(st_in[q % 2], 16 * (q // 2 + 1))
                    if s[1] == "m":
                        V.tensor_copy(st[q % 2][:, :, DV], nst[:, h, :]).then_inc(st_n, 1)
                        dve.wait_ge(st_n, h + 1)
                elif s[0] == "head":
                    which, h = s[1], s[2]
                    q = head_no[s]
                    x = st[q % 2]
                    wd = DV + 1 if which == "m" else DV
                    for n in range(NB):
                        b = job(j + 1 + n)
                        k = carry[:, h, NC + n:NC + n + 1] if which == "m" else \
                            pw[:, h, (n + 1) * LS - 1:(n + 1) * LS]
                        i = V.scalar_tensor_tensor(x[:, n, 0:wd], x[:, n, 0:wd], k, b[:, 0:wd], ALU.mult, ALU.add)
                        free(i, j + 1 + n)
                    dve.wait_ge(aux_free[(j + NB) % 4], (j + NB) // 4 + 1)
                    if which == "m":
                        link(V.tensor_copy(nout[:, h, 0:NB], x[:, :, DV]))
                    dve.sem_inc(st_new, 1)
                elif s[0] == "tnorm":
                    tnorm(s[1], s[2])
                elif s[0] == "bt":
                    which, n = s[1], s[2]
                    b = job(j)
                    if which == "m" and n == 0:
                        for k in range(2):
                            dve.wait_ge(st_out[k], out_count(6 + k))
                    g = gt_take()
                    if which == "g":
                        V.tensor_tensor(gt[:, g % NGT, :], gt[:, g % NGT, :], sgt[:, :], ALU.mult).then_inc(silu_used, 1)
                        dve.wait_ge(silu_used, n + 1)
                    k = gains[:, NORM_M if which == "m" else NORM_G, n:n + 1]
                    free(V.scalar_tensor_tensor(bt_t[:, 0, 0:TP], b, k, gt[:, g % NGT, 0:TP], ALU.mult, ALU.mult), j)
                    free(V.scalar_tensor_tensor(bt_t[:, 0, TP:], job(j + 1)[:, 0:TS], k, gt[:, g % NGT, TP:],
                                                ALU.mult, ALU.mult), j + 1)
                    for a in range(2):
                        dve.wait_ge(aux_free[(j + a) % 4], (j + a) // 4 + 1)
                    dve.sem_inc(gt_used, 1)
                    dve.sem_inc(bt_pre, 1)
                    m = n + (KT if which == "g" else 0)
                    dve.wait_ge(bt_hi, m + 1)
                    split_lo_of((hmlo if which == "m" else alo)[:, n, :], bt_t[:, 0, :],
                                (hmhi if which == "m" else ahi)[:, n, :], bt_lo)
                    dve.wait_ge(bt_lo, m + 1)

        @block.scalar
        def _(act):
            A = nc.scalar
            n_step = [0]

            def link(ins):
                n_step[0] += 1
                ins.then_inc(act_step, 1)
                act.wait_ge(act_step, n_step[0])

            def hi_part(u):
                s, n = u % 2, width(u)
                act.wait_ge(raw_in[s], raw_count(u))
                if u >= 2:
                    used(act, u - 2)
                A.activation(whi[:, s, 0:n], wraw[:, s, 0:n], ACT.Copy).then_inc(split_hi, 1)

            def root(src, dst, done):
                A.activation(dst, src, ACT.Sqrt).then_inc(done, 1)

            gate_use = []
            for s in sched:
                if s[0] == "bt":
                    gate_use.append(((ZMO if s[1] == "m" else ZGG) + s[2], s[1] == "g"))
                elif s[0] == "tile" and units[s[1]][0] in ("pa", "pb"):
                    kind, i = tiles_of(*units[s[1]])[s[2]]
                    gate_use.append(((ZGA if kind == "pa" else ZGB) + i, False))
            ng = {"gt": 0, "gl": 0, "stg": 0, "tn": 0, "lv": 0}

            def gate_load():
                k = ng["gl"]
                if k >= len(gate_use):
                    return
                ng["gl"] += 1
                if k >= NGT:
                    act.wait_ge(gt_used, k - NGT + 1)
                z = gate_use[k][0]
                act.wait_ge(stg_out[z % 2], 16 * (z // 2 + 1))
                act.dma_start(gt[:, k % NGT, :], zs[z, :, :]).then_inc(gt_in[k % NGT], 16)

            def gate_sigmoid():
                k = ng["gt"]
                ng["gt"] += 1
                act.wait_ge(gt_in[k % NGT], 16 * (k // NGT + 1))
                silu = gate_use[k][1]
                if silu:
                    m = sum(x[1] for x in gate_use[:k])
                    if m:
                        act.wait_ge(silu_used, m)
                A.activation(sgt[:, :] if silu else gt[:, k % NGT, :], gt[:, k % NGT, :], ACT.Sigmoid).then_inc(gt_sig, 1)

            def state_load(q):
                if q >= 2:
                    act.wait_ge(st_out[q % 2], out_count(q - 2))
                if q == 5:
                    act.wait_ge(cp_out, 32)
                src = ins["C_in"] if q < H else ins["S_in"]
                act.dma_start(st[q % 2][:, :, 0:DV], src[q % H, :, :, :]).then_inc(st_in[q % 2], 16)

            def copy_out(j, dst, src_p, wd):
                act.wait_ge(aux_ready, j + 1)
                i = A.activation(dst, aux[0:src_p, j % 4, 0:wd], ACT.Copy)
                i.then_inc(aux_free[j % 4], 1)
                act.wait_ge(aux_free[j % 4], j // 4 + 1)
                act.sem_inc(h_out, 1)

            for n in range(4):
                act.dma_start(xT[:, 2 * n:2 * n + 2, :], ins["xT"][:, 2 * n:2 * n + 2, :]).then_inc(x_in[n], 16)
            act.wait_ge(gains_in, 16)
            for s in sched:
                j, t = job_at[s], tile_at.get(s)
                if s[0] == "norm_in":
                    for k in range(KT):
                        act.wait_ge(x_in[k // 2], 16)
                        A.activation(ahi[:, k, :], xT[:, k, :], ACT.Copy, scale=gains[:, NORM_MIX, k:k + 1])\
                            .then_inc(a_hi, 1)
                        if k >= 2:
                            act.wait_ge(in_sq_used, k - 1)
                        A.activation(sq[:, k % 2, :], xT[:, k, :], ACT.Square).then_inc(in_sq, 1)
                        if k == 0:
                            hi_part(0)
                        if k == KT - 1:
                            hi_part(1)
                elif s[0] == "unit":
                    u = s[1]
                    if u >= 1 and u + 1 < len(units):
                        hi_part(u + 1)
                elif s[0] == "tile":
                    kind, i = tiles_of(*units[s[1]])[s[2]]
                    tt = t
                    if kind in ("mv", "gv"):
                        h, c = i
                        if c in V_BY_VECTOR:
                            continue
                        t0, ln = chunk_span(c)
                        if kind == "mv" and h == 0 and c == 0:
                            act.wait_ge(a_lo, KT)
                            act.wait_ge(rs_diag, 1)
                            A.activation(vm[:, 0:NC, :, DV], ones[:, 0:NC * H]
                                         .rearrange("p (c h) -> p c h", h=H), ACT.Copy)
                            A.activation(vm[0:TS, NC, :, DV], ones[0:TS, 0:H], ACT.Copy)
                        if kind == "gv" and h == 0 and c == 0:
                            act.wait_ge(cp_out, 16)
                            act.wait_ge(aux_ready, job_at[("m1", NC)] + 4)
                        if kind == "mv" and 1 <= h <= 2 and c == 0:
                            state_load(h - 1)
                        act.wait_ge(tile_ready, tt + 1)
                        dst = vm[0:ln, c, h, 0:DV] if kind == "mv" else vg[0:ln, c, h, :]
                        A.activation(dst, ps[0:ln, tt % 2, 0, 0:DV], ACT.Copy, scale=rscol[0:ln, c:c + 1])\
                            .then_inc(tile_free[tt % 2], 1)
                        act.wait_ge(tile_free[tt % 2], tt // 2 + 1)
                        act.sem_inc(v_ready, 1)
                    elif kind in ("mo", "gg", "ga", "gb"):
                        k = ng["stg"]
                        ng["stg"] += 1
                        act.wait_ge(tile_free[tt % 2], tt // 2 + 1)
                        act.dma_start(zs[k, :, :], stg[:, k % 2, :]).then_inc(stg_out[k % 2], 16)
                    elif kind in ("pa", "pb"):
                        gate_sigmoid()
                        if kind == "pb":
                            act.wait_ge(mg_pre, i + 1)
                            A.activation(mghi[:, i, :], merged[:, i, :], ACT.Copy).then_inc(mg_hi, 1)
                        if kind == "pb" and i == KT - 1:
                            act.wait_ge(mg_lo, KT)
                            for k in range(2):
                                act.dma_start(xr[:, k, :], ins["xT"][:, k, :]).then_inc(xr_in[k], 16)
                        gate_load()
                    elif kind == "wo":
                        act.wait_ge(h_pre, i + 1)
                        act.dma_start(hs[i, :, :], hst[:, i % 2, :]).then_inc(hs_out[i % 2], 16)
                        if i + 2 < KT:
                            act.dma_start(xr[:, i % 2, :], ins["xT"][:, i + 2, :]).then_inc(xr_in[i % 2], 16)
                        A.activation(ahi[:, i, :], hst[:, i % 2, :], ACT.Copy,
                                     scale=gains[:, NORM_FFN, i:i + 1]).then_inc(c_hi, 1)
                    elif kind == "gate":
                        act.wait_ge(ff_g, 2 * i + 1)
                        A.activation(convout[:, i, 0:2], gbuf[:, TP:TP + 2], ACT.Copy)
                        A.activation(convout[:, i, 2:].rearrange("p (b s) -> p b s", s=2),
                                     gbuf[:, 2 + TP:].rearrange("p (b s) -> p b s", s=2 + LS)[:, :, LS:],
                                     ACT.Copy).then_inc(ff_g, 1)
                        act.wait_ge(ff_cv, i + 1)
                        A.activation(sg[:, 2:], cv[:, 2:], ACT.Sigmoid).then_inc(ff_sg, 1)
                    elif kind == "val":
                        act.wait_ge(ff_pre, i + 1)
                        if i == 0:
                            act.wait_ge(hs_out[0], 16 * KT // 2)
                            act.wait_ge(hs_out[1], 16 * KT // 2)
                        A.activation(achi[:, i, :], af[:, :], ACT.Copy).then_inc(ff_hi, 1)
                        if i == FT - 1:
                            act.wait_ge(tile_ready, tt + 1)
                            act.dma_start(h2[:, :, :], hs.rearrange("k p t -> p k t")).then_inc(h2_in, 16)
                            act.dma_start(praw[:, :, :], ins["pT"]).then_inc(p_in, 16)
                            act.wait_ge(ff_g, 2 * FT)
                            act.dma_start(outs["conv"], convout[:, :, :]).then_inc(out_done, 16)
                    elif kind == "down" and i == 0:
                        act.wait_ge(p_in, 16)
                        A.activation(phi[:, :, :], praw[:, :, :], ACT.Copy).then_inc(p_hi, PK)
                    elif kind == "pproj":
                        if i == 0:
                            act.wait_ge(h2_new, KT)
                        A.activation(ehi[:, i, :], h2[:, i, :], ACT.Copy,
                                     scale=gains[:, NORM_PLE, i:i + 1]).then_inc(e_hi, 1)
                    elif kind == "pgate" and i == KT - 1:
                        for a in range(2):
                            act.wait_ge(pg_pre, i + a + 1)
                            x = sgp[:, i % 2, a * HALF:(a + 1) * HALF]
                            A.activation(x, x, ACT.Sigmoid).then_inc(pg_sig, 1)
                    elif kind == "pgate":
                        act.wait_ge(pg_pre, i + 1)
                        A.activation(sgp[:, i % 2, :], sgp[:, i % 2, :], ACT.Sigmoid).then_inc(pg_sig, 1)
                        if 1 <= i <= NY_POOL:
                            act.wait_ge(h3_new, i)
                            A.activation(yt[:, i - 1, :], h3[:, i - 1, :], ACT.Copy,
                                         scale=gains[:, NORM_OUT, i - 1:i]).then_inc(y_pre, 1)
                elif s[0] == "rsum":
                    n = s[1]
                    act.wait_ge(ms_ready, n + 1)
                    root(stat[:, 0, :], rscol[:, :] if n == 0 else stat[:, 1, :], ms_root)
                elif s == ("rspread", 3):
                    for n in range(NY_POOL, KT):
                        act.wait_ge(y_ready, n - NY_POOL + 1)
                        act.dma_start(outs["yT"][:, n, :], yt[:, n, :]).then_inc(y_out, 16)
                elif s == ("rows", 0):
                    act.wait_ge(row_abs, 1)
                    x = rowt[ROW_T][:, :]
                    link(A.activation(x, x, ACT.Exp, scale=-1.0))
                    A.activation(x, x, ACT.Ln, bias=1.0).then_inc(row_ln, 1)
                elif s == ("rows", 2):
                    act.wait_ge(row_pre, 1)
                    x = rowt[ROW_T][:, :]
                    A.activation(ri[:, :], ri[:, :], ACT.Exp)
                    A.activation(rr[32:32 + H, :], x, ACT.Exp)
                    A.activation(rr[64:64 + H, :], rowt[ROW_M][:, :], ACT.Exp, scale=-1.0)
                    A.activation(rowc[:, 4, :], rowc[:, 4, :], ACT.Exp).then_inc(row_exp, 4)
                    act.dma_start(outs["m"], mout[:, :]).then_inc(out_done, 16)
                elif s[0] == "m1":
                    c = s[1]
                    t0, ln = chunk_span(c)
                    act.wait_ge(p_pre, c + 1)
                    A.activation(pw[0:ln, :, 0:ln], pw[0:ln, :, 0:ln], ACT.Exp).then_inc(p_exp, 1)
                elif s[0] == "m2":
                    c = s[1]
                    for h in range(H):
                        copy_out(j + H + h, vm[:, c, h, :], P, DV + 1)
                    if c == NC - 1:
                        act.wait_ge(c_ready, NC * H + 1)
                        act.dma_start(outs["C_p"], cst[:, 0, :, 0:DV]).then_inc(cp_out, 16)
                elif s[0] == "head":
                    which, h = s[1], s[2]
                    q = head_no[s]
                    wd = DV + 1 if which == "m" else DV
                    if q >= 1 and q + 1 < 2 * H:
                        state_load(q + 1)
                    act.wait_ge(aux_ready, j + 1)
                    i = A.activation(so[:, 0, 0:wd], aux[0:TS, j % 4, 0:wd], ACT.Copy)
                    i.then_inc(aux_free[j % 4], 1)
                    act.wait_ge(aux_free[j % 4], j // 4 + 1)
                    act.wait_ge(aux_ready, j + 1 + NB)
                    link(A.activation((vm if which == "m" else vg)[0:TS, NC, h, 0:wd], so[:, 0, 0:wd], ACT.Copy))
                    act.sem_inc(h_out, 1)
                    act.wait_ge(st_new, q + 1)
                    dst = outs["C_s"] if which == "m" else outs["S_s"]
                    act.dma_start(dst[h, :, :, :], st[q % 2][:, :, 0:DV]).then_inc(st_out[q % 2], 16)
                    if q == 3:
                        act.dma_start(outs["n"], nout[:, :, :]).then_inc(out_done, 16)
                elif s[0] == "la":
                    act.wait_ge(la_abs, s[1] + 1)
                    x = stg[:, s[1] % 2, :]
                    link(A.activation(x, x, ACT.Exp, scale=-1.0))
                    A.activation(x, x, ACT.Ln, bias=1.0).then_inc(la_ln, 1)
                elif s[0] == "gpre":
                    c = s[1]
                    t0, ln = chunk_span(c)
                    act.wait_ge(g_go, c + 1)
                    act.wait_ge(kd_sub, c + 1)
                    A.activation(kf[:, :, 0:ln], kf[:, :, 0:ln], ACT.Exp, scale=1 / TAU).then_inc(kd_exp, 1)
                    A.activation(pw[:, :, 0:ln], cum[:, :, t0:t0 + ln], ACT.Exp, scale=1 / TAU).then_inc(eb_ready, 1)
                elif s[0] == "lpre":
                    c, g = s[1:]
                    ln = chunk_span(c)[1]
                    for n, w in enumerate(levels_of(c, g)):
                        ng["lv"] += 1
                        act.wait_ge(xl_sub, ng["lv"])
                        x = xl_buffer(c, g, n)[:, :, 0:ln].rearrange("p h (b s) -> p h b s", s=2 * w)
                        A.activation(x[:, :, :, 0:w], x[:, :, :, 0:w], ACT.Exp, scale=-1 / TAU)
                        A.activation(x[:, :, :, w:], x[:, :, :, w:], ACT.Exp, scale=1 / TAU).then_inc(xl_exp, 1)
                elif s[0] == "gout":
                    c = s[1]
                    for h in range(H):
                        copy_out(j + H + h, vg[:, c, h, :], P, DV)
                    if c == NC - 1:
                        act.wait_ge(s_ready, NC * H)
                        act.dma_start(outs["S_p"], gst[:, 0, :, :]).then_inc(cp_out, 16)
                elif s[0] == "tnorm":
                    ng["tn"] += 1
                    act.wait_ge(tn_pre, ng["tn"])
                    ln = chunk_span(s[2])[1]
                    root(nsm[0:ln, 2, :], nsm[0:ln, 3, :], tn_root)
                elif s[0] == "bt":
                    m = s[2] + (KT if s[1] == "g" else 0)
                    if m == 0:
                        act.wait_ge(tn_done, 2 * (NC + 1))
                        for _ in range(NGT):
                            gate_load()
                    gate_sigmoid()
                    act.wait_ge(bt_pre, m + 1)
                    A.activation((hmhi if s[1] == "m" else ahi)[:, s[2], :], bt_t[:, 0, :], ACT.Copy)\
                        .then_inc(bt_hi, 1)
                    gate_load()
            act.wait_ge(out_done, 48)
            act.wait_ge(y_out, 16 * KT)
            for k in range(2):
                act.wait_ge(st_out[k], out_count(6 + k))
            act.wait_ge(cp_out, 32)


def pack(w, width):
    k, n = w.shape
    v = w.reshape(k // P, P, n // width, width).transpose(2, 1, 0, 3)
    return np.ascontiguousarray(v).reshape(n // width, P, k // P * width)


def vec(g):
    return np.ascontiguousarray(g.reshape(-1, P).T)


def constants():
    i = np.arange(P)
    s, t = i[:, None], i[None, :]
    cmask = np.zeros((P, 8, P), np.float32)
    for n, w in enumerate(PROMPT_LEVELS):
        cmask[:, n, :] = (s // (2 * w) == t // (2 * w)) & (s // w % 2 == 0) & (t // w % 2 == 1)
    cmask[:, 7, :] = s == t
    nmask = np.full((P, 2, P), -1e30, np.float32)
    nmask[:, 0, :][s <= t] = 0.0
    nmask[:, 1, :][(s <= t) & (s // LS == t // LS)] = 0.0
    sel = np.zeros((H, H, P), np.float32)
    for h in range(H):
        sel[h, h, :] = 1.0
    bmask = (np.arange(TS)[:, None] // LS == np.arange(NB)[None, :]).astype(np.float32)
    return {"ident": np.eye(P, dtype=np.float32), "cmask": cmask, "nmask": nmask, "sel": sel, "bmask": bmask}


def kernel(x_prompt, x_sample, state_mlstm_C, state_mlstm_n, state_mlstm_m, state_gla_S,
           state_ffn_conv, p_prompt, p_sample, norm_mix_g, w_in, b_mi, b_mf, g_mnorm, w_lr2,
           b_lr2, g_gnorm, w_pa, w_pb, w_o, norm_ffn_g, w_up, conv_w, conv_b, w_down,
           norm_ple_g, w_ple_gate, w_ple_proj, final_norm_g):
    import concourse.bacc as bacc
    from concourse.bass_utils import run_bass_kernel_spmd as run

    a = np.asarray

    def tokens(p, s):
        x = np.concatenate([a(p).reshape(TP, -1), a(s).reshape(TS, -1)], axis=0)
        return np.ascontiguousarray(x.T.reshape(-1, P, T).transpose(1, 0, 2))

    w = a(w_in)[0]
    sizes = [512, 512, 1024, 4, 4, 1024, 512, 512, 1024, RANK, 1024, 1024, 1024]
    o = np.concatenate([[0], np.cumsum(sizes)])
    col = {n: w[:, o[k]:o[k + 1]] for k, n in enumerate(
        ("mq", "mk", "mv", "mi", "mf", "mo", "gq", "gk", "gv", "glr", "gg", "ga", "gb"))}
    main = np.concatenate([col[n] for n in ("mq", "mk", "mv", "gq", "gk", "gv", "mo", "gg", "ga", "gb")], axis=1)
    misc = np.concatenate([col["mi"], col["mf"], col["glr"]], axis=1)
    misc_cols = np.zeros((P, KT, P), np.float32)
    for at, n, lo in ((0, H, 0), (32, H, H), (64, RANK, 2 * H)):
        misc_cols[:, :, at:at + n] = misc.reshape(KT, P, -1).transpose(1, 0, 2)[:, :, lo:lo + n]
    up = a(w_up)[0].reshape(D, 2, FT, P).transpose(0, 2, 1, 3).reshape(D, 2 * FF)
    arrays = dict(
        xT=tokens(x_prompt, x_sample), pT=tokens(p_prompt, p_sample),
        C_in=np.ascontiguousarray(a(state_mlstm_C)[0].transpose(1, 2, 0, 3)),
        S_in=np.ascontiguousarray(a(state_gla_S)[0].transpose(1, 2, 0, 3)),
        nst=np.ascontiguousarray(a(state_mlstm_n)[0].transpose(2, 1, 0)),
        m0=np.ascontiguousarray(a(state_mlstm_m)[0].T),
        convst=np.ascontiguousarray(a(state_ffn_conv)[0].reshape(NB, 2, FT, P).transpose(3, 2, 0, 1)),
        gains=np.ascontiguousarray(np.stack([vec(a(g).reshape(-1)) for g in (
            norm_mix_g, g_mnorm, g_gnorm, norm_ffn_g, norm_ple_g, final_norm_g)], axis=1)),
        convw=np.ascontiguousarray(a(conv_w)[0].reshape(3, FT, P).transpose(2, 0, 1)),
        convb=vec(a(conv_b)[0]), blr=vec(a(b_lr2)[0]),
        bgate=np.ascontiguousarray(np.stack([a(b_mi)[0], a(b_mf)[0]], axis=1)),
        wlr=np.ascontiguousarray(a(w_lr2)[0]),
        w_misc=misc_cols.reshape(P, KT * P),
        w_in=pack(main, 2 * P), w_pa=pack(a(w_pa)[0], 2 * P), w_pb=pack(a(w_pb)[0], 2 * P),
        w_o=pack(a(w_o)[0], 2 * P), w_up=pack(up, 2 * P), w_down=pack(a(w_down)[0], P),
        w_pproj=pack(a(w_ple_proj)[0], D), w_pgate=pack(a(w_ple_gate)[0], 2 * P),
    )
    arrays.update(constants())

    nc = bacc.Bacc("TRN2", target_bir_lowering=False, num_devices=1)
    ins = {n: nc.dram_tensor(f"in_{n}", x.shape, mybir.dt.from_np(x.dtype), kind="ExternalInput").ap()
           for n, x in arrays.items()}
    shapes = dict(yT=(P, KT, T), C_p=(P, H, DV), S_p=(P, H, DV), n=(P, H, NB + 1), m=(H, NB + 1),
                  conv=(P, FT, 2 + 2 * NB), C_s=(H, P, NB, DV), S_s=(H, P, NB, DV))
    outs = {n: nc.dram_tensor(f"out_{n}", s, F32, kind="ExternalOutput").ap() for n, s in shapes.items()}
    build(nc, ins, outs)
    r = run(nc, [{f"in_{n}": x for n, x in arrays.items()}], core_ids=[0]).results[0]
    g = {n: a(r[f"out_{n}"]) for n in shapes}

    y = g["yT"].transpose(2, 1, 0).reshape(T, D)
    n, m, conv = g["n"], g["m"], g["conv"]
    cv = conv.transpose(2, 1, 0).reshape(2 + 2 * NB, FF)
    c = np.ascontiguousarray
    return (c(y[:TP]).reshape(1, TP, D), c(y[TP:]).reshape(NB, LS, D),
            c(g["C_p"].transpose(1, 0, 2))[None, None], c(n[:, :, NB].T)[None, None], c(m[:, NB])[None, None],
            c(g["S_p"].transpose(1, 0, 2))[None, None], c(cv[:2])[None, None],
            c(g["C_s"].transpose(2, 0, 1, 3))[None], c(n[:, :, :NB].transpose(2, 1, 0))[None],
            c(m[:, :NB].T)[None], c(g["S_s"].transpose(2, 0, 1, 3))[None],
            c(cv[2:].reshape(NB, 2, FF))[None])
```

```python
from contextlib import ExitStack

import numpy as np
import concourse.bass as bass
from concourse import mybir

F32 = mybir.dt.float32
F32R = mybir.dt.float32r
I8 = mybir.dt.int8
ALU = mybir.AluOpType
ACT = mybir.ActivationFunctionType

P = 128
D = 1024
KT = D // P
TP, NB, LS = 512, 8, 8
TS = NB * LS
T = TP + TS
HALF = T // 2
H = 4
DK, DV = 128, 256
L = 128
NC = TP // L
FF = 2688
FT = FF // P
PLE = 256
PK = PLE // P
RANK = 16
TAU = 16.0
EPS = 1e-6
NY_POOL = 3
NGT = 4
V_BY_VECTOR = {"mv": (1, 3), "gv": (0, 1, 3)}
UW = 2048
NORM_MIX, NORM_M, NORM_G, NORM_FFN, NORM_PLE, NORM_OUT = range(6)
PROMPT_LEVELS = [64, 32, 16, 8, 4, 2, 1]
SAMPLE_LEVELS = [4, 2, 1]
ZMO, ZGG, ZGA, ZGB = 0, 8, 16, 24


def chunk_span(c):
    return (c * L, L) if c < NC else (TP, TS)


def plan():
    units = [("misc", 0)]
    units += [("mq", i) for i in range(2)] + [("mk", i) for i in range(2)] + [("mv", i) for i in range(4)]
    units += [("gq", i) for i in range(2)] + [("gk", i) for i in range(2)] + [("gv", i) for i in range(4)]
    units += [(n, i) for n in ("mo", "gg", "ga", "gb") for i in range(4)]
    units += [(n, i) for n in ("pa", "pb", "wo") for i in range(4)]
    units += [("up", i) for i in range(FT)] + [("down", i) for i in range(2 * KT)]
    units += [("pproj", 0)] + [("pgate", i) for i in range(6)]
    at = {x: n for n, x in enumerate(units)}
    sched = [("norm_in",)]

    def unit(kind, i, after=None, before=()):
        u = at[(kind, i)]
        sched.append(("unit", u))
        sched.extend(before)
        for n in range(2 if kind == "pgate" else len(tiles_of(kind, i))):
            sched.append(("tile", u, n))
            sched.extend((after or {}).get(n, ()))

    def units_of(kind, n, after):
        for i in range(n):
            unit(kind, i, {0: after.get(2 * i, ()), 1: after.get(2 * i + 1, ())})

    unit("misc", 0, before=(("rsum", 0), ("rspread", 0)))
    units_of("mq", 2, {0: [("rows", 0)], 1: [("rows", 1)]})
    units_of("mk", 2, {0: [("rows", 2)], 2: [("rows", 3)]})
    for i in range(4):
        unit("mv", i, {2: [("m1", 0)]} if i == 3 else None)
    units_of("gq", 2, {n: [("m2", n), ("m1", n + 1), *([("tnorm", "m", n - 1)] if n else [])] for n in range(NC)})
    units_of("gk", 2, {0: [("hpre", "m", 0)], 1: [("head", "m", 0)],
                       2: [("hpre", "m", 1)], 3: [("head", "m", 1)]})
    unit("gv", 0, {1: [("hpre", "m", 2)], 3: [("head", "m", 2)], 4: [("la", 0)]})
    unit("gv", 1, {1: [("la_scan", 0), ("hpre", "m", 3)], 3: [("head", "m", 3)], 4: [("la", 1)]})
    unit("gv", 2, {1: [("la_scan", 1)], 2: [("la", 2)], 4: [("la_scan", 2)]})
    unit("gv", 3, {0: [("la", 3)], 2: [("la_scan", 3)], 4: [("gpre", 0), ("lpre", 0, 0)]})
    for c in range(NC):
        units_of_gate = {
            0: [("gkt", c), ("lev", c, 0), ("lpre", c, 1)],
            1: [("lev", c, 1), ("lpre", c, 2), ("tnorm", *(("g", c - 1) if c else ("m", 3)))],
            2: [("lev", c, 2), ("lpre", c, 3)],
            3: [("lev", c, 3), ("gout", c), ("gpre", c + 1), ("lpre", c + 1, 0)],
        }
        kind, i = ("mo", 2 * c) if c < 2 else ("gg", 2 * c - 4)
        unit(kind, i, {n: units_of_gate[n] for n in range(2)})
        unit(kind, i + 1, {n: units_of_gate[2 + n] for n in range(2)})
    units_of("ga", 4, {0: [("gkt", NC), ("lev", NC, 0), ("lpre", NC, 1), ("hpre", "g", 0)],
                       1: [("lev", NC, 1)],
                       2: [("head", "g", 0), ("tnorm", "g", NC - 1)], 3: [("hpre", "g", 1)], 4: [("head", "g", 1), ("tnorm", "m", NC)],
                       5: [("hpre", "g", 2)], 6: [("head", "g", 2)], 7: [("hpre", "g", 3)]})
    units_of("gb", 4, {0: [("head", "g", 3), ("tnorm", "g", NC)], 2: [("bt", "m", 0), ("bt", "m", 1)],
                       3: [("bt", "m", 2)], 4: [("bt", "m", 3), ("bt", "m", 4)], 5: [("bt", "m", 5)],
                       6: [("bt", "m", 6), ("bt", "m", 7)], 7: [("bt", "g", 0)]})
    units_of("pa", 4, {n: [("bt", "g", n + 1)] for n in range(7)})
    units_of("pb", 4, {})
    units_of("wo", 4, {})
    for i in range(FT):
        unit("up", i, before=(("rsum", 1), ("rspread", 1)) if i == 0 else ())
    for i in range(2 * KT):
        unit("down", i)
    unit("pproj", 0, {KT - 2: [("rsum", 2)]}, )
    out = {10: [("rsum", 3)], 12: [("rspread", 3)] + [("yout", n) for n in range(3)],
           13: [("yout", n) for n in range(3, 6)], 14: [("yout", 6), ("yout", 7)]}
    for i in range(4):
        unit("pgate", i, {n: out.get(2 * i + n, ()) for n in range(2)}, before=(("rspread", 2),) if i == 0 else ())
    for i in (2, 3):
        for n in (2, 3):
            g = 2 * i + n + 2
            sched.append(("tile", at[("pgate", i)], n))
            sched.extend(out.get(g, ()))
        if i == 2:
            sched.append(("split", at[("pgate", 4)]))
    for i in (4, 5):
        unit("pgate", i, {n: out.get(2 * i + 4 + n, ()) for n in range(2)})
    sched += [("rsum", 4), ("rspread", 4)]
    return units, sched


MID = {("misc", 0, 0): {KT: ("rsum", 0)}, ("mq", 0, 0): {5: ("rspread", 0)},
       ("up", 0, 0): {KT - 1: ("rsum", 1)}, ("up", 0, 1): {4: ("rspread", 1)},
       ("pgate", 0, 0): {KT: ("rspread", 2)}}
SPANS = [(2 * L, T), (0, 2 * L)]
PLE_ORDER = [(0, n) for n in range(KT)] + [(1, (n + 4) % KT) for n in range(KT)]


def chunks_of(n):
    return {3: (2, 3, 4), 4: (0, 1)}.get(n, tuple(range(NC + 1)))


def levels_of(c, g):
    return (PROMPT_LEVELS if c < NC else SAMPLE_LEVELS)[2 * g:2 * g + 2]


def tiles_of(kind, i):
    if kind == "misc":
        return [("misc", 0)]
    if kind in ("mv", "gv"):
        return [(kind, (i, c)) for c in range(NC + 1)]
    if kind == "up":
        return [("gate", i), ("val", i)]
    if kind == "down":
        return [("down", i // 2)] if i % 2 else []
    if kind == "pproj":
        return [("pproj", n) for n in range(KT)]
    if kind == "pgate":
        return [("pgate", g) for g in {0: (0, 1), 1: (2, 3), 2: (4, 5, 8, 9), 3: (6, 7, 10, 11),
                                       4: (12, 13), 5: (14, 15)}[i]]
    return [(kind, 2 * i), (kind, 2 * i + 1)]


def aux_jobs(stage):
    if stage[0] in ("rsum", "gkt"):
        return 1 + (stage[0] == "gkt")
    if stage[0] in ("rspread", "bt", "la"):
        return 1 if stage in (("rspread", 3), ("rspread", 4)) else 2
    if stage[0] == "rows":
        return 3 if stage[1] == 3 else 0
    if stage[0] == "m1":
        return 4
    if stage[0] in ("m2", "gout"):
        return 2 * H
    if stage[0] == "lev":
        return len(levels_of(*stage[1:]))
    if stage[0] == "head":
        return 1 + NB
    return 0


def build(nc, ins, outs):
    units, sched = plan()
    tile_at, job_at, nt, nj = {}, {}, 0, 0
    bank_of, use_of, bank0 = [], [], 0
    tiles_until = {}
    for s in sched:
        if s[0] == "unit":
            tile_at[s] = nt
        elif s[0] == "tile":
            tile_at[s] = nt
            nt += 1
            tiles_until[s[1]] = nt
        job_at[s] = nj
        n = aux_jobs(s)
        order = [bank0 + k for k in range(n)]
        if s[0] == "head":
            order = [bank0 + 1 + k % 3 for k in range(NB)] + [bank0]
        for b in order:
            bank_of.append(b % 4)
            use_of.append(bank_of.count(b % 4))
        bank0 += 3 if s[0] == "head" else n
        nj += n

    zs = nc.dram_tensor("gate_scratch", [32, P, T], F32).ap()
    hs = nc.dram_tensor("residual_scratch", [KT, P, T], F32).ap()

    with ExitStack() as ctx:
        base = 16512
        where = [base]

        def at(name, shape, dt, offset):
            return nc.alloc_sbuf_tensor_at(name, shape, dt, offset=offset)

        def put(name, shape, dt=F32):
            n = int(np.prod(shape[1:])) * (1 if dt == I8 else 4)
            t = at(name, shape, dt, where[0])
            where[0] += (n + 31) // 32 * 32
            return t

        ident = put("ident", [P, P])
        ones = put("ones", [P, P])
        cmask = put("cmask", [P, 8, P], I8)
        nmask = put("nmask", [P, 2, P])
        bmask = put("bmask", [P, NB])
        gains = put("gains", [P, 6, KT])
        convw = put("convw", [P, 3, FT])
        convb = put("convb", [P, FT])
        blr = put("blr", [P, H])
        bgate = put("bgate", [H, 2])
        m0 = put("m0", [H, NB])
        wlr = put("wlr", [RANK, H * DK])
        nst = put("nst", [P, H, NB])
        nout = put("nout", [P, H, NB + 1])
        mout = put("mout", [H, NB + 1])
        convst = put("convst", [P, FT, NB, 2])
        stat = put("stat", [P, 3, NC + 1])
        wraw = put("wraw", [P, 2, UW])
        whi = put("whi", [P, 2, UW], F32R)
        wlo = put("wlo", [P, 2, UW], F32R)
        X = where[0]
        fm = [P, KT, T]
        ahi = at("ahi", fm, F32R, X)
        alo = at("alo", fm, F32R, X + 18432)
        VM = X + 36864
        vm = at("vm", [P, NC + 1, H, DV + 1], F32, VM)
        xT = at("xT", fm, F32, VM)
        VG = VM + 20576
        vg = at("vg", [P, NC + 1, H, DV], F32, VG)
        cst = at("cst", [P, 2, H, DV + 1], F32, VG)
        cmaskf = at("cmaskf", [P, 8, P], F32, VG)
        r1 = at("r1", [H, T], F32, VG + 8224)
        ri = at("ri", [H, T], F32, VG + 8224 + 2304)
        rr = at("rr", [P, T], F32, VG + 8224 + 4608)
        sel = at("sel", [H, H, P], F32, VG + 8224 + 6912)
        QM = VG + 20480
        mq = at("mq", [P, H, T], F32, QM)
        mk = at("mk", [P, H, T], F32, QM + 9216)
        cum = at("cum", [P, H, T], F32, QM)
        stg = at("stg", [P, 2, T], F32, QM + 9216)
        xl01 = at("xl01", [P, 2, H, L], F32, QM + 9216 + 4608)
        v2 = at("v2", [P, 2, DV + 2], F32R, QM + 9216 + 4608)
        k2 = at("k2", [P, P], F32R, QM + 9216 + 4608 + 2080)
        QG = QM + 18432
        gq = at("gq", [P, H, T], F32, QG)
        gk = at("gk", [P, H, T], F32, QG + 9216)
        rowt = [at(f"rowt{i}", [H, T], F32, QG + 2304 * i) for i in range(8)]
        ROW_LI, ROW_XF, ROW_LF, ROW_B, ROW_M, ROW_D0, ROW_D1, ROW_T = range(8)
        ST = QG + 18432
        st = [at(f"st{i}", [P, NB, DV + 1], F32, ST + 8224 * i) for i in range(2)]
        gst = at("gst", [P, 2, H, DV], F32, ST + 8224)
        acc0 = at("acc0", [P, T], F32, ST)
        sq = at("sq", [P, 2, T], F32, ST + 2304)
        G0 = ST + 16448
        pw = at("pw", [P, H, L], F32, G0)
        qt = at("qt", [P, H, L], F32, G0 + 2048)
        att = at("att", [P, H, L], F32, G0 + 4096)
        ktok = at("ktok", [P, H, L], F32, G0 + 6144)
        QB = G0 + 8192
        qb = at("qb", [P, T], F32, QB)
        kb = at("kb", [P, NB, P], F32R, QB + 2304)
        kf = at("kf", [P, H, L], F32, QB + 2304)
        xl3 = at("xl3", [P, 1, H, L], F32, QB + 2304 + 2048)
        MK = QB + 6400 + 1056
        reset = at("reset", [P, T], F32, MK)
        glr = at("glr", [RANK, T], F32, MK + 2304)
        xl2 = at("xl2", [P, 1, H, L], F32, MK + 2304)
        rs = at("rs", [P, T], F32, MK + 4608)
        SM = MK + 6912
        colT = at("colT", [P, NC + 1, 3, H], F32, SM)
        carry = at("carry", [P, H, NC + NB], F32, SM + 256)
        rscol = at("rscol", [P, NC + 1], F32, SM + 448)
        nstat = at("nstat", [P, H, 6], F32, SM + 480)
        nmv = at("nmv", [P, H, 2], F32, SM + 576)
        nsm = at("nsm", [P, 6, H], F32, SM + 608)
        rowc = at("rowc", [H, 5, NC + NB], F32, SM + 704)
        assert SM + 704 + 240 <= 229368, SM + 944 - 229368
        hmhi = at("hmhi", fm, F32R, QG)
        hmlo = at("hmlo", fm, F32R, QG + 18432)
        gt = at("gt", [P, NGT, T], F32, G0 + 2048)
        sgt = at("sgt", [P, T], F32, MK)
        bt_t = at("bt_t", [P, 1, T], F32, QB + 4608)
        merged = at("merged", fm, F32, VM)
        mghi = at("mghi", fm, F32R, VG)
        mglo = at("mglo", fm, F32R, QM)
        xr = at("xr", [P, 2, T], F32, VM)
        hst = at("hst", [P, 2, T], F32, VM + 4608)
        achi = at("achi", [P, FT, T], F32R, X + 36864)
        aclo = at("aclo", [P, FT, T], F32R, X + 36864 + FT * T * 4)
        FS = X + 36864 + 2 * FT * T * 4
        GW = 2 + TP + NB * (2 + LS)
        gbuf = at("gbuf", [P, GW], F32, FS)
        cv = at("cv", [P, GW], F32, FS + 2400)
        sg = at("sg", [P, GW], F32, FS + 4800)
        vrs = at("vrs", [P, T], F32, FS + 7200)
        af = at("af", [P, T], F32, FS + 9504)
        acc = at("acc", [P, T], F32, FS + 11808)
        sq2 = at("sq2", [P, T], F32, FS + 14112)
        rsv = at("rsv", [P, T], F32, FS + 16416)
        convout = at("convout", [P, FT, 2 + 2 * NB], F32, FS + 18720)
        sqp = [sq2, af]
        h2 = at("h2", fm, F32, X)
        h3 = at("h3", fm, F32, X + 18432)
        ehi = at("ehi", fm, F32R, X + 36864)
        elo = at("elo", fm, F32R, X + 36864 + 18432)
        pj = at("pj", fm, F32, X + 36864 * 2)
        praw = at("praw", [P, PK, T], F32, X + 18432)
        phi = at("phi", [P, PK, T], F32R, X + 18432 + 4608)
        plo = at("plo", [P, PK, T], F32R, X + 18432 + 9216)
        sgp = at("sgp", [P, 2, T], F32, X + 36864 * 3)
        yt = at("yt", fm, F32, X + 36864 * 3 + 4608)

        ps = ctx.enter_context(nc.psum_tensor("ps", [P, 2, 2, 512], F32))
        aux = ctx.enter_context(nc.psum_tensor("aux", [P, 4, 512], F32))

        def sem(name):
            return ctx.enter_context(nc.semaphore(name))

        def sems(name, n):
            return [sem(f"{name}{i}") for i in range(n)]

        raw_in = sems("raw_in", 2)
        split_hi = sem("split_hi")
        split_lo = sem("split_lo")
        half_done = sem("half_done")
        tile_ready = sem("tile_ready")
        tile_free = sems("tile_free", 2)
        aux_ready = sem("aux_ready")
        aux_free = sems("aux_free", 4)
        const_in = sem("const_in")
        ident_in = sem("ident_in")
        gains_in = sem("gains_in")
        x_in = sems("x_in", 4)
        dve_step = sem("dve_step")
        act_step = sem("act_step")
        pool_step = sem("pool_step")
        init_done = sem("init_done")
        in_sq = sem("in_sq")
        in_sq_used = sem("in_sq_used")
        a_hi = sem("a_hi")
        a_lo = sem("a_lo")
        sq_sum = sem("sq_sum")
        ms_ready = sem("ms_ready")
        ms_root = sem("ms_root")
        rs_diag = sem("rs_diag")
        rs_ready = sem("rs_ready")
        row_abs = sem("row_abs")
        row_ln = sem("row_ln")
        row_pre = sem("row_pre")
        row_exp = sem("row_exp")
        rows_zero = sem("rows_zero")
        fm_ready = sem("fm_ready")
        v_ready = sem("v_ready")
        p_pre = sem("p_pre")
        p_exp = sem("p_exp")
        qt_ready = sem("qt_ready")
        kt_ready = sem("kt_ready")
        at_ready = sem("at_ready")
        c_ready = sem("c_ready")
        s_ready = sem("s_ready")
        kv_go = sem("kv_go")
        kv_hi = sem("kv_hi")
        blk_ready = sem("blk_ready")
        st_in = sems("st_in", 2)
        st_n = sem("st_n")
        st_new = sem("st_new")
        st_out = sems("st_out", 2)
        cp_out = sem("cp_out")
        out_done = sem("out_done")
        h_out = sem("h_out")
        la_abs = sem("la_abs")
        la_ln = sem("la_ln")
        cum_ready = sem("cum_ready")
        g_go = sem("g_go")
        eb_ready = sem("eb_ready")
        kd_sub = sem("kd_sub")
        kd_exp = sem("kd_exp")
        kf_ready = sem("kf_ready")
        xl_sub = sem("xl_sub")
        xl_exp = sem("xl_exp")
        xl_ready = sem("xl_ready")
        stg_full = sem("stg_full")
        stg_out = sems("stg_out", 2)
        tn_pre = sem("tn_pre")
        tn_root = sem("tn_root")
        tn_done = sem("tn_done")
        gt_in = sems("gt_in", NGT)
        gt_sig = sem("gt_sig")
        gt_used = sem("gt_used")
        silu_used = sem("silu_used")
        bt_pre = sem("bt_pre")
        bt_hi = sem("bt_hi")
        bt_lo = sem("bt_lo")
        mg_pre = sem("mg_pre")
        mg_hi = sem("mg_hi")
        mg_lo = sem("mg_lo")
        xr_in = sems("xr_in", 2)
        h_pre = sem("h_pre")
        c_hi = sem("c_hi")
        c_lo = sem("c_lo")
        hs_out = sems("hs_out", 2)
        ff_g = sem("ff_g")
        ff_cv = sem("ff_cv")
        ff_sg = sem("ff_sg")
        ff_pre = sem("ff_pre")
        ff_hi = sem("ff_hi")
        ff_lo = sem("ff_lo")
        h2_in = sem("h2_in")
        h2_new = sem("h2_new")
        p_in = sem("p_in")
        p_hi = sem("p_hi")
        p_lo = sem("p_lo")
        pj_ready = sem("pj_ready")
        e_hi = sem("e_hi")
        e_lo = sem("e_lo")
        pg_pre = sem("pg_pre")
        pg_sig = sem("pg_sig")
        h3_new = sem("h3_new")
        h3_sq = sem("h3_sq")
        sq_used = sem("sq_used")
        y_pre = sem("y_pre")
        yp_ready = sem("yp_ready")
        y_ready = sem("y_ready")
        y_out = sem("y_out")

        block = ctx.enter_context(nc.Block())

        def two(ap):
            return ap.rearrange("p (a b) -> p a b", a=2)

        def tile(t):
            return ps[:, t % 2, :, 0:HALF]

        def bcast(ap, n, where_):
            shape = list(ap.shape)
            return ap.unsqueeze(where_).broadcast_to(shape[:where_] + [n] + shape[where_:])

        def f32(ap):
            return ap.bitcast(F32)

        def head_jobs():
            return [s for s in sched if s[0] == "head"]

        head_no = {s: n for n, s in enumerate(head_jobs())}

        def out_count(q):
            return 16 * (q // 2 + 1)

        h_out_of, copied, = {}, 0
        for s in sched:
            if s[0] in ("m2", "gout"):
                copied += H
                h_out_of[(s[0][0], s[1])] = copied
            elif s[0] == "head":
                copied += 1
                h_out_of[(s[1], NC)] = copied

        def xl_buffer(c, g, n):
            return (xl01[:, 0], xl01[:, 1], xl2[:, 0], xl3[:, 0])[2 * (g % 2) + n]

        @block.sync
        def _(sp):
            sp.dma_start(gains[:, :, :], ins["gains"]).then_inc(gains_in, 16)
            for u, (kind, i) in enumerate(units):
                s = u % 2
                if u == 1:
                    sp.wait_ge(x_in[3], 16)
                if u >= 2:
                    sp.wait_ge(split_hi, u - 1)
                    sp.wait_ge(split_lo, u - 1)
                if kind == "misc":
                    sp.dma_start(wraw[:, 0, 0:KT * P], ins["w_misc"]).then_inc(raw_in[0], 16)
                else:
                    src = {"pa": "w_pa", "pb": "w_pb", "wo": "w_o", "up": "w_up", "pproj": "w_pproj",
                           "pgate": "w_pgate", "down": "w_down"}.get(kind, "w_in")
                    if src == "w_in":
                        row = {"mq": 0, "mk": 2, "mv": 4, "gq": 8, "gk": 10, "gv": 12,
                               "mo": 16, "gg": 20, "ga": 24, "gb": 28}[kind] + i
                        sp.dma_start(wraw[:, s, :], ins["w_in"][row, :, :]).then_inc(raw_in[s], 16)
                        if u == 1:
                            sp.dma_start(ident[:, :], ins["ident"]).then_inc(ident_in, 16)
                            for n, dst in (("cmask", cmaskf[:, :, :]), ("nmask", nmask[:, :, :]),
                                           ("sel", sel[:, :, :]), ("bmask", bmask[:, :]), ("convw", convw[:, :, :]),
                                           ("convb", convb[:, :]), ("blr", blr[:, :]), ("bgate", bgate[:, :]),
                                           ("m0", m0[:, :]), ("wlr", wlr[:, :]), ("nst", nst[:, :, :]),
                                           ("convst", convst[:, :, :, :])):
                                sp.dma_start(dst, ins[n]).then_inc(const_in, 16)
                    elif kind == "down":
                        a, b = (0, 11 * P) if i % 2 == 0 else (11 * P, FF)
                        sp.dma_start(wraw[:, s, 0:b - a], ins["w_down"][i // 2, :, a:b]).then_inc(raw_in[s], 16)
                    else:
                        sp.dma_start(wraw[:, s, :], ins[src][i % 4 if kind == "pgate" else i, :, :]).then_inc(raw_in[s], 16)

            for g, (a, n) in enumerate(PLE_ORDER[:KT + NY_POOL]):
                sp.wait_ge(yp_ready if a else y_ready, g - a * KT + 1)
                lo, hi = SPANS[a]
                sp.dma_start(outs["yT"][:, n, lo:hi], yt[:, n, lo:hi]).then_inc(y_out, 16)

        NCONST = 12 * 16

        def raw_count(u):
            return 16 * (u // 2 + 1)

        def width(u):
            kind, i = units[u]
            if kind == "misc":
                return KT * P
            if kind == "down":
                return 11 * P if i % 2 == 0 else 10 * P
            return UW

        def used(eng, u):
            kind, i = units[u]
            if kind == "down" and i % 2 == 0:
                eng.wait_ge(half_done, i // 2 + 1)
            else:
                eng.wait_ge(tile_ready, tiles_until[u])

        @block.gpsimd
        def _(pool):
            for u in range(len(units)):
                s, n = u % 2, width(u)
                pool.wait_ge(raw_in[s], raw_count(u))
                pool.wait_ge(split_hi, u + 1)
                if u >= 2:
                    used(pool, u - 2)
                nc.gpsimd.tensor_tensor(wlo[:, s, 0:n], wraw[:, s, 0:n], f32(whi[:, s, 0:n]), ALU.subtract)\
                    .then_inc(split_lo, 1)
            pool.wait_ge(rs_ready, 5)
            lo, hi = SPANS[1]
            for k, (_, n) in enumerate(PLE_ORDER[KT:KT + NY_POOL]):
                pool.wait_ge(y_pre, k + 1)
                nc.gpsimd.tensor_tensor(yt[:, n, lo:hi], yt[:, n, lo:hi], rsv[:, lo:hi], ALU.mult)\
                    .then_inc(yp_ready, 1)

        @block.tensor
        def _(pe):
            def bank(j):
                if use_of[j] > 1:
                    pe.wait_ge(aux_free[bank_of[j]], use_of[j] - 1)
                return aux[:, bank_of[j], :]

            def slot(t):
                if t >= 2:
                    pe.wait_ge(tile_free[t % 2], t // 2)

            def rsum(n):
                pe.wait_ge(sq_sum, n + 1)
                src, b = acc if n else acc0, bank(job_at[("rsum", n)])
                for c in chunks_of(n):
                    t0, ln = chunk_span(c)
                    mm = nc.tensor.matmul(b[0:ln, c:c + 1], src[:, t0:t0 + ln], ones[:, 0:1], start=True, stop=True)
                mm.then_inc(aux_ready, 1)

            def rspread(n):
                pe.wait_ge(rs_diag, n + 1)
                j, d = job_at[("rspread", n)], vrs if n else sq[:, 1]
                if n >= 3:
                    b, (lo, hi) = bank(j), SPANS[n - 3]
                    full = min(hi, TP)
                    mm = nc.tensor.matmul(b[:, 0:full - lo], ones[:, :], d[:, lo:full], start=True, stop=True)
                    if hi > TP:
                        mm = nc.tensor.matmul(b[:, TP - lo:hi - lo], ones[0:TS, :], d[0:TS, TP:], start=True, stop=True)
                    mm.then_inc(aux_ready, 1)
                    return
                nc.tensor.matmul(bank(j), ones[:, :], d[:, 0:TP], start=True, stop=True).then_inc(aux_ready, 1)
                nc.tensor.matmul(bank(j + 1)[:, 0:TS], ones[0:TS, :], d[0:TS, TP:], start=True, stop=True)\
                    .then_inc(aux_ready, 1)

            def mid_stage(s):
                (rsum if s[0] == "rsum" else rspread)(s[1])

            def product(t, blocks, hi, lo, s, start=True, stop=True, ready=None, mid={}, low_part=None):
                for n, (col, k) in enumerate(blocks):
                    if n in mid:
                        mid_stage(mid[n])
                    if ready:
                        for q, before in ready:
                            pe.wait_ge(q, before + k + 1)
                    first, last = start and n == 0, stop and n == len(blocks) - 1
                    wh, wl = whi[:, s, col:col + P], wlo[:, s, col:col + P]
                    for x, w, f, e in ((hi, wh, first, False), (lo, wh, False, False), (hi, wl, False, last)):
                        if w is wl and low_part:
                            continue
                        for a in range(2):
                            mm = nc.tensor.matmul(ps[:, t % 2, a, 0:HALF], w, x[:, k, a * HALF:(a + 1) * HALF],
                                                  start=f, stop=e)
                if low_part:
                    pe.wait_ge(split_lo, low_part)
                    for n, (col, k) in enumerate(blocks):
                        for a in range(2):
                            mm = nc.tensor.matmul(ps[:, t % 2, a, 0:HALF], wlo[:, s, col:col + P],
                                                  hi[:, k, a * HALF:(a + 1) * HALF],
                                                  start=False, stop=n == len(blocks) - 1)
                if stop:
                    mm.then_inc(tile_ready, 1)
                if len(blocks) in mid:
                    mid_stage(mid[len(blocks)])
                return mm

            def span_product(t, place, s, low_part, ready=None, mid={}):
                (lo, hi), m = SPANS[place[0]], place[1] % 2
                out = ps[:, t % 2, 0, 0:hi - lo]
                if low_part is None:
                    for k in range(KT):
                        for q, before in ready or ():
                            pe.wait_ge(q, before + k + 1)
                        col = (2 * k + m) * P
                        wh, wl = whi[:, s, col:col + P], wlo[:, s, col:col + P]
                        for x, w, f, e in ((ehi, wh, k == 0, False), (elo, wh, False, False),
                                           (ehi, wl, False, k == KT - 1)):
                            mm = nc.tensor.matmul(out, w, x[:, k, lo:hi], start=f, stop=e)
                else:
                    for k in range(KT):
                        col = (2 * k + m) * P
                        nc.tensor.matmul(out, whi[:, s, col:col + P], ehi[:, k, lo:hi], start=k == 0, stop=False)
                        nc.tensor.matmul(out, whi[:, s, col:col + P], elo[:, k, lo:hi], start=False, stop=False)
                    pe.wait_ge(split_lo, low_part)
                    for k in range(KT):
                        col = (2 * k + m) * P
                        mm = nc.tensor.matmul(out, wlo[:, s, col:col + P], ehi[:, k, lo:hi],
                                              start=False, stop=k == KT - 1)
                mm.then_inc(tile_ready, 1)
                if KT in mid:
                    mid_stage(mid[KT])

            counts = {"lv": 0}
            for s in sched:
                j, t = job_at[s], tile_at.get(s)
                if s[0] == "unit":
                    u = s[1]
                    kind, i = units[u]
                    pe.wait_ge(split_hi, u + 1)
                    if kind in ("misc", "down"):
                        pe.wait_ge(split_lo, u + 1)
                    if kind == "down" and i % 2 == 0:
                        slot(t)
                        product(t, [(b * P, b) for b in range(11)], achi, aclo, u % 2, stop=False,
                                ready=((ff_hi, 0), (ff_lo, 0)) if i == 0 else None).then_inc(half_done, 1)
                elif s[0] == "tile":
                    u, n = s[1:]
                    kind, i = units[u]
                    w = u % 2
                    mid = MID.get((kind, i, n), {})
                    if kind != "down":
                        slot(t)
                    if kind == "misc":
                        product(t, [(k * P, k) for k in range(KT)], ahi, alo, w, ready=((a_hi, 0), (a_lo, 0)), mid=mid)
                    elif kind in ("mv", "gv"):
                        t0, ln = chunk_span(n)
                        out = ps[0:ln, t % 2, 0, 0:DV]
                        for k in range(KT):
                            wh = whi[:, w, k * DV:(k + 1) * DV]
                            nc.tensor.matmul(out, ahi[:, k, t0:t0 + ln], wh, start=k == 0, stop=False)
                            nc.tensor.matmul(out, alo[:, k, t0:t0 + ln], wh, start=False, stop=False)
                        if n == 0:
                            pe.wait_ge(split_lo, u + 1)
                        for k in range(KT):
                            mm = nc.tensor.matmul(out, ahi[:, k, t0:t0 + ln], wlo[:, w, k * DV:(k + 1) * DV],
                                                  start=False, stop=k == KT - 1)
                        mm.then_inc(tile_ready, 1)
                    elif kind == "down":
                        product(t, [(b * P, 11 + b) for b in range(10)], achi, aclo, w, start=False,
                                ready=((ff_hi, 0), (ff_lo, 0)) if i == 1 else None)
                    elif kind == "pproj":
                        pe.wait_ge(p_hi, PK)
                        pe.wait_ge(p_lo, PK)
                        product(t, [(k * D + n * P, k) for k in range(PK)], phi, plo, w,
                                low_part=u + 1 if n == 0 else None)
                    elif kind == "pgate":
                        low = u + 1 if n == 0 and i > 0 else None
                        if i == 0 and n == 0:
                            pe.wait_ge(split_lo, u + 1)
                        span_product(t, PLE_ORDER[tiles_of(kind, i)[n][1]], w, low, ((e_hi, 0), (e_lo, 0)) if (i, n) == (0, 0) else None, mid)
                    else:
                        hi, lo, ready = {
                            "pa": (hmhi, hmlo, ((bt_hi, 0), (bt_lo, 0))), "pb": (ahi, alo, ((bt_hi, KT), (bt_lo, KT))), "wo": (mghi, mglo, ((mg_hi, 0), (mg_lo, 0))),
                            "up": (ahi, alo, ((c_hi, 0), (c_lo, 0))), 
                        }.get(kind, (ahi, alo, None))
                        if i > 0 or n > 0:
                            ready = None
                        if ready:
                            pe.wait_ge(split_lo, u + 1)
                        product(t, [(k * 2 * P + n * P, k) for k in range(KT)], hi, lo, w, ready=ready, mid=mid,
                                low_part=u + 1 if n == 0 and not ready else None)
                elif s[0] == "bt":
                    which, n = s[1], s[2]
                    v = vm if which == "m" else vg
                    pe.wait_ge(tn_done, 2 * (NC + 1))
                    hd, c0 = n // 2, (n % 2) * P
                    b = bank(j)
                    for c in range(NC):
                        mm = nc.tensor.transpose(b[:, c * L:(c + 1) * L], v[:, c, hd, c0:c0 + P], ident[:, :])
                    mm.then_inc(aux_ready, 1)
                    nc.tensor.transpose(bank(j + 1)[:, 0:TS], v[0:TS, NC, hd, c0:c0 + P], ident[0:TS, 0:TS])\
                        .then_inc(aux_ready, 1)
                elif s[0] == "rsum" and s[1] >= 2:
                    rsum(s[1])
                elif s[0] == "rspread" and s[1] >= 3:
                    rspread(s[1])
                elif s[0] == "rows" and s[1] == 3:
                    pe.wait_ge(row_exp, 4)
                    pe.wait_ge(const_in, NCONST)
                    b = bank(j)
                    for c in range(NC):
                        mm = nc.tensor.transpose(b[:, c * P:(c + 1) * P], rr[:, c * L:(c + 1) * L], ident[:, :])
                    mm.then_inc(aux_ready, 1)
                    b = bank(j + 1)
                    nc.tensor.transpose(b[0:TS, 0:P], rr[:, TP:T], ident[:, :]).then_inc(aux_ready, 1)
                    b = bank(j + 2)
                    n = NC + NB
                    for h in range(H):
                        mm = nc.tensor.matmul(b[:, h * n:(h + 1) * n], sel[:, h, :], rowc[:, 4, :],
                                              start=True, stop=True)
                    mm.then_inc(aux_ready, 1)
                elif s[0] == "m1":
                    c = s[1]
                    t0, ln = chunk_span(c)
                    b = bank(j)
                    for h in range(H):
                        mm = nc.tensor.matmul(b[:, h * ln:(h + 1) * ln], sel[:, h, :], r1[:, t0:t0 + ln],
                                              start=True, stop=True)
                    mm.then_inc(aux_ready, 1)
                    b = bank(j + 1)
                    for h in range(H):
                        mm = nc.tensor.matmul(b[:, h * ln:(h + 1) * ln], sel[:, h, :], ri[:, t0:t0 + ln],
                                              start=True, stop=True)
                    mm.then_inc(aux_ready, 1)
                    if c == 0:
                        pe.wait_ge(fm_ready, 2 * H)
                    b = bank(j + 2)
                    for h in range(H):
                        mm = nc.tensor.transpose(b[0:ln, h * P:(h + 1) * P], mk[:, h, t0:t0 + ln], ident[:, :])
                    mm.then_inc(aux_ready, 1)
                    b = bank(j + 3)
                    for h in range(H):
                        mm = nc.tensor.matmul(b[0:ln, h * ln:(h + 1) * ln], mk[:, h, t0:t0 + ln],
                                              mq[:, h, t0:t0 + ln], start=True, stop=True)
                    mm.then_inc(aux_ready, 1)
                elif s[0] == "m2":
                    c = s[1]
                    if c == 0:
                        pe.wait_ge(v_ready, H * (NC + 1))
                    pe.wait_ge(kt_ready, c + 1)
                    for h in range(H):
                        b = bank(j + h)
                        nc.tensor.matmul(b[:, 0:DV + 1], ktok[:, h, :], vm[:, c, h, :], start=True, stop=True)\
                            .then_inc(aux_ready, 1)
                    pe.wait_ge(at_ready, c + 1)
                    pe.wait_ge(qt_ready, c + 1)
                    for h in range(H):
                        b = bank(j + H + h)
                        mm = nc.tensor.matmul(b[:, 0:DV + 1], att[:, h, :], vm[:, c, h, :],
                                              start=True, stop=c == 0)
                        if c:
                            pe.wait_ge(c_ready, H * (c - 1) + h + 1)
                            mm = nc.tensor.matmul(b[:, 0:DV + 1], qt[:, h, :], cst[:, c % 2, h, :],
                                                  start=False, stop=True)
                        mm.then_inc(aux_ready, 1)
                elif s[0] == "head":
                    which, h = s[1], s[2]
                    q = head_no[s]
                    v, wd = (vm, DV + 1) if which == "m" else (vg, DV)
                    pe.wait_ge(at_ready, (NC + 1) * (1 + (which == "g")))
                    pe.wait_ge(blk_ready, q + 1)
                    pe.wait_ge(st_in[q % 2], 16 * (q // 2 + 1))
                    if which == "m":
                        pe.wait_ge(st_n, h + 1)
                    else:
                        pe.wait_ge(v_ready, 2 * H * (NC + 1))
                    even = wd + wd % 2
                    out = bank(j + NB)
                    nc.tensor.matmul(out[0:TS, 0:wd], att[0:TS, h, 0:TS], v[0:TS, NC, h, 0:wd], start=True, stop=False)
                    for n in range(NB):
                        nc.tensor.matmul(out[0:TS, 0:wd], qb[:, n * TS:(n + 1) * TS], st[q % 2][:, n, 0:wd],
                                         start=False, stop=n == NB - 1)
                        b = bank(j + n)
                        nc.tensor.matmul(b[:, 0:even], kb[:, n, :], v2[:, 0, 0:even], start=True, stop=False)
                        nc.tensor.matmul(b[:, 0:even], kb[:, n, :], v2[:, 1, 0:even], start=False, stop=True)\
                            .then_inc(aux_ready, 2 if n == NB - 1 else 1)
                elif s[0] == "la":
                    h = s[1]
                    for a in range(2):
                        nc.tensor.matmul(bank(j + a)[:, 0:HALF], wlr[:, h * DK:(h + 1) * DK],
                                         glr[:, a * HALF:(a + 1) * HALF], start=True, stop=True)\
                            .then_inc(aux_ready, 1)
                elif s[0] == "gkt":
                    c = s[1]
                    t0, ln = chunk_span(c)
                    if c == 0:
                        pe.wait_ge(fm_ready, 4 * H)
                    b = bank(j)
                    for h in range(H):
                        mm = nc.tensor.matmul(b[0:ln, h * ln:(h + 1) * ln], gk[:, h, t0:t0 + ln],
                                              gq[:, h, t0:t0 + ln], start=True, stop=True)
                    mm.then_inc(aux_ready, 1)
                    pe.wait_ge(kf_ready, c + 1)
                    b = bank(j + 1)
                    for h in range(H):
                        mm = nc.tensor.transpose(b[0:ln, h * P:(h + 1) * P], kf[:, h, 0:ln], ident[:, :])
                    mm.then_inc(aux_ready, 1)
                elif s[0] == "lev":
                    c, g = s[1:]
                    ln = chunk_span(c)[1]
                    for n, w in enumerate(levels_of(c, g)):
                        counts["lv"] += 1
                        pe.wait_ge(xl_ready, counts["lv"])
                        xl = xl_buffer(c, g, n)
                        b = bank(j + n)
                        for h in range(H):
                            late = xl[:, h, 0:ln].rearrange("p (b s) -> p b s", s=2 * w)[:, :, w:]
                            mm = nc.tensor.matmul(b[0:ln, h * ln // 2:(h + 1) * ln // 2]
                                                  .rearrange("p (b s) -> p b s", s=w),
                                                  xl[:, h, 0:ln], late, start=True, stop=True)
                        mm.then_inc(aux_ready, 1)
                elif s[0] == "gout":
                    c = s[1]
                    if c == 0:
                        pe.wait_ge(v_ready, 2 * H * (NC + 1))
                    pe.wait_ge(kt_ready, NC + 1 + c + 1)
                    for h in range(H):
                        b = bank(j + h)
                        nc.tensor.matmul(b[:, 0:DV], ktok[:, h, :], vg[:, c, h, :], start=True, stop=True)\
                            .then_inc(aux_ready, 1)
                    pe.wait_ge(at_ready, NC + 1 + c + 1)
                    pe.wait_ge(qt_ready, NC + 1 + c + 1)
                    for h in range(H):
                        b = bank(j + H + h)
                        mm = nc.tensor.matmul(b[:, 0:DV], att[:, h, :], vg[:, c, h, :], start=True, stop=c == 0)
                        if c:
                            pe.wait_ge(s_ready, H * (c - 1) + h + 1)
                            mm = nc.tensor.matmul(b[:, 0:DV], qt[:, h, :], gst[:, c % 2, h, :],
                                                  start=False, stop=True)
                        mm.then_inc(aux_ready, 1)

        @block.vector
        def _(dve):
            V = nc.vector
            n_step = [0]

            def link(ins):
                n_step[0] += 1
                ins.then_inc(dve_step, 1)
                dve.wait_ge(dve_step, n_step[0])

            def job(j):
                dve.wait_ge(aux_ready, j + 1)
                return aux[:, bank_of[j], :]

            def free(ins, j):
                ins.then_inc(aux_free[bank_of[j]], 1)

            V.memset(ones[:, :], 1.0)
            V.memset(reset[:, :], 1.0)
            V.memset(qb[:, :], 0.0)
            V.memset(stat[:, :, :], 1.0)
            V.memset(rscol[:, :], 1.0)
            link(V.memset(rowc[:, :, :], 0.0))
            V.memset(reset[:, 0:TP:L], 0.0)
            V.memset(reset[:, TP:T:LS], 0.0).then_inc(init_done, 1)
            dve.wait_ge(init_done, 1)

            lv = 0
            ng = {"gt": 0, "stg": 0, "tn": 0}

            def rsum(n, j):
                ms, y, t = stat[:, 0, :], rscol[:, :] if n == 0 else stat[:, 1, :], stat[:, 2, :]
                b = job(j)
                c0, c1 = chunks_of(n)[0], min(chunks_of(n)[-1] + 1, NC)
                i = V.tensor_scalar(ms[:, c0:c1], b[:, c0:c1], 1.0 / D, EPS, ALU.mult, ALU.add)
                if NC in chunks_of(n):
                    i = V.tensor_scalar(ms[0:TS, NC:], b[0:TS, NC:NC + 1], 1.0 / D, EPS, ALU.mult, ALU.add)
                free(i, j)
                dve.wait_ge(aux_free[bank_of[j]], use_of[j])
                dve.sem_inc(ms_ready, 1)
                dve.wait_ge(ms_root, n + 1)
                link(V.reciprocal(y, y))
                link(V.scalar_tensor_tensor(t, y, -0.5, y, ALU.mult, ALU.mult))
                link(V.tensor_tensor(t, t, ms, ALU.mult))
                link(V.scalar_tensor_tensor(y, t, 1.5, y, ALU.add, ALU.mult))
                if n == 0:
                    dve.wait_ge(ident_in, 16)
                d = vrs if n else sq[:, 1]
                i = V.tensor_tensor(d[:, c0 * P:c1 * P].rearrange("p (c s) -> p c s", s=P),
                                    bcast(ident[:, :], c1 - c0, 1), bcast(y[:, c0:c1], P, 2), ALU.mult)
                if NC in chunks_of(n):
                    i = V.tensor_scalar(d[0:TS, TP:], ident[0:TS, 0:TS], y[0:TS, NC:NC + 1], None, ALU.mult)
                i.then_inc(rs_diag, 1)

            def rspread(n, j):
                out = rsv if n else rs
                if n >= 3:
                    lo, hi = SPANS[n - 3]
                    free(V.tensor_copy(out[:, lo:hi], job(j)[:, 0:hi - lo]), j)
                    dve.wait_ge(aux_free[bank_of[j]], use_of[j])
                    dve.sem_inc(rs_ready, 1)
                    return
                free(V.tensor_copy(out[:, 0:TP], job(j)), j)
                i = V.tensor_copy(out[:, TP:], job(j + 1)[:, 0:TS])
                free(i, j + 1)
                for a in range(2):
                    dve.wait_ge(aux_free[bank_of[j + a]], use_of[j + a])
                dve.sem_inc(rs_ready, 1)

            def split_lo_of(dst, src, hi, done):
                V.tensor_tensor(dst, src, f32(hi), ALU.subtract).then_inc(done, 1)

            def add_square(n, x):
                if n == 0:
                    link(V.tensor_tensor(acc[:, :], x, x, ALU.mult))
                else:
                    link(V.tensor_tensor(sq2[:, :], x, x, ALU.mult))
                    i = V.tensor_tensor(acc[:, :], acc[:, :], sq2[:, :], ALU.add)
                    if n == KT - 1:
                        i.then_inc(sq_sum, 1)
                    else:
                        link(i)

            def evac(kind, i, t):
                dve.wait_ge(tile_ready, t + 1)
                full, fr = tile(t), tile_free[t % 2]
                if kind == "misc":
                    p = ps[:, t % 2, :, 0:HALF]
                    V.tensor_tensor(two(rowt[ROW_LI][:, :]), p[0:H], two(rs[0:H, :]), ALU.mult)
                    V.tensor_copy(two(rowt[ROW_XF][:, :]), p[32:32 + H])
                    V.tensor_copy(two(glr[:, :]), p[64:64 + RANK]).then_inc(fr, 1)
                    dve.wait_ge(fr, t // 2 + 1)
                    V.tensor_tensor(rowt[ROW_XF][:, :], rowt[ROW_XF][:, :], rs[0:H, :], ALU.mult)
                    link(V.tensor_tensor(glr[:, :], glr[:, :], rs[0:RANK, :], ALU.mult))
                elif kind in ("mq", "mk", "gq", "gk"):
                    dst = {"mq": mq, "mk": mk, "gq": gq, "gk": gk}[kind][:, i, :]
                    c = DK ** -0.5 if kind in ("mk", "gq") else 1.0
                    ins_ = V.scalar_tensor_tensor(two(dst), full, c, two(rs[:, :]), ALU.mult, ALU.mult)
                    ins_.then_inc(fr, 1)
                    dve.wait_ge(fr, t // 2 + 1)
                    dve.sem_inc(fm_ready, 1)
                elif kind in ("mo", "gg", "ga", "gb"):
                    k = ng["stg"]
                    ng["stg"] += 1
                    if k >= 2:
                        dve.wait_ge(stg_out[k % 2], 16 * (k // 2))
                    V.tensor_tensor(two(stg[:, k % 2, :]), full, two(rs[:, :]), ALU.mult).then_inc(fr, 1)
                elif kind == "pa":
                    g = gt_take()
                    V.tensor_tensor(two(merged[:, i, :]), full, two(gt[:, g % NGT, :]), ALU.mult).then_inc(fr, 1)
                    dve.wait_ge(fr, t // 2 + 1)
                    dve.sem_inc(gt_used, 1)
                elif kind == "pb":
                    if i == 0:
                        for k in range(2):
                            dve.wait_ge(stg_out[k], 16 * 16)
                    g = gt_take()
                    V.tensor_tensor(two(gt[:, g % NGT, :]), full, two(gt[:, g % NGT, :]), ALU.mult).then_inc(fr, 1)
                    dve.wait_ge(fr, t // 2 + 1)
                    link(V.tensor_tensor(merged[:, i, :], merged[:, i, :], gt[:, g % NGT, :], ALU.add))
                    dve.sem_inc(gt_used, 1)
                    dve.sem_inc(mg_pre, 1)
                    dve.wait_ge(mg_hi, i + 1)
                    split_lo_of(mglo[:, i, :], merged[:, i, :], mghi[:, i, :], mg_lo)
                elif kind == "wo":
                    dve.wait_ge(xr_in[i % 2], 16 * (i // 2 + 1))
                    if i >= 2:
                        dve.wait_ge(hs_out[i % 2], 16 * (i // 2))
                    x = hst[:, i % 2, :]
                    V.tensor_tensor(two(x), full, two(xr[:, i % 2, :]), ALU.add).then_inc(fr, 1)
                    dve.wait_ge(fr, t // 2 + 1)
                    dve.sem_inc(h_pre, 1)
                    add_square(i, x)
                    dve.wait_ge(c_hi, i + 1)
                    V.scalar_tensor_tensor(alo[:, i, :], x, gains[:, NORM_FFN, i:i + 1], f32(ahi[:, i, :]),
                                           ALU.mult, ALU.subtract).then_inc(c_lo, 1)
                elif kind == "gate":
                    if i >= 1:
                        dve.wait_ge(ff_g, 2 * i)
                    p0, p1 = ps[:, t % 2, 0, :], ps[:, t % 2, 1, :]
                    n1 = TP - HALF
                    tail = gbuf[:, 2 + TP:].rearrange("p (b s) -> p b s", s=2 + LS)
                    if i == 0:
                        V.memset(gbuf[:, 0:2], 0.0)
                    V.tensor_copy(tail[:, :, 0:2], convst[:, i, :, :])
                    V.tensor_tensor(gbuf[:, 2:2 + HALF], p0[:, 0:HALF], rsv[:, 0:HALF], ALU.mult)
                    V.tensor_tensor(gbuf[:, 2 + HALF:2 + TP], p1[:, 0:n1], rsv[:, HALF:TP], ALU.mult)
                    V.tensor_tensor(tail[:, :, 2:], p1[:, n1:HALF].rearrange("p (b s) -> p b s", s=LS),
                                    rsv[:, TP:].rearrange("p (b s) -> p b s", s=LS), ALU.mult).then_inc(fr, 1)
                    dve.wait_ge(fr, t // 2 + 1)
                    dve.sem_inc(ff_g, 1)
                    n = GW - 2
                    c = cv[:, 2:]
                    link(V.tensor_scalar(c, gbuf[:, 2:], convw[:, 2, i:i + 1], convb[:, i:i + 1], ALU.mult, ALU.add))
                    link(V.scalar_tensor_tensor(c, gbuf[:, 1:1 + n], convw[:, 1, i:i + 1], c, ALU.mult, ALU.add))
                    V.scalar_tensor_tensor(c, gbuf[:, 0:n], convw[:, 0, i:i + 1], c, ALU.mult, ALU.add)\
                        .then_inc(ff_cv, 1)
                elif kind == "val":
                    V.tensor_tensor(two(vrs[:, :]), full, two(rsv[:, :]), ALU.mult).then_inc(fr, 1)
                    dve.wait_ge(ff_sg, i + 1)
                    link(V.tensor_tensor(cv[:, 2:], cv[:, 2:], sg[:, 2:], ALU.mult))
                    dve.wait_ge(fr, t // 2 + 1)
                    tail = cv[:, 2 + TP:].rearrange("p (b s) -> p b s", s=2 + LS)
                    V.tensor_tensor(af[:, 0:TP], cv[:, 2:2 + TP], vrs[:, 0:TP], ALU.mult)
                    V.tensor_tensor(af[:, TP:].rearrange("p (b s) -> p b s", s=LS), tail[:, :, 2:],
                                    vrs[:, TP:].rearrange("p (b s) -> p b s", s=LS), ALU.mult).then_inc(ff_pre, 1)
                    dve.wait_ge(ff_hi, i + 1)
                    split_lo_of(aclo[:, i, :], af[:, :], achi[:, i, :], ff_lo)
                    dve.wait_ge(ff_lo, i + 1)
                elif kind == "down":
                    if i == 0:
                        dve.wait_ge(p_hi, PK)
                        V.tensor_tensor(plo[:, :, :], praw[:, :, :], f32(phi[:, :, :]), ALU.subtract)\
                            .then_inc(p_lo, PK)
                        dve.wait_ge(h2_in, 16)
                    x = h2[:, i, :]
                    V.tensor_tensor(two(x), full, two(x), ALU.add).then_inc(fr, 1)
                    dve.wait_ge(fr, t // 2 + 1)
                    dve.sem_inc(h2_new, 1)
                    add_square(i, x)
                elif kind == "pproj":
                    V.tensor_copy(two(pj[:, i, :]), full).then_inc(fr, 1)
                    dve.wait_ge(fr, t // 2 + 1)
                    dve.wait_ge(e_hi, i + 1)
                    V.scalar_tensor_tensor(elo[:, i, :], h2[:, i, :], gains[:, NORM_PLE, i:i + 1],
                                           f32(ehi[:, i, :]), ALU.mult, ALU.subtract).then_inc(e_lo, 1)
                elif kind == "pgate":
                    g, (lo, hi) = i, SPANS[PLE_ORDER[i][0]]
                    if g >= 2:
                        dve.wait_ge(h3_new, g - 1)
                    V.tensor_tensor(sgp[:, g % 2, 0:hi - lo], ps[:, t % 2, 0, 0:hi - lo], rsv[:, lo:hi], ALU.mult)\
                        .then_inc(fr, 1)
                    dve.wait_ge(fr, t // 2 + 1)
                    dve.sem_inc(pg_pre, 1)
                    if g >= 1:
                        merge_ple(g - 1)
                    if g >= 2:
                        sum_square(g - 2)
                    if g == 2 * KT - 1:
                        merge_ple(g)
                        sum_square(g - 1)
                        sum_square(g)

            def merge_ple(g):
                n, (lo, hi) = PLE_ORDER[g][1], SPANS[g // KT]
                x = sgp[:, g % 2, 0:hi - lo]
                dve.wait_ge(pg_sig, g + 1)
                link(V.tensor_tensor(x, x, pj[:, n, lo:hi], ALU.mult))
                V.tensor_tensor(h3[:, n, lo:hi], x, h2[:, n, lo:hi], ALU.add).then_inc(h3_new, 1)

            def sum_square(g):
                n, (lo, hi) = g % KT, SPANS[g // KT]
                dve.wait_ge(h3_sq, g + 1)
                x = sqp[g % 2][:, lo:hi]
                if n == 0:
                    i = V.tensor_copy(acc[:, lo:hi], x)
                else:
                    i = V.tensor_tensor(acc[:, lo:hi], acc[:, lo:hi], x, ALU.add)
                if n == KT - 1:
                    i.then_inc(sq_sum, 1)
                else:
                    i.then_inc(sq_used, 1)
                    dve.wait_ge(sq_used, g - g // KT + 1)

            def gt_take():
                k = ng["gt"]
                ng["gt"] += 1
                dve.wait_ge(gt_sig, k + 1)
                return k

            def tnorm(which, c):
                n = ng["tn"]
                ng["tn"] += 1
                t0, ln = chunk_span(c)
                v = (vm if which == "m" else vg)[0:ln, c]
                S = [nsm[0:ln, k, :] for k in range(6)]
                mean, var = nmv[0:ln, :, 0], nmv[0:ln, :, 1]
                dve.wait_ge(h_out, h_out_of[(which, c)])
                for h in range(H):
                    i = V.bn_stats(nstat[0:ln, h, :], v[:, h, 0:DV])
                link(i)
                for h in range(H):
                    i = V.bn_aggr(nmv[0:ln, h, :], nstat[0:ln, h, :])
                link(i)
                if which == "m":
                    link(V.scalar_tensor_tensor(S[0], v[:, :, DV], -1.0, v[:, :, DV], ALU.mult, ALU.max))
                    link(V.tensor_tensor(S[0], S[0], colT[0:ln, c, 2, :], ALU.max))
                    link(V.reciprocal(S[1], S[0]))
                    link(V.tensor_tensor(S[2], var, S[1], ALU.mult))
                    link(V.tensor_tensor(S[2], S[2], S[1], ALU.mult))
                else:
                    link(V.tensor_tensor(S[2], mean, mean, ALU.mult))
                    link(V.tensor_tensor(S[2], S[2], var, ALU.add))
                V.tensor_scalar(S[2], S[2], 1.0, EPS, ALU.mult, ALU.add).then_inc(tn_pre, 1)
                dve.wait_ge(tn_root, n + 1)
                link(V.reciprocal(S[3], S[3]))
                link(V.scalar_tensor_tensor(S[4], S[3], -0.5, S[3], ALU.mult, ALU.mult))
                link(V.tensor_tensor(S[4], S[4], S[2], ALU.mult))
                link(V.scalar_tensor_tensor(S[3], S[4], 1.5, S[3], ALU.add, ALU.mult))
                if which == "m":
                    link(V.tensor_tensor(S[3], S[3], S[1], ALU.mult))
                for h in range(H):
                    if which == "m":
                        i = V.tensor_scalar(v[:, h, 0:DV], v[:, h, 0:DV], nmv[0:ln, h, 0:1], nsm[0:ln, 3, h:h + 1],
                                            ALU.subtract, ALU.mult)
                    else:
                        i = V.tensor_scalar(v[:, h, 0:DV], v[:, h, 0:DV], nsm[0:ln, 3, h:h + 1], None, ALU.mult)
                i.then_inc(tn_done, 1)
                dve.wait_ge(tn_done, n + 1)

            for s in sched:
                j, t = job_at[s], tile_at.get(s)
                if s[0] == "norm_in":
                    dve.wait_ge(gains_in, 16)
                    for k in range(KT):
                        dve.wait_ge(a_hi, k + 1)
                        V.scalar_tensor_tensor(alo[:, k, :], xT[:, k, :], gains[:, NORM_MIX, k:k + 1],
                                               f32(ahi[:, k, :]), ALU.mult, ALU.subtract).then_inc(a_lo, 1)
                        dve.wait_ge(in_sq, k + 1)
                        if k == 0:
                            i = V.tensor_copy(acc0[:, :], sq[:, 0, :])
                        else:
                            i = V.tensor_tensor(acc0[:, :], acc0[:, :], sq[:, k % 2, :], ALU.add)
                        i.then_inc(in_sq_used, 1)
                        dve.wait_ge(in_sq_used, k + 1)
                    dve.sem_inc(sq_sum, 1)
                elif s[0] == "unit":
                    continue
                elif s[0] == "tile":
                    kind, i = tiles_of(*units[s[1]])[s[2]]
                    if kind not in ("mv", "gv"):
                        evac(kind, i, t)
                    elif i[1] in V_BY_VECTOR[kind]:
                        h, c = i
                        if kind == "gv" and h == 0:
                            dve.wait_ge(cp_out, 16)
                            dve.wait_ge(aux_ready, job_at[("m1", NC)] + 4)
                        dve.wait_ge(tile_ready, t + 1)
                        dst = vm[:, c, h, 0:DV] if kind == "mv" else vg[:, c, h, :]
                        V.tensor_scalar(dst, ps[:, t % 2, 0, 0:DV], rscol[:, c:c + 1], None, ALU.mult)\
                            .then_inc(tile_free[t % 2], 1)
                        dve.wait_ge(tile_free[t % 2], t // 2 + 1)
                        dve.sem_inc(v_ready, 1)
                elif s[0] == "rsum":
                    rsum(s[1], j)
                elif s[0] == "rspread":
                    rspread(s[1], j)
                    if s[1] == 4:
                        lo, hi = SPANS[1]
                        for _, n in PLE_ORDER[KT + NY_POOL:]:
                            V.scalar_tensor_tensor(yt[:, n, lo:hi], h3[:, n, lo:hi], gains[:, NORM_OUT, n:n + 1],
                                                   rsv[:, lo:hi], ALU.mult, ALU.mult).then_inc(y_ready, 1)
                elif s[0] == "yout":
                    n, (lo, hi) = s[1], SPANS[0]
                    V.scalar_tensor_tensor(yt[:, n, lo:hi], h3[:, n, lo:hi], gains[:, NORM_OUT, n:n + 1],
                                           rsv[:, lo:hi], ALU.mult, ALU.mult).then_inc(y_ready, 1)
                elif s[0] == "rows" and s[1] == 0:
                    dve.wait_ge(const_in, NCONST)
                    R = [x[:, :] for x in rowt]
                    V.tensor_copy(cmask[:, :, :], cmaskf[:, :, :])
                    link(V.memset(rr[:, :], 0.0))
                    V.tensor_scalar(R[ROW_LI], R[ROW_LI], bgate[:, 0:1], None, ALU.add)
                    link(V.tensor_scalar(R[ROW_XF], R[ROW_XF], bgate[:, 1:2], None, ALU.add))
                    V.scalar_tensor_tensor(R[ROW_T], R[ROW_XF], -1.0, R[ROW_XF], ALU.mult, ALU.max)\
                        .then_inc(row_abs, 1)
                elif s[0] == "rows" and s[1] == 1:
                    dve.wait_ge(row_ln, 1)
                    link(V.scalar_tensor_tensor(R[ROW_LF], R[ROW_XF], 0.0, R[ROW_T], ALU.min, ALU.subtract))
                    V.tensor_tensor_scan(R[ROW_B], reset[0:H, :], R[ROW_LF], 0.0, ALU.mult, ALU.add)
                    V.tensor_copy(R[ROW_D0], R[ROW_LF])
                    V.tensor_copy(R[ROW_D1], R[ROW_LI])
                    link(V.tensor_tensor(rowc[:, 0, 0:NB], R[ROW_LF][:, TP:T:LS], m0[:, :], ALU.add))
                    V.memset(R[ROW_D0][:, TP:T:LS], -3.0e38)
                    link(V.tensor_tensor(R[ROW_D1][:, TP:T:LS], rowc[:, 0, 0:NB], R[ROW_LI][:, TP:T:LS], ALU.max))
                    link(V.tensor_tensor_scan(R[ROW_M], R[ROW_D0], R[ROW_D1], 0.0, ALU.add, ALU.max))
                elif s[0] == "rows" and s[1] == 2:
                    V.memset(rowc[:, 1, 0:1], 0.0)
                    V.tensor_copy(rowc[:, 1, 1:NC], R[ROW_M][:, L - 1:TP - 1:L])
                    V.tensor_copy(rowc[:, 1, NC:], m0[:, :])
                    V.tensor_copy(rowc[:, 2, 0:NC], R[ROW_B][:, L - 1:TP:L])
                    V.tensor_copy(rowc[:, 2, NC:], R[ROW_B][:, TP + LS - 1:T:LS])
                    V.tensor_copy(rowc[:, 3, 0:NC], R[ROW_M][:, L - 1:TP:L])
                    V.tensor_copy(rowc[:, 3, NC:], R[ROW_M][:, TP + LS - 1:T:LS])
                    V.tensor_tensor(r1[:, :], R[ROW_B], R[ROW_M], ALU.subtract)
                    link(V.tensor_tensor(rr[0:H, :], R[ROW_LI], R[ROW_B], ALU.subtract))
                    V.tensor_copy(mout[:, 0:NB], rowc[:, 3, NC:])
                    V.tensor_copy(mout[:, NB:], rowc[:, 3, NC - 1:NC])
                    link(V.tensor_tensor(rowc[:, 2, :], rowc[:, 2, :], rowc[:, 3, :], ALU.subtract))
                    link(V.tensor_tensor(rowc[:, 4, :], rowc[:, 2, :], rowc[:, 1, :], ALU.add))

                    def spread(dst, row, k):
                        for lo, hi, n, w, c0 in ((0, TP, NC, L, 0), (TP, T, NB, LS, NC)):
                            V.tensor_tensor(dst[:, lo:hi].rearrange("p (c s) -> p c s", s=w),
                                            row[:, lo:hi].rearrange("p (c s) -> p c s", s=w),
                                            bcast(rowc[:, k, c0:c0 + n], w, 2), ALU.add)
                    spread(ri[:, :], r1[:, :], 1)
                    spread(R[ROW_T], rr[0:H, :], 2)
                    link(V.tensor_scalar(rowc[:, 4, :], rowc[:, 4, :], 0.0, None, ALU.min))
                    V.tensor_scalar(ri[:, :], ri[:, :], 0.0, None, ALU.min)
                    V.tensor_scalar(R[ROW_T], R[ROW_T], 0.0, None, ALU.min).then_inc(row_pre, 1)
                elif s[0] == "rows":
                    b = job(j)
                    for c in range(NC):
                        i = V.tensor_copy(colT[:, c], b[:, c * P:(c + 1) * P]
                                          .rearrange("p (r k) -> p r k", k=32)[:, 0:3, 0:H])
                    free(i, j)
                    b = job(j + 1)
                    free(V.tensor_copy(colT[0:TS, NC], b[0:TS, 0:P].rearrange("p (r k) -> p r k", k=32)[:, 0:3, 0:H]),
                         j + 1)
                    b = job(j + 2)
                    free(V.tensor_copy(carry[:, :, :].rearrange("p h c -> p (h c)"), b[:, 0:H * (NC + NB)]), j + 2)
                    dve.wait_ge(aux_free[bank_of[j + 2]], use_of[j + 2])
                elif s[0] == "m1":
                    c = s[1]
                    t0, ln = chunk_span(c)

                    def hv(x, n=ln):
                        return x.rearrange("p (h s) -> p h s", h=H)
                    b = job(j)
                    for h in range(H):
                        i = V.scalar_tensor_tensor(pw[0:ln, h, 0:ln], b[0:ln, h * ln:(h + 1) * ln],
                                                   colT[0:ln, c, 0, h:h + 1], nmask[0:ln, int(c == NC), 0:ln],
                                                   ALU.add, ALU.min)
                    free(i, j)
                    dve.wait_ge(aux_free[bank_of[j]], use_of[j])
                    dve.sem_inc(p_pre, 1)
                    b = job(j + 1)
                    i = V.tensor_tensor(qt[:, :, 0:ln], mq[:, :, t0:t0 + ln], hv(b[:, 0:H * ln]), ALU.mult)
                    free(i, j + 1)
                    dve.wait_ge(aux_free[bank_of[j + 1]], use_of[j + 1])
                    dve.sem_inc(qt_ready, 1)
                    b = job(j + 2)
                    i = V.tensor_tensor(ktok[0:ln, :, :], hv(b[0:ln, 0:H * P]), bcast(colT[0:ln, c, 1, :], P, 2),
                                        ALU.mult)
                    free(i, j + 2)
                    dve.wait_ge(aux_free[bank_of[j + 2]], use_of[j + 2])
                    dve.sem_inc(kt_ready, 1)
                    b = job(j + 3)
                    dve.wait_ge(p_exp, c + 1)
                    i = V.tensor_tensor(att[0:ln, :, 0:ln], pw[0:ln, :, 0:ln], hv(b[0:ln, 0:H * ln]), ALU.mult)
                    free(i, j + 3)
                    dve.wait_ge(aux_free[bank_of[j + 3]], use_of[j + 3])
                    dve.sem_inc(at_ready, 1)
                elif s[0] == "m2":
                    c = s[1]
                    for h in range(H):
                        b = job(j + h)
                        new = cst[:, (c + 1) % 2, h, :]
                        if c == 0:
                            i = V.tensor_copy(new, b[:, 0:DV + 1])
                        else:
                            i = V.scalar_tensor_tensor(new, cst[:, c % 2, h, :], carry[:, h, c:c + 1],
                                                       b[:, 0:DV + 1], ALU.mult, ALU.add)
                        free(i, j + h)
                        dve.wait_ge(aux_free[bank_of[j + h]], use_of[j + h])
                        dve.sem_inc(c_ready, 1)
                    if c == NC - 1:
                        V.tensor_copy(nout[:, :, NB], cst[:, 0, :, DV]).then_inc(c_ready, 1)
                elif s[0] == "la":
                    h = s[1]
                    for a in range(2):
                        b = job(j + a)
                        i = V.tensor_scalar(cum[:, h, a * HALF:(a + 1) * HALF], b[:, 0:HALF], blr[:, h:h + 1],
                                            None, ALU.add)
                        free(i, j + a)
                    dve.wait_ge(aux_free[bank_of[j + 1]], use_of[j + 1])
                    V.scalar_tensor_tensor(stg[:, h % 2, :], cum[:, h, :], -1.0, cum[:, h, :], ALU.mult, ALU.max)\
                        .then_inc(la_abs, 1)
                elif s[0] == "la_scan":
                    h = s[1]
                    dve.wait_ge(la_ln, h + 1)
                    link(V.scalar_tensor_tensor(cum[:, h, :], cum[:, h, :], 0.0, stg[:, h % 2, :],
                                                ALU.min, ALU.subtract))
                    V.tensor_tensor_scan(cum[:, h, :], reset[:, :], cum[:, h, :], 0.0, ALU.mult, ALU.add)\
                        .then_inc(cum_ready, 1)
                elif s[0] == "gpre":
                    c = s[1]
                    t0, ln = chunk_span(c)
                    sl = L if c < NC else LS
                    cc = cum[:, :, t0:t0 + ln]
                    dve.wait_ge(aux_ready, j)
                    if c == 0:
                        dve.wait_ge(cum_ready, H)
                    dve.sem_inc(g_go, 1)
                    link(V.memset(att[:, :, :], 0.0))
                    for h in range(H):
                        x = cc[:, h, :].rearrange("p (b s) -> p b s", s=sl)
                        i = V.tensor_tensor(kf[:, h, 0:ln].rearrange("p (b s) -> p b s", s=sl),
                                            bcast(x[:, :, sl - 1], sl, 2), x, ALU.subtract)
                    i.then_inc(kd_sub, 1)
                    dve.wait_ge(kd_exp, c + 1)
                    V.tensor_tensor(kf[:, :, 0:ln], kf[:, :, 0:ln], gk[:, :, t0:t0 + ln], ALU.mult)\
                        .then_inc(kf_ready, 1)
                    dve.wait_ge(eb_ready, c + 1)
                    V.tensor_tensor(qt[:, :, 0:ln], pw[:, :, 0:ln], gq[:, :, t0:t0 + ln], ALU.mult)\
                        .then_inc(qt_ready, 1)
                elif s[0] == "lpre":
                    c, g = s[1:]
                    t0, ln = chunk_span(c)
                    cc = cum[:, :, t0:t0 + ln]
                    for n, w in enumerate(levels_of(c, g)):
                        xl = xl_buffer(c, g, n)
                        for h in range(H):
                            x = cc[:, h, :].rearrange("p (b s) -> p b s", s=2 * w)
                            i = V.tensor_tensor(xl[:, h, 0:ln].rearrange("p (b s) -> p b s", s=2 * w), x,
                                                bcast(x[:, :, w - 1], 2 * w, 2), ALU.subtract)
                        i.then_inc(xl_sub, 1)
                    for n, w in enumerate(levels_of(c, g)):
                        lv += 1
                        dve.wait_ge(xl_exp, lv)
                        xl = xl_buffer(c, g, n)[:, :, 0:ln]
                        for src, lo in ((gk, 0), (gq, w)):
                            x = xl.rearrange("p h (b s) -> p h b s", s=2 * w)[:, :, :, lo:lo + w]
                            y = src[:, :, t0:t0 + ln].rearrange("p h (b s) -> p h b s", s=2 * w)[:, :, :, lo:lo + w]
                            i = V.tensor_tensor(x, x, y, ALU.mult)
                        i.then_inc(xl_ready, 1)
                elif s[0] == "gkt":
                    c = s[1]
                    ln = chunk_span(c)[1]
                    b = job(j)
                    i = V.copy_predicated(att[0:ln, :, 0:ln], bcast(cmask[0:ln, 7, 0:ln], H, 1),
                                          b[0:ln, 0:H * ln].rearrange("p (h s) -> p h s", h=H))
                    free(i, j)
                    b = job(j + 1)
                    i = V.tensor_copy(ktok[0:ln, :, :], b[0:ln, 0:H * P].rearrange("p (h s) -> p h s", h=H))
                    free(i, j + 1)
                    for a in range(2):
                        dve.wait_ge(aux_free[bank_of[j + a]], use_of[j + a])
                    dve.sem_inc(kt_ready, 1)
                elif s[0] == "lev":
                    c, g = s[1:]
                    ln = chunk_span(c)[1]
                    for n, w in enumerate(levels_of(c, g)):
                        b = job(j + n)
                        k = PROMPT_LEVELS.index(w)

                        def late(x):
                            return x.rearrange("p h (b s) -> p h b s", s=2 * w)[:, :, :, w:]
                        i = V.copy_predicated(late(att[0:ln, :, 0:ln]), late(bcast(cmask[0:ln, k, 0:ln], H, 1)),
                                              b[0:ln, 0:H * ln // 2].rearrange("p (h b s) -> p h b s", h=H, s=w))
                        free(i, j + n)
                        dve.wait_ge(aux_free[bank_of[j + n]], use_of[j + n])
                    if g == (3 if c < NC else 1):
                        dve.sem_inc(at_ready, 1)
                elif s[0] == "gout":
                    c = s[1]
                    if c == 0:
                        dve.wait_ge(st_out[1], out_count(3))
                    for h in range(H):
                        b = job(j + h)
                        new = gst[:, (c + 1) % 2, h, :]
                        if c == 0:
                            i = V.tensor_copy(new, b[:, 0:DV])
                        else:
                            i = V.scalar_tensor_tensor(new, gst[:, c % 2, h, :], pw[:, h, L - 1:L], b[:, 0:DV],
                                                       ALU.mult, ALU.add)
                        free(i, j + h)
                        dve.wait_ge(aux_free[bank_of[j + h]], use_of[j + h])
                        dve.sem_inc(s_ready, 1)
                elif s[0] == "hpre":
                    h = s[2]
                    q = head_no[("head",) + s[1:]]
                    dve.wait_ge(aux_ready, j)
                    V.tensor_copy(qb[:, :].rearrange("p (b s) -> p b s", s=TS + LS)[:, :, 0:LS],
                                  qt[:, h, 0:TS].rearrange("p (b s) -> p b s", s=LS))
                    v = vm if s[1] == "m" else vg
                    wd = DV + 1 if s[1] == "m" else DV
                    dve.sem_inc(kv_go, 1)
                    if q == 0:
                        V.tensor_scalar(v2[:, :, DV + 1], ones[:, 0:2], 0.0, None, ALU.mult)
                    dve.wait_ge(kv_hi, q + 1)
                    dve.wait_ge(v_ready, (1 + (s[1] == "g")) * H * (NC + 1))
                    V.tensor_tensor(k2[TS:P, :], ktok[0:TS, h, :], f32(k2[0:TS, :]), ALU.subtract).then_inc(dve_step, 1)
                    n_step[0] += 1
                    for r in (0, TS):
                        V.tensor_tensor(v2[r:r + TS, 1, 0:wd], v[0:TS, NC, h, 0:wd], f32(v2[0:TS, 0, 0:wd]), ALU.subtract)
                    dve.wait_ge(dve_step, n_step[0])
                    V.tensor_tensor(kb[:, :, :], bcast(f32(k2[:, :]), NB, 1), bcast(bmask[:, :], P, 2), ALU.mult)\
                        .then_inc(blk_ready, 1)
                    dve.wait_ge(st_in[q % 2], 16 * (q // 2 + 1))
                    if s[1] == "m":
                        V.tensor_copy(st[q % 2][:, :, DV], nst[:, h, :]).then_inc(st_n, 1)
                        dve.wait_ge(st_n, h + 1)
                elif s[0] == "head":
                    which, h = s[1], s[2]
                    q = head_no[s]
                    x = st[q % 2]
                    wd = DV + 1 if which == "m" else DV
                    for n in range(NB):
                        b = job(j + n)
                        k = carry[:, h, NC + n:NC + n + 1] if which == "m" else \
                            pw[:, h, (n + 1) * LS - 1:(n + 1) * LS]
                        i = V.scalar_tensor_tensor(x[:, n, 0:wd], x[:, n, 0:wd], k, b[:, 0:wd], ALU.mult, ALU.add)
                        free(i, j + n)
                    dve.wait_ge(aux_free[bank_of[j + NB - 1]], use_of[j + NB - 1])
                    if which == "m":
                        link(V.tensor_copy(nout[:, h, 0:NB], x[:, :, DV]))
                    dve.sem_inc(st_new, 1)
                elif s[0] == "tnorm":
                    tnorm(s[1], s[2])
                elif s[0] == "bt":
                    which, n = s[1], s[2]
                    b = job(j)
                    if which == "m" and n == 0:
                        for k in range(2):
                            dve.wait_ge(st_out[k], out_count(6 + k))
                    g = gt_take()
                    if which == "g":
                        V.tensor_tensor(gt[:, g % NGT, :], gt[:, g % NGT, :], sgt[:, :], ALU.mult).then_inc(silu_used, 1)
                        dve.wait_ge(silu_used, n + 1)
                    k = gains[:, NORM_M if which == "m" else NORM_G, n:n + 1]
                    free(V.scalar_tensor_tensor(bt_t[:, 0, 0:TP], b, k, gt[:, g % NGT, 0:TP], ALU.mult, ALU.mult), j)
                    free(V.scalar_tensor_tensor(bt_t[:, 0, TP:], job(j + 1)[:, 0:TS], k, gt[:, g % NGT, TP:],
                                                ALU.mult, ALU.mult), j + 1)
                    for a in range(2):
                        dve.wait_ge(aux_free[bank_of[j + a]], use_of[j + a])
                    dve.sem_inc(gt_used, 1)
                    dve.sem_inc(bt_pre, 1)
                    m = n + (KT if which == "g" else 0)
                    dve.wait_ge(bt_hi, m + 1)
                    split_lo_of((hmlo if which == "m" else alo)[:, n, :], bt_t[:, 0, :],
                                (hmhi if which == "m" else ahi)[:, n, :], bt_lo)
                    dve.wait_ge(bt_lo, m + 1)

        @block.scalar
        def _(act):
            A = nc.scalar
            n_step = [0]

            def link(ins):
                n_step[0] += 1
                ins.then_inc(act_step, 1)
                act.wait_ge(act_step, n_step[0])

            def hi_part(u):
                s, n = u % 2, width(u)
                act.wait_ge(raw_in[s], raw_count(u))
                if u >= 2:
                    used(act, u - 2)
                A.activation(whi[:, s, 0:n], wraw[:, s, 0:n], ACT.Copy).then_inc(split_hi, 1)

            def root(src, dst, done):
                A.activation(dst, src, ACT.Sqrt).then_inc(done, 1)

            gate_use = []
            for s in sched:
                if s[0] == "bt":
                    gate_use.append(((ZMO if s[1] == "m" else ZGG) + s[2], s[1] == "g"))
                elif s[0] == "tile" and units[s[1]][0] in ("pa", "pb"):
                    kind, i = tiles_of(*units[s[1]])[s[2]]
                    gate_use.append(((ZGA if kind == "pa" else ZGB) + i, False))
            ng = {"gt": 0, "gl": 0, "stg": 0, "tn": 0, "lv": 0}

            def gate_load():
                k = ng["gl"]
                if k >= len(gate_use):
                    return
                ng["gl"] += 1
                if k >= NGT:
                    act.wait_ge(gt_used, k - NGT + 1)
                z = gate_use[k][0]
                act.wait_ge(stg_out[z % 2], 16 * (z // 2 + 1))
                act.dma_start(gt[:, k % NGT, :], zs[z, :, :]).then_inc(gt_in[k % NGT], 16)

            def gate_sigmoid():
                k = ng["gt"]
                ng["gt"] += 1
                act.wait_ge(gt_in[k % NGT], 16 * (k // NGT + 1))
                silu = gate_use[k][1]
                if silu:
                    m = sum(x[1] for x in gate_use[:k])
                    if m:
                        act.wait_ge(silu_used, m)
                A.activation(sgt[:, :] if silu else gt[:, k % NGT, :], gt[:, k % NGT, :], ACT.Sigmoid).then_inc(gt_sig, 1)

            def square(g):
                n, (lo, hi) = PLE_ORDER[g][1], SPANS[g // KT]
                act.wait_ge(h3_new, g + 1)
                if g >= 2:
                    m = g - 2
                    if m % KT == KT - 1:
                        act.wait_ge(sq_sum, 4)
                    else:
                        act.wait_ge(sq_used, m - m // KT + 1)
                A.activation(sqp[g % 2][:, lo:hi], h3[:, n, lo:hi], ACT.Square).then_inc(h3_sq, 1)
                if 0 <= g - KT < NY_POOL:
                    A.activation(yt[:, n, lo:hi], h3[:, n, lo:hi], ACT.Copy,
                                 scale=gains[:, NORM_OUT, n:n + 1]).then_inc(y_pre, 1)

            def state_load(q):
                if q >= 2:
                    act.wait_ge(st_out[q % 2], out_count(q - 2))
                if q == 5:
                    act.wait_ge(cp_out, 32)
                src = ins["C_in"] if q < H else ins["S_in"]
                act.dma_start(st[q % 2][:, :, 0:DV], src[q % H, :, :, :]).then_inc(st_in[q % 2], 16)

            def copy_out(j, dst, src_p, wd):
                act.wait_ge(aux_ready, j + 1)
                i = A.activation(dst, aux[0:src_p, bank_of[j], 0:wd], ACT.Copy)
                i.then_inc(aux_free[bank_of[j]], 1)
                act.wait_ge(aux_free[bank_of[j]], use_of[j])
                act.sem_inc(h_out, 1)

            for n in range(4):
                act.dma_start(xT[:, 2 * n:2 * n + 2, :], ins["xT"][:, 2 * n:2 * n + 2, :]).then_inc(x_in[n], 16)
            act.wait_ge(gains_in, 16)
            for s in sched:
                j, t = job_at[s], tile_at.get(s)
                if s[0] == "norm_in":
                    for k in range(KT):
                        act.wait_ge(x_in[k // 2], 16)
                        A.activation(ahi[:, k, :], xT[:, k, :], ACT.Copy, scale=gains[:, NORM_MIX, k:k + 1])\
                            .then_inc(a_hi, 1)
                        if k >= 2:
                            act.wait_ge(in_sq_used, k - 1)
                        A.activation(sq[:, k % 2, :], xT[:, k, :], ACT.Square).then_inc(in_sq, 1)
                        if k == 0:
                            hi_part(0)
                        if k == KT - 1:
                            hi_part(1)
                elif s[0] == "unit":
                    u = s[1]
                    if u >= 1 and u + 1 < len(units) and units[u + 1] != ("pgate", 4):
                        hi_part(u + 1)
                elif s[0] == "split":
                    hi_part(s[1])
                elif s[0] == "tile":
                    kind, i = tiles_of(*units[s[1]])[s[2]]
                    tt = t
                    if kind in ("mv", "gv"):
                        h, c = i
                        if c in V_BY_VECTOR[kind]:
                            continue
                        t0, ln = chunk_span(c)
                        if kind == "mv" and h == 0 and c == 0:
                            act.wait_ge(a_lo, KT)
                            act.wait_ge(rs_diag, 1)
                            A.activation(vm[:, 0:NC, :, DV], ones[:, 0:NC * H]
                                         .rearrange("p (c h) -> p c h", h=H), ACT.Copy)
                            A.activation(vm[0:TS, NC, :, DV], ones[0:TS, 0:H], ACT.Copy)
                        if kind == "gv" and h == 0 and c == 2:
                            act.wait_ge(cp_out, 16)
                            act.wait_ge(aux_ready, job_at[("m1", NC)] + 4)
                        if kind == "mv" and 1 <= h <= 2 and c == 0:
                            state_load(h - 1)
                        act.wait_ge(tile_ready, tt + 1)
                        dst = vm[0:ln, c, h, 0:DV] if kind == "mv" else vg[0:ln, c, h, :]
                        A.activation(dst, ps[0:ln, tt % 2, 0, 0:DV], ACT.Copy, scale=rscol[0:ln, c:c + 1])\
                            .then_inc(tile_free[tt % 2], 1)
                        act.wait_ge(tile_free[tt % 2], tt // 2 + 1)
                        act.sem_inc(v_ready, 1)
                    elif kind in ("mo", "gg", "ga", "gb"):
                        k = ng["stg"]
                        ng["stg"] += 1
                        act.wait_ge(tile_free[tt % 2], tt // 2 + 1)
                        act.dma_start(zs[k, :, :], stg[:, k % 2, :]).then_inc(stg_out[k % 2], 16)
                    elif kind in ("pa", "pb"):
                        gate_sigmoid()
                        if kind == "pb":
                            act.wait_ge(mg_pre, i + 1)
                            A.activation(mghi[:, i, :], merged[:, i, :], ACT.Copy).then_inc(mg_hi, 1)
                        if kind == "pb" and i == KT - 1:
                            act.wait_ge(mg_lo, KT)
                            for k in range(2):
                                act.dma_start(xr[:, k, :], ins["xT"][:, k, :]).then_inc(xr_in[k], 16)
                        gate_load()
                    elif kind == "wo":
                        act.wait_ge(h_pre, i + 1)
                        act.dma_start(hs[i, :, :], hst[:, i % 2, :]).then_inc(hs_out[i % 2], 16)
                        if i + 2 < KT:
                            act.dma_start(xr[:, i % 2, :], ins["xT"][:, i + 2, :]).then_inc(xr_in[i % 2], 16)
                        A.activation(ahi[:, i, :], hst[:, i % 2, :], ACT.Copy,
                                     scale=gains[:, NORM_FFN, i:i + 1]).then_inc(c_hi, 1)
                    elif kind == "gate":
                        act.wait_ge(ff_g, 2 * i + 1)
                        A.activation(convout[:, i, 0:2], gbuf[:, TP:TP + 2], ACT.Copy)
                        A.activation(convout[:, i, 2:].rearrange("p (b s) -> p b s", s=2),
                                     gbuf[:, 2 + TP:].rearrange("p (b s) -> p b s", s=2 + LS)[:, :, LS:],
                                     ACT.Copy).then_inc(ff_g, 1)
                        act.wait_ge(ff_cv, i + 1)
                        A.activation(sg[:, 2:], cv[:, 2:], ACT.Sigmoid).then_inc(ff_sg, 1)
                    elif kind == "val":
                        act.wait_ge(ff_pre, i + 1)
                        if i == 0:
                            act.wait_ge(hs_out[0], 16 * KT // 2)
                            act.wait_ge(hs_out[1], 16 * KT // 2)
                        A.activation(achi[:, i, :], af[:, :], ACT.Copy).then_inc(ff_hi, 1)
                        if i == FT - 1:
                            act.wait_ge(tile_ready, tt + 1)
                            act.dma_start(h2[:, :, :], hs.rearrange("k p t -> p k t")).then_inc(h2_in, 16)
                            act.dma_start(praw[:, :, :], ins["pT"]).then_inc(p_in, 16)
                            act.wait_ge(ff_g, 2 * FT)
                            act.dma_start(outs["conv"], convout[:, :, :]).then_inc(out_done, 16)
                    elif kind == "down" and i == 0:
                        act.wait_ge(p_in, 16)
                        A.activation(phi[:, :, :], praw[:, :, :], ACT.Copy).then_inc(p_hi, PK)
                    elif kind == "pproj":
                        if i == 0:
                            act.wait_ge(h2_new, KT)
                        A.activation(ehi[:, i, :], h2[:, i, :], ACT.Copy,
                                     scale=gains[:, NORM_PLE, i:i + 1]).then_inc(e_hi, 1)
                    elif kind == "pgate":
                        g, (lo, hi) = i, SPANS[PLE_ORDER[i][0]]
                        act.wait_ge(pg_pre, g + 1)
                        x = sgp[:, g % 2, 0:hi - lo]
                        A.activation(x, x, ACT.Sigmoid).then_inc(pg_sig, 1)
                        for k in [g - 1] * (g >= 1) + [g] * (g == 2 * KT - 1):
                            square(k)

                elif s[0] == "rsum":
                    n = s[1]
                    act.wait_ge(ms_ready, n + 1)
                    root(stat[:, 0, :], rscol[:, :] if n == 0 else stat[:, 1, :], ms_root)
                elif s == ("rspread", 4):
                    lo, hi = SPANS[1]
                    for k, (_, n) in enumerate(PLE_ORDER[KT + NY_POOL:]):
                        act.wait_ge(y_ready, KT + k + 1)
                        act.dma_start(outs["yT"][:, n, lo:hi], yt[:, n, lo:hi]).then_inc(y_out, 16)
                elif s == ("rows", 0):
                    act.wait_ge(row_abs, 1)
                    x = rowt[ROW_T][:, :]
                    link(A.activation(x, x, ACT.Exp, scale=-1.0))
                    A.activation(x, x, ACT.Ln, bias=1.0).then_inc(row_ln, 1)
                elif s == ("rows", 2):
                    act.wait_ge(row_pre, 1)
                    x = rowt[ROW_T][:, :]
                    A.activation(ri[:, :], ri[:, :], ACT.Exp)
                    A.activation(rr[32:32 + H, :], x, ACT.Exp)
                    A.activation(rr[64:64 + H, :], rowt[ROW_M][:, :], ACT.Exp, scale=-1.0)
                    A.activation(rowc[:, 4, :], rowc[:, 4, :], ACT.Exp).then_inc(row_exp, 4)
                    act.dma_start(outs["m"], mout[:, :]).then_inc(out_done, 16)
                elif s[0] == "m1":
                    c = s[1]
                    t0, ln = chunk_span(c)
                    act.wait_ge(p_pre, c + 1)
                    A.activation(pw[0:ln, :, 0:ln], pw[0:ln, :, 0:ln], ACT.Exp).then_inc(p_exp, 1)
                elif s[0] == "m2":
                    c = s[1]
                    for h in range(H):
                        copy_out(j + H + h, vm[:, c, h, :], P, DV + 1)
                    if c == NC - 1:
                        act.wait_ge(c_ready, NC * H + 1)
                        act.dma_start(outs["C_p"], cst[:, 0, :, 0:DV]).then_inc(cp_out, 16)
                elif s[0] == "hpre":
                    which, h = s[1], s[2]
                    q = head_no[("head", which, h)]
                    wd = DV + 1 if which == "m" else DV
                    act.wait_ge(kv_go, q + 1)
                    A.activation(k2[0:TS, :], ktok[0:TS, h, :], ACT.Copy)
                    for r in (0, TS):
                        i = A.activation(v2[r:r + TS, 0, 0:wd], (vm if which == "m" else vg)[0:TS, NC, h, 0:wd], ACT.Copy)
                    i.then_inc(kv_hi, 1)
                elif s[0] == "head":
                    which, h = s[1], s[2]
                    q = head_no[s]
                    wd = DV + 1 if which == "m" else DV
                    if q >= 1 and q + 1 < 2 * H:
                        state_load(q + 1)
                    act.wait_ge(aux_ready, j + NB + 1)
                    o = bank_of[j + NB]
                    A.activation((vm if which == "m" else vg)[0:TS, NC, h, 0:wd], aux[0:TS, o, 0:wd], ACT.Copy)\
                        .then_inc(aux_free[o], 1)
                    act.wait_ge(aux_free[o], use_of[j + NB])
                    act.sem_inc(h_out, 1)
                    act.wait_ge(st_new, q + 1)
                    dst = outs["C_s"] if which == "m" else outs["S_s"]
                    act.dma_start(dst[h, :, :, :], st[q % 2][:, :, 0:DV]).then_inc(st_out[q % 2], 16)
                    if q == 3:
                        act.dma_start(outs["n"], nout[:, :, :]).then_inc(out_done, 16)
                elif s[0] == "la":
                    act.wait_ge(la_abs, s[1] + 1)
                    x = stg[:, s[1] % 2, :]
                    link(A.activation(x, x, ACT.Exp, scale=-1.0))
                    A.activation(x, x, ACT.Ln, bias=1.0).then_inc(la_ln, 1)
                elif s[0] == "gpre":
                    c = s[1]
                    t0, ln = chunk_span(c)
                    act.wait_ge(g_go, c + 1)
                    act.wait_ge(kd_sub, c + 1)
                    A.activation(kf[:, :, 0:ln], kf[:, :, 0:ln], ACT.Exp, scale=1 / TAU).then_inc(kd_exp, 1)
                    A.activation(pw[:, :, 0:ln], cum[:, :, t0:t0 + ln], ACT.Exp, scale=1 / TAU).then_inc(eb_ready, 1)
                elif s[0] == "lpre":
                    c, g = s[1:]
                    ln = chunk_span(c)[1]
                    for n, w in enumerate(levels_of(c, g)):
                        ng["lv"] += 1
                        act.wait_ge(xl_sub, ng["lv"])
                        x = xl_buffer(c, g, n)[:, :, 0:ln].rearrange("p h (b s) -> p h b s", s=2 * w)
                        A.activation(x[:, :, :, 0:w], x[:, :, :, 0:w], ACT.Exp, scale=-1 / TAU)
                        A.activation(x[:, :, :, w:], x[:, :, :, w:], ACT.Exp, scale=1 / TAU).then_inc(xl_exp, 1)
                elif s[0] == "gout":
                    c = s[1]
                    for h in range(H):
                        copy_out(j + H + h, vg[:, c, h, :], P, DV)
                    if c == NC - 1:
                        act.wait_ge(s_ready, NC * H)
                        act.dma_start(outs["S_p"], gst[:, 0, :, :]).then_inc(cp_out, 16)
                elif s[0] == "tnorm":
                    ng["tn"] += 1
                    act.wait_ge(tn_pre, ng["tn"])
                    ln = chunk_span(s[2])[1]
                    root(nsm[0:ln, 2, :], nsm[0:ln, 3, :], tn_root)
                elif s[0] == "bt":
                    m = s[2] + (KT if s[1] == "g" else 0)
                    if m == 0:
                        act.wait_ge(tn_done, 2 * (NC + 1))
                        for _ in range(NGT):
                            gate_load()
                    gate_sigmoid()
                    act.wait_ge(bt_pre, m + 1)
                    A.activation((hmhi if s[1] == "m" else ahi)[:, s[2], :], bt_t[:, 0, :], ACT.Copy)\
                        .then_inc(bt_hi, 1)
                    gate_load()
            act.wait_ge(out_done, 48)
            act.wait_ge(y_out, 16 * 2 * KT)
            for k in range(2):
                act.wait_ge(st_out[k], out_count(6 + k))
            act.wait_ge(cp_out, 32)


def pack(w, width):
    k, n = w.shape
    v = w.reshape(k // P, P, n // width, width).transpose(2, 1, 0, 3)
    return np.ascontiguousarray(v).reshape(n // width, P, k // P * width)


def vec(g):
    return np.ascontiguousarray(g.reshape(-1, P).T)


def constants():
    i = np.arange(P)
    s, t = i[:, None], i[None, :]
    cmask = np.zeros((P, 8, P), np.float32)
    for n, w in enumerate(PROMPT_LEVELS):
        cmask[:, n, :] = (s // (2 * w) == t // (2 * w)) & (s // w % 2 == 0) & (t // w % 2 == 1)
    cmask[:, 7, :] = s == t
    nmask = np.full((P, 2, P), -1e30, np.float32)
    nmask[:, 0, :][s <= t] = 0.0
    nmask[:, 1, :][(s <= t) & (s // LS == t // LS)] = 0.0
    sel = np.zeros((H, H, P), np.float32)
    for h in range(H):
        sel[h, h, :] = 1.0
    bmask = (i[:, None] % TS // LS == np.arange(NB)[None, :]).astype(np.float32)
    return {"ident": np.eye(P, dtype=np.float32), "cmask": cmask, "nmask": nmask, "sel": sel, "bmask": bmask}


def kernel(x_prompt, x_sample, state_mlstm_C, state_mlstm_n, state_mlstm_m, state_gla_S,
           state_ffn_conv, p_prompt, p_sample, norm_mix_g, w_in, b_mi, b_mf, g_mnorm, w_lr2,
           b_lr2, g_gnorm, w_pa, w_pb, w_o, norm_ffn_g, w_up, conv_w, conv_b, w_down,
           norm_ple_g, w_ple_gate, w_ple_proj, final_norm_g):
    import concourse.bacc as bacc
    from concourse.bass_utils import run_bass_kernel_spmd as run

    a = np.asarray

    def tokens(p, s):
        x = np.concatenate([a(p).reshape(TP, -1), a(s).reshape(TS, -1)], axis=0)
        return np.ascontiguousarray(x.T.reshape(-1, P, T).transpose(1, 0, 2))

    w = a(w_in)[0]
    sizes = [512, 512, 1024, 4, 4, 1024, 512, 512, 1024, RANK, 1024, 1024, 1024]
    o = np.concatenate([[0], np.cumsum(sizes)])
    col = {n: w[:, o[k]:o[k + 1]] for k, n in enumerate(
        ("mq", "mk", "mv", "mi", "mf", "mo", "gq", "gk", "gv", "glr", "gg", "ga", "gb"))}
    main = np.concatenate([col[n] for n in ("mq", "mk", "mv", "gq", "gk", "gv", "mo", "gg", "ga", "gb")], axis=1)
    misc = np.concatenate([col["mi"], col["mf"], col["glr"]], axis=1)
    misc_cols = np.zeros((P, KT, P), np.float32)
    for at, n, lo in ((0, H, 0), (32, H, H), (64, RANK, 2 * H)):
        misc_cols[:, :, at:at + n] = misc.reshape(KT, P, -1).transpose(1, 0, 2)[:, :, lo:lo + n]
    up = a(w_up)[0].reshape(D, 2, FT, P).transpose(0, 2, 1, 3).reshape(D, 2 * FF)
    arrays = dict(
        xT=tokens(x_prompt, x_sample), pT=tokens(p_prompt, p_sample),
        C_in=np.ascontiguousarray(a(state_mlstm_C)[0].transpose(1, 2, 0, 3)),
        S_in=np.ascontiguousarray(a(state_gla_S)[0].transpose(1, 2, 0, 3)),
        nst=np.ascontiguousarray(a(state_mlstm_n)[0].transpose(2, 1, 0)),
        m0=np.ascontiguousarray(a(state_mlstm_m)[0].T),
        convst=np.ascontiguousarray(a(state_ffn_conv)[0].reshape(NB, 2, FT, P).transpose(3, 2, 0, 1)),
        gains=np.ascontiguousarray(np.stack([vec(a(g).reshape(-1)) for g in (
            norm_mix_g, g_mnorm, g_gnorm, norm_ffn_g, norm_ple_g, final_norm_g)], axis=1)),
        convw=np.ascontiguousarray(a(conv_w)[0].reshape(3, FT, P).transpose(2, 0, 1)),
        convb=vec(a(conv_b)[0]), blr=vec(a(b_lr2)[0]),
        bgate=np.ascontiguousarray(np.stack([a(b_mi)[0], a(b_mf)[0]], axis=1)),
        wlr=np.ascontiguousarray(a(w_lr2)[0]),
        w_misc=misc_cols.reshape(P, KT * P),
        w_in=pack(main, 2 * P), w_pa=pack(a(w_pa)[0], 2 * P), w_pb=pack(a(w_pb)[0], 2 * P),
        w_o=pack(a(w_o)[0], 2 * P), w_up=pack(up, 2 * P), w_down=pack(a(w_down)[0], P),
        w_pproj=pack(a(w_ple_proj)[0], D), w_pgate=pack(a(w_ple_gate)[0], 2 * P),
    )
    arrays.update(constants())

    nc = bacc.Bacc("TRN2", target_bir_lowering=False, num_devices=1)
    ins = {n: nc.dram_tensor(f"in_{n}", x.shape, mybir.dt.from_np(x.dtype), kind="ExternalInput").ap()
           for n, x in arrays.items()}
    shapes = dict(yT=(P, KT, T), C_p=(P, H, DV), S_p=(P, H, DV), n=(P, H, NB + 1), m=(H, NB + 1),
                  conv=(P, FT, 2 + 2 * NB), C_s=(H, P, NB, DV), S_s=(H, P, NB, DV))
    outs = {n: nc.dram_tensor(f"out_{n}", s, F32, kind="ExternalOutput").ap() for n, s in shapes.items()}
    build(nc, ins, outs)
    r = run(nc, [{f"in_{n}": x for n, x in arrays.items()}], core_ids=[0]).results[0]
    g = {n: a(r[f"out_{n}"]) for n in shapes}

    y = g["yT"].transpose(2, 1, 0).reshape(T, D)
    n, m, conv = g["n"], g["m"], g["conv"]
    cv = conv.transpose(2, 1, 0).reshape(2 + 2 * NB, FF)
    c = np.ascontiguousarray
    return (c(y[:TP]).reshape(1, TP, D), c(y[TP:]).reshape(NB, LS, D),
            c(g["C_p"].transpose(1, 0, 2))[None, None], c(n[:, :, NB].T)[None, None], c(m[:, NB])[None, None],
            c(g["S_p"].transpose(1, 0, 2))[None, None], c(cv[:2])[None, None],
            c(g["C_s"].transpose(2, 0, 1, 3))[None], c(n[:, :, :NB].transpose(2, 1, 0))[None],
            c(m[:, :NB].T)[None], c(g["S_s"].transpose(2, 0, 1, 3))[None],
            c(cv[2:].reshape(NB, 2, FF))[None])
```
